# Optimizing a Trainium2 kernel written in Bass

```python
import math
import jax, jax.numpy as jnp
from jax import lax
import numpy as np

D_MODEL = 2048
BATCH = 1
SEQ = 512
DEPTH = 2

PLE_DIM = 256
HEAD_DIM = 128
NSA_HEADS = D_MODEL // 256
NSA_KV_GROUPS = 2
NSA_HPG = NSA_HEADS // NSA_KV_GROUPS
NSA_WIDTH = NSA_HEADS * HEAD_DIM
KV_W = NSA_KV_GROUPS * HEAD_DIM
CMP_LEN = 32
CMP_STRIDE = 16
SEL_BLOCK = 64
SEL_TOPK = 16
WINDOW = 512
Q_BLOCK = 128
HG_HEADS = D_MODEL // 256
HG_DK = 128
HG_DV = 128
HG_WIDTH = HG_HEADS * HG_DV
HG_CHUNK = 64
CONV_CH = D_MODEL
CONV_K = 31
N_EVEN = (DEPTH + 1) // 2
N_ODD = DEPTH // 2
DEEPNORM_ALPHA = (2.0 * DEPTH) ** 0.25
DEEPNORM_BETA = (8.0 * DEPTH) ** -0.25
LN_EPS = 1e-5
EVEN_SPLITS = (NSA_WIDTH, KV_W, KV_W, KV_W, KV_W, KV_W, KV_W, NSA_HEADS * 3, NSA_WIDTH,
               HG_HEADS * HG_DK, HG_HEADS * HG_DK, HG_WIDTH, HG_WIDTH)
EVEN_IN = sum(EVEN_SPLITS)

kernel_name = "hybrid_nsa_hgrn2_conformer_deepnorm"

def _layernorm(x, g, b):
    xf = x.astype(jnp.float32)
    mu = jnp.mean(xf, axis=-1, keepdims=True)
    var = jnp.mean(jnp.square(xf - mu), axis=-1, keepdims=True)
    return ((xf - mu) * lax.rsqrt(var + LN_EPS) * g + b).astype(x.dtype)

def _masked_softmax(s, mask):
    s = jnp.where(mask, s.astype(jnp.float32), -1e30)
    return jnp.where(mask, jax.nn.softmax(s, axis=-1), 0.0)

def _alibi_slopes(n):
    return jnp.asarray(2.0 ** (-8.0 * np.arange(1, n + 1) / n), jnp.float32)

def _cmp_sel_overlap(n_cmp, n_sel):
    s = np.arange(n_cmp)[:, None] * CMP_STRIDE
    b = np.arange(n_sel)[None, :] * SEL_BLOCK
    ov = np.clip(np.minimum(s + CMP_LEN, b + SEL_BLOCK) - np.maximum(s, b), 0, None) / CMP_LEN
    return jnp.asarray(ov, jnp.float32)

def _nsa(q, k_cmp, v_cmp, k_slc, v_slc, k_win, v_win, gates, pe_k, w1_k, w2_k, pe_v, w1_v, w2_v):
    B, T, _ = q.shape
    G, Hg, dh = NSA_KV_GROUPS, NSA_HPG, HEAD_DIM
    q = q.reshape(B, T, G, Hg, dh) * dh ** -0.5

    def compress(raw, pe, w1, w2):
        r = raw.reshape(B, T // CMP_STRIDE, CMP_STRIDE, G, dh)
        blk = jnp.concatenate([r[:, :-1], r[:, 1:]], axis=2) + pe[:, None, :]
        blk = blk.transpose(0, 1, 3, 2, 4).reshape(B, -1, G, CMP_LEN * dh)
        return jax.nn.gelu(blk @ w1) @ w2

    kc = compress(k_cmp, pe_k, w1_k, w2_k)
    vc = compress(v_cmp, pe_v, w1_v, w2_v)
    n_cmp = T // CMP_STRIDE - 1
    cmp_end = jnp.arange(n_cmp) * CMP_STRIDE + CMP_LEN - 1
    n_sel = T // SEL_BLOCK
    topk = min(SEL_TOPK, n_sel)
    overlap = _cmp_sel_overlap(n_cmp, n_sel)
    ks = k_slc.reshape(B, n_sel, SEL_BLOCK, G, dh).transpose(0, 3, 1, 2, 4)
    vs = v_slc.reshape(B, n_sel, SEL_BLOCK, G, dh).transpose(0, 3, 1, 2, 4)
    pad = ((0, 0), (WINDOW, 0), (0, 0), (0, 0))
    kw = jnp.pad(k_win.reshape(B, T, G, dh), pad)
    vw = jnp.pad(v_win.reshape(B, T, G, dh), pad)
    gates = jax.nn.sigmoid(gates.astype(jnp.float32)).reshape(B, T, G, Hg, 3)
    slopes = _alibi_slopes(NSA_HEADS).reshape(1, G, Hg, 1, 1)
    bidx = jnp.arange(B)[:, None, None, None]
    gidx = jnp.arange(G)[None, :, None, None]
    sel_j = jnp.arange(n_sel)
    m_sel = topk * SEL_BLOCK

    def block(bi):
        t0 = bi * Q_BLOCK
        tpos = t0 + jnp.arange(Q_BLOCK)
        qb = lax.dynamic_slice_in_dim(q, t0, Q_BLOCK, axis=1)
        d_c = tpos[:, None] - cmp_end[None, :]
        s = jnp.einsum('btghd,bngd->bghtn', qb, kc) - slopes * d_c
        p_c = _masked_softmax(s, d_c >= 0)
        o_c = jnp.einsum('bghtn,bngd->btghd', p_c, vc)
        imp = jnp.einsum('bghtn,nj->bgtj', p_c, overlap)
        cur = (tpos // SEL_BLOCK)[:, None]
        forced = (sel_j == 0) | (sel_j == cur) | (sel_j == cur - 1)
        imp = jnp.where(forced, 1e9, imp)
        imp = jnp.where(sel_j * SEL_BLOCK > tpos[:, None], -1e9, imp)
        _, idx = lax.top_k(imp, topk)
        kg = ks[bidx, gidx, idx].reshape(B, G, Q_BLOCK, m_sel, dh)
        vg = vs[bidx, gidx, idx].reshape(B, G, Q_BLOCK, m_sel, dh)
        pos = (idx[..., None] * SEL_BLOCK + jnp.arange(SEL_BLOCK)).reshape(B, G, 1, Q_BLOCK, m_sel)
        d_s = tpos[:, None] - pos
        s = jnp.einsum('btghd,bgtmd->bghtm', qb, kg) - slopes * d_s
        p_s = _masked_softmax(s, d_s >= 0)
        o_s = jnp.einsum('bghtm,bgtmd->btghd', p_s, vg)
        kwb = lax.dynamic_slice_in_dim(kw, t0, Q_BLOCK + WINDOW, axis=1)
        vwb = lax.dynamic_slice_in_dim(vw, t0, Q_BLOCK + WINDOW, axis=1)
        kpos = t0 - WINDOW + jnp.arange(Q_BLOCK + WINDOW)
        d_w = tpos[:, None] - kpos[None, :]
        mask_w = (d_w >= 0) & (d_w < WINDOW) & (kpos >= 0)[None, :]
        s = jnp.einsum('btghd,bsgd->bghts', qb, kwb) - slopes * d_w
        p_w = _masked_softmax(s, mask_w)
        o_w = jnp.einsum('bghts,bsgd->btghd', p_w, vwb)
        gb = lax.dynamic_slice_in_dim(gates, t0, Q_BLOCK, axis=1)
        return gb[..., 0:1] * o_c + gb[..., 1:2] * o_s + gb[..., 2:3] * o_w

    out = lax.map(block, jnp.arange(T // Q_BLOCK))
    return out.transpose(1, 0, 2, 3, 4, 5).reshape(B, T, NSA_WIDTH)

def _hgrn2(q, k, logf, v):
    B, T, H, dk = q.shape
    dv = v.shape[-1]
    n = T // HG_CHUNK

    def to_chunks(a):
        return a.reshape(B, n, HG_CHUNK, H, a.shape[-1]).transpose(1, 0, 3, 2, 4)

    qc, kc, gc, vc = to_chunks(q), to_chunks(k), to_chunks(logf), to_chunks(v)
    gc = jnp.cumsum(gc, axis=3)
    mask = jnp.tril(jnp.ones((HG_CHUNK, HG_CHUNK), bool))[:, :, None]

    def step(S, inp):
        q_, k_, g_, v_ = inp
        o_inter = jnp.einsum('bhtk,bhkv->bhtv', q_ * jnp.exp(g_), S)
        diff = g_[:, :, :, None, :] - g_[:, :, None, :, :]
        decay = jnp.where(mask, jnp.exp(jnp.where(mask, diff, 0.0)), 0.0)
        a = jnp.einsum('bhtk,bhtsk,bhsk->bhts', q_, decay, k_)
        o = o_inter + jnp.einsum('bhts,bhsv->bhtv', a, v_)
        g_last = g_[:, :, -1, :]
        S = jnp.exp(g_last)[..., None] * S + jnp.einsum(
            'bhsk,bhsv->bhkv', k_ * jnp.exp(g_last[:, :, None, :] - g_), v_)
        return S, o

    S0 = jnp.zeros((B, H, dk, dv), jnp.float32)
    _, o = lax.scan(step, S0, (qc, kc, gc, vc))
    return o.transpose(1, 0, 3, 2, 4).reshape(B, T, H, dv)

def _even_layer(x, w_in, pe_k, w1_k, w2_k, pe_v, w1_v, w2_v, hg_norm, lb, w_out):
    B, T, _ = x.shape
    parts = jnp.split(x @ w_in, np.cumsum(EVEN_SPLITS)[:-1].tolist(), axis=-1)
    nq, kc, vc, ks, vs, kw, vw, ng, nz, hq, hf, hi, hz = parts
    a = _nsa(nq, kc, vc, ks, vs, kw, vw, ng, pe_k, w1_k, w2_k, pe_v, w1_v, w2_v)
    hq = jax.nn.silu(hq.astype(jnp.float32)).reshape(B, T, HG_HEADS, HG_DK)
    hf = hf.astype(jnp.float32).reshape(B, T, HG_HEADS, HG_DK)
    lbh = lb.reshape(HG_HEADS, HG_DK)
    f = lbh + (1.0 - lbh) * jax.nn.sigmoid(hf)
    k = (1.0 - lbh) * jax.nn.sigmoid(-hf)
    o = _hgrn2(hq, k, jnp.log(f), hi.astype(jnp.float32).reshape(B, T, HG_HEADS, HG_DV))
    o = o * lax.rsqrt(jnp.mean(jnp.square(o), axis=-1, keepdims=True) + LN_EPS)
    o = o.reshape(B, T, HG_WIDTH) * hg_norm
    y = jnp.concatenate([a * jax.nn.silu(nz), o * jax.nn.silu(hz)], axis=-1).astype(x.dtype)
    return y @ w_out

def _conv_layer(x, w_in, conv_w, conv_b, ln_g, ln_b, w_out):
    a, b, z = jnp.split(x @ w_in, 3, axis=-1)
    u = a * jax.nn.sigmoid(b)
    c = lax.conv_general_dilated(u, conv_w[:, None, :].astype(u.dtype), window_strides=(1,),
                                 padding=[(CONV_K - 1, 0)], dimension_numbers=('NWC', 'WIO', 'NWC'),
                                 feature_group_count=CONV_CH) + conv_b
    c = _layernorm(c, ln_g, ln_b)
    return (jax.nn.silu(c) * jax.nn.silu(z)) @ w_out

def setup_inputs(seed: int = 0) -> dict:
    key = jax.random.key(seed)
    ks = jax.random.split(key, 24)

    def nrm(k, shape, scale):
        return jax.random.normal(k, shape, jnp.float32) * scale

    cw = CMP_LEN * HEAD_DIM
    return {
        'x': nrm(ks[0], (BATCH, SEQ, D_MODEL), 1.0),
        'p': nrm(ks[1], (DEPTH, BATCH, SEQ, PLE_DIM), 1.0),
        'ev_w_in': nrm(ks[2], (N_EVEN, D_MODEL, EVEN_IN), D_MODEL ** -0.5),
        'ev_cmp_pe_k': nrm(ks[3], (N_EVEN, CMP_LEN, HEAD_DIM), 0.1),
        'ev_cmp_w1_k': nrm(ks[4], (N_EVEN, cw, HEAD_DIM), cw ** -0.5),
        'ev_cmp_w2_k': nrm(ks[5], (N_EVEN, HEAD_DIM, HEAD_DIM), HEAD_DIM ** -0.5),
        'ev_cmp_pe_v': nrm(ks[6], (N_EVEN, CMP_LEN, HEAD_DIM), 0.1),
        'ev_cmp_w1_v': nrm(ks[7], (N_EVEN, cw, HEAD_DIM), cw ** -0.5),
        'ev_cmp_w2_v': nrm(ks[8], (N_EVEN, HEAD_DIM, HEAD_DIM), HEAD_DIM ** -0.5),
        'ev_hg_norm': 1.0 + nrm(ks[9], (N_EVEN, HG_WIDTH), 0.1),
        'hgrn_lb': nrm(ks[10], (N_EVEN, HG_HEADS * HG_DK), 1.0),
        'ev_w_out': nrm(ks[11], (N_EVEN, NSA_WIDTH + HG_WIDTH, D_MODEL),
                        (NSA_WIDTH + HG_WIDTH) ** -0.5 * DEEPNORM_BETA),
        'od_w_in': nrm(ks[12], (N_ODD, D_MODEL, 3 * CONV_CH), D_MODEL ** -0.5),
        'od_conv_w': nrm(ks[13], (N_ODD, CONV_K, CONV_CH), CONV_K ** -0.5),
        'od_conv_b': nrm(ks[14], (N_ODD, CONV_CH), 0.02),
        'od_ln_g': 1.0 + nrm(ks[15], (N_ODD, CONV_CH), 0.1),
        'od_ln_b': nrm(ks[16], (N_ODD, CONV_CH), 0.02),
        'od_w_out': nrm(ks[17], (N_ODD, CONV_CH, D_MODEL), CONV_CH ** -0.5 * DEEPNORM_BETA),
        'post_ln_g': 1.0 + nrm(ks[18], (DEPTH, D_MODEL), 0.1),
        'post_ln_b': nrm(ks[19], (DEPTH, D_MODEL), 0.02),
        'ple_w': nrm(ks[20], (DEPTH, PLE_DIM, D_MODEL), PLE_DIM ** -0.5),
        'ple_gate_w': nrm(ks[21], (DEPTH, D_MODEL, D_MODEL), D_MODEL ** -0.5),
    }

def reference(x, p, ev_w_in, ev_cmp_pe_k, ev_cmp_w1_k, ev_cmp_w2_k, ev_cmp_pe_v, ev_cmp_w1_v,
              ev_cmp_w2_v, ev_hg_norm, hgrn_lb, ev_w_out, od_w_in, od_conv_w, od_conv_b, od_ln_g,
              od_ln_b, od_w_out, post_ln_g, post_ln_b, ple_w, ple_gate_w):
    lb_all = jnp.cumsum(jax.nn.softmax(hgrn_lb.astype(jnp.float32), axis=0), axis=0)
    lb_all = lb_all - lb_all[0:1]
    for i in range(DEPTH):
        j = i // 2
        if i % 2 == 0:
            y = _even_layer(x, ev_w_in[j], ev_cmp_pe_k[j], ev_cmp_w1_k[j], ev_cmp_w2_k[j],
                            ev_cmp_pe_v[j], ev_cmp_w1_v[j], ev_cmp_w2_v[j], ev_hg_norm[j],
                            lb_all[j], ev_w_out[j])
        else:
            y = _conv_layer(x, od_w_in[j], od_conv_w[j], od_conv_b[j], od_ln_g[j], od_ln_b[j],
                            od_w_out[j])
        x = _layernorm(DEEPNORM_ALPHA * x + y, post_ln_g[i], post_ln_b[i])
        x = x + (p[i] @ ple_w[i]) * jax.nn.sigmoid(x @ ple_gate_w[i])
    return x


_drawn_inputs = setup_inputs


def setup_inputs(seed=0):
    import zlib

    import numpy as np

    out = dict(_drawn_inputs(seed))
    spreads = {}
    factors = {'ev_cmp_pe_k': 8.0,
     'ev_cmp_w1_k': 8.0,
     'ev_cmp_w2_k': 8.0,
     'ev_cmp_pe_v': 8.0,
     'ev_hg_norm': 4.736,
     'od_conv_b': 8.0,
     'od_ln_g': 3.973,
     'od_ln_b': 24.696}
    for name, (base, spread) in spreads.items():
        noise = np.random.default_rng([zlib.crc32(name.encode()), seed]).standard_normal(out[name].shape)
        drawn = base * np.exp(spread * noise) if base else spread * noise
        out[name] = __import__('jax').numpy.asarray(drawn.astype(out[name].dtype))
    for name, factor in factors.items():
        out[name] = (out[name] * factor).astype(out[name].dtype)
    return out
```

```python
import numpy as np
from contextlib import ExitStack

import concourse.bass as bass
from concourse import mybir

P = 128
T = 512
D = 2048
KC = D // P
NT = T // P
HEADS = 8
GROUPS = 2
HPG = HEADS // GROUPS
CMP_LEN, CMP_STRIDE = 32, 16
NCMP = T // CMP_STRIDE - 1
CONV_K = 31
PLE_K = 2
ALPHA = (2.0 * 2) ** 0.25
EPS = 1e-5
NEG = -1e30
LN_FLOOR = 2.0 ** -63

W_KV = 0
W_HEAD = 13
W_PLE = (61, 143)
W_OUT = (63, 145)
W_GATE = (79, 161)
W_CONV = 95
W_TILES = 177
G_PLE = (61, 157)
G_OUT = (77, 173)
G_GATE = (93, 189)
G_CONV = 109

HALVES = (64, 32, 16, 8, 4, 2, 1)
LEVELS = 8
DIAG = 6
LEVEL_OF = (0, 1, 2, 3, 4, 5, 7)

C_LNG = 0
C_LNB = C_LNG + 32
C_CG = C_LNB + 32
C_CB = C_CG + KC
C_CBIAS = C_CB + KC
C_CW = C_CBIAS + KC
C_NORM = C_CW + KC * CONV_K
C_LBRAW = C_NORM + HEADS
C_PE = C_LBRAW + HEADS
C_SLOPE = C_PE + 2 * CMP_LEN
C_SEEN = C_SLOPE + HEADS
C_ID = C_SEEN + 1
C_DIST = C_ID + P
C_DISTC = C_DIST + T
C_TILE = C_DISTC + NT * NCMP
NPAR = C_TILE + NT


def constants():
    t = np.arange(P)[:, None]
    slope = np.broadcast_to(2.0 ** (-8.0 * np.arange(1, HEADS + 1) / HEADS), (P, HEADS))
    seen = (t >= CMP_LEN - 1).astype(np.float32)
    x = np.arange(T)[None, :] - (T - P) - t
    dist = np.where(x <= 0, x, NEG)
    end = np.arange(NCMP) * CMP_STRIDE + CMP_LEN - 1
    tt = np.arange(NT)[None, :, None] * P + t[:, :, None]
    distc = np.where(end <= tt, end - tt, NEG).reshape(P, -1)
    tile = np.arange(P)[:, None] // 32 == np.arange(NT)[None, :]
    cols = np.concatenate([slope, seen, np.eye(P), dist, distc, tile], axis=1).astype(np.float32)
    masks = np.zeros((P, LEVELS, P), np.float32)
    s, u = np.arange(P)[:, None], np.arange(P)[None, :]
    for e, half in enumerate(HALVES):
        masks[:, LEVEL_OF[e], :] = (s // (2 * half) == u // (2 * half)) & (s % (2 * half) < half) & (u % (2 * half) >= half)
    masks[:, DIAG, :] = s == u
    return cols, masks.reshape(P, -1)


class Idx:

    def __init__(self, base, mul=0, var=0):
        self.base, self.mul, self.var = base, mul, var

    def n(self, off=0):
        return self.var * self.mul + (self.base + off) if self.mul else self.base + off

    def half(self, off=0):
        return self.var * (self.mul // 2) + (self.base // 2 + off) if self.mul else self.base // 2 + off

    def plus(self, k):
        return Idx(self.base + k, self.mul, self.var)

    @property
    def slot(self):
        return self.base % 2


def wait(eng, sem, value):
    if not isinstance(value, int) or value > 0:
        eng.wait_ge(sem, value)


def build(nc, xT, wall, w1, w2, pT, par_in, masks_in, out):
    F = mybir.dt.float32
    R = mybir.dt.float32r
    U8 = mybir.dt.uint8
    ALU = mybir.AluOpType
    ACT = mybir.ActivationFunctionType
    ds = bass.ds
    x2_dram = nc.dram_tensor("x2_residual", [P, KC * T], F).ap()

    with ExitStack() as ctx:
        def sb(name, shape, dt=F):
            return ctx.enter_context(nc.sbuf_tensor(name, shape, dt))

        sems = {}

        def S(name):
            if name not in sems:
                sems[name] = ctx.enter_context(nc.semaphore(name))
            return sems[name]

        w_raw = sb("w_raw", [P, 2, D])
        w_hi = sb("w_hi", [P, 2, D], R)
        w_lo = sb("w_lo", [P, 2, D], R)
        a_hi = sb("a_hi", [P, KC, T], R)
        a_lo = sb("a_lo", [P, KC, T], R)
        Y = sb("Y", [P, KC * T])
        Z = sb("Z", [P, KC * T])
        tmp = sb("tmp", [P, 2688])
        par = sb("par", [P, NPAR])
        msk = sb("msk", [P, LEVELS, P], U8)
        ones = sb("ones", [P, P])
        p_hi = sb("p_hi", [P, PLE_K, T], R)
        p_lo = sb("p_lo", [P, PLE_K, T], R)
        bias = sb("bias", [P, T + NT * NCMP])
        kcT = sb("kcT", [P, GROUPS * NCMP])
        vc4 = sb("vc4", [P, GROUPS, P])
        gates = sb("gates", [P, 3 * HEADS, NT])
        mx = sb("mx", [P, 12])
        nmx = sb("nmx", [P, 12])
        rsum = sb("rsum", [P, 12])
        rg = sb("rg", [P, 12])
        eglast = sb("eglast", [P, NT])
        lb = sb("lb", [P, 4, HEADS])
        ident = par[:, C_ID:C_ID + P]

        def pcol(c, j):
            return par[:, ds(j + c, 1)] if not isinstance(j, int) else par[:, c + j:c + j + 1]

        def chunk(buf, j):
            return buf[:, ds(j * T, T)] if not isinstance(j, int) else buf[:, j * T:(j + 1) * T]

        ksT, kwT, vs, vw = [[Z[:, (2 * n + g) * T:(2 * n + g + 1) * T] for g in range(GROUPS)] for n in range(4)]
        ZU = 8 * T
        prob = Z[:, ZU:ZU + 1280]
        qT = Z[:, ZU + 1280:ZU + 1792]
        ring = [Z[:, ZU + T * r:ZU + T * (r + 1)] for r in range(3)]
        kp = Z[:, ZU:ZU + T]
        probT = Z[:, ZU + 1792:ZU + 3072]
        viT = Z[:, ZU + 1792:ZU + 1792 + T]
        kpT = Z[:, ZU + 1792 + T:ZU + 1792 + 2 * T]
        gg = Z[:, ZU + 3072:ZU + 3584]
        vi = gg
        kk = Z[:, ZU + 3584:ZU + 4096]
        blk = [Z[:, ZU + n * 1984:ZU + (n + 1) * 1984].rearrange("p (l n) -> p l n", l=CMP_LEN) for n in range(2)]
        sg = tmp[:, 0:T]
        osb = tmp[:, T:2 * T]
        qg = tmp[:, 2 * T:3 * T]
        sq_h = rst_h = qg
        qq = tmp[:, 3 * T:4 * T]
        state = tmp[:, 3 * T:3 * T + 3 * P]
        probcT = tmp[:, 4 * T:5 * T]
        AT = tmp[:, 4 * T:5 * T]
        probc = tmp[:, 5 * T:5 * T + P]
        probc31 = probc.rearrange("p (t n) -> p t n", t=NT)[:, :, 0:NCMP]
        nz_s = Y[:, 7 * T:8 * T]
        hz_s = Y[:, 15 * T:16 * T]
        p_raw0 = vT2 = tmp[:, 0:2 * T]
        gT = tmp[0:3 * HEADS, 2 * T:3 * T]
        gel_k = tmp[:, 3 * T:3 * T + GROUPS * NCMP]
        gel_v = tmp[:, 3 * T + 64:3 * T + 64 + GROUPS * P]
        w2_sb = tmp[:, 3 * T + 320:3 * T + 320 + 2 * P]
        w1_sb = [Y[:, 4096 * n:4096 * (n + 1)] for n in range(2)]
        ln_sq = [tmp[:, 0:T], tmp[:, T:2 * T]]
        ln_rst = tmp[:, 2 * T:3 * T]
        ln_v = tmp[:, 3 * T:4 * T]
        ln_sum = tmp[:, 2108:2108 + T]
        UW = T + CONV_K - 1
        U = [tmp[:, n * UW:(n + 1) * UW] for n in range(2)]
        odd = tmp[:, 2 * UW:2 * UW + T]
        conv_sg = tmp[:, 2 * UW + T:2 * UW + 2 * T]
        p_raw1 = Z[:, 14 * T:16 * T]

        POFF = (0, 128, 384, 768)
        TOFF = (0, 512, 1024, 896)

        def prob_of(ti):
            return prob[:, POFF[ti]:POFF[ti] + (ti + 1) * P]

        def pb(name):
            return ctx.enter_context(nc.psum_tensor(name, [P, T], F))

        G = [pb("G0"), pb("G1")]
        X = [pb("X0"), pb("X1"), pb("X2")]
        TB = [pb("T0"), pb("T1"), pb("T2")]
        O = X[0]
        SCORES = ((3, X[0], 0), (2, X[1], 0), (0, X[1], 3 * P), (1, X[2], 0))

        def drained(g):
            return S(f"bank_free{g.slot}"), g.half(1)

        def frees(ins, g):
            ins.then_inc(S(f"bank_free{g.slot}"), 1)

        def landed(w):
            return S(f"w_landed{w.slot}"), w.half(1) * 16

        def head_tile(h, k):
            return Idx(W_HEAD + 6 * h + k) if isinstance(h, int) else Idx(W_HEAD + k, 6, h)

        def before(w):
            return Idx(w.base - 6, w.mul, w.var)

        block = ctx.enter_context(nc.Block())

        @block.sync
        def _(sp):
            for n in range(4):
                at = slice(n * 4 * T, (n + 1) * 4 * T)
                sp.dma_start(Z[:, at], xT[:, at]).then_inc(S(f"x_landed{n}"), 16)
                if n < 2:
                    sp.dma_start(w_raw[:, n, :], wall[n]).then_inc(S(f"w_landed{n}"), 16)
            sp.wait_ge(S("w_split"), 1)
            sp.dma_start(w_raw[:, 0, :], wall[2]).then_inc(S("w_landed0"), 16)
            with sp.Fori(0, (W_TILES - 3) // 2) as i:
                for k in range(2):
                    sp.wait_ge(S("w_split"), i * 2 + (k + 2))
                    sp.dma_start(w_raw[:, 1 - k, :], wall[ds(i * 2 + (k + 3), 1)].rearrange("a p n -> p (a n)")).then_inc(
                        S(f"w_landed{1 - k}"), 16)

        @block.gpsimd
        def _(pool):
            pool.dma_start(par[:, :], par_in).then_inc(S("par_landed"), 16)
            pool.dma_start(p_raw0, pT[0]).then_inc(S("p0_landed"), 16)
            pool.dma_start(w1_sb[0], w1[0]).then_inc(S("w1k_landed"), 16)
            pool.dma_start(w1_sb[1], w1[1]).then_inc(S("w1v_landed"), 16)
            pool.dma_start(w2_sb, w2).then_inc(S("w2_landed"), 16)
            pool.wait_ge(S("p_split"), 1)
            pool.dma_start(p_raw0, masks_in).then_inc(S("msk_landed"), 16)
            for layer in range(2):
                for n in range(4):
                    pool.wait_ge(S(f"act_split{layer}"), 4 * (n + 1))
                    src = (xT, x2_dram)[layer][:, n * 4 * T:(n + 1) * 4 * T]
                    pool.dma_start(Y[:, n * 4 * T:(n + 1) * 4 * T], src).then_inc(S(f"res_landed{layer}_{n}"), 16)
                dst = (x2_dram, out)[layer]
                with pool.Fori(0, KC) as j:
                    pool.wait_ge(S(f"x_out{layer}"), j + 1)
                    pool.dma_start(chunk(dst, j), chunk(Y, j)).then_inc(S(f"stored{layer}"), 16)
                if layer == 0:
                    pool.dma_start(p_raw1, pT[1]).then_inc(S("p1_landed"), 16)
                pool.wait_ge(S(f"stored{layer}"), 16 * KC)

        @block.tensor
        def _(pe):
            def mm(o, l, r, start=True, stop=True):
                return pe.matmul(o, l, r, start=start, stop=stop)

            def gemm(w, g, acts=None):
                pe.wait_ge(S("w_split"), w.n(1))
                wait(pe, S(f"bank_free{g.slot}"), g.half())
                o = G[g.slot][:, :]
                for k in range(KC):
                    if acts:
                        pe.wait_ge(S(acts), k + 1)
                    hi, lo = w_hi[:, w.slot, k * P:(k + 1) * P], w_lo[:, w.slot, k * P:(k + 1) * P]
                    mm(o, hi, a_hi[:, k, :], k == 0, False)
                    mm(o, hi, a_lo[:, k, :], False, False)
                    last = mm(o, lo, a_hi[:, k, :], False, k == KC - 1)
                last.then_inc(S("gemm_done"), 1)

            def gemms(w, g, n):
                with pe.Fori(0, n // 2) as i:
                    for k in range(2):
                        gemm(Idx(w + k, 2, i), Idx(g + k, 2, i))

            def ple_pack(layer, u):
                w = Idx(W_PLE[layer] + u)
                pe.wait_ge(S("w_split"), w.n(1))
                pe.wait_ge(S("p_split"), layer + 1)
                for c in range(8):
                    g = Idx(G_PLE[layer] + 8 * u + c)
                    pe.wait_ge(S(f"bank_free{g.slot}"), g.half())
                    o = G[g.slot][:, :]
                    for k in range(PLE_K):
                        at = (c * PLE_K + k) * P
                        hi, lo = w_hi[:, w.slot, at:at + P], w_lo[:, w.slot, at:at + P]
                        mm(o, hi, p_hi[:, k, :], k == 0, False)
                        mm(o, hi, p_lo[:, k, :], False, False)
                        last = mm(o, lo, p_hi[:, k, :], False, k == PLE_K - 1)
                    last.then_inc(S("gemm_done" if c == 7 else "ple_done"), 1)

            gemm(Idx(0), Idx(0), acts="x_split")
            gemm(Idx(1), Idx(1))
            gemms(2, 2, 4)
            for n in range(2):
                pe.wait_ge(S("w1k_landed" if n == 0 else "w1v_landed"), 16)
                pe.wait_ge(*drained(Idx(2 * n + 1)))
                for l in range(CMP_LEN):
                    last = mm(X[n][:, 0:GROUPS * NCMP], w1_sb[n][:, l * P:(l + 1) * P], blk[n][:, l, :],
                              l == 0, l == CMP_LEN - 1)
                last.then_inc(S("cmp_hidden"), 1)
            gemm(Idx(6), Idx(6))
            pe.wait_ge(S("w2_landed"), 16)
            pe.wait_ge(S("gelu_done"), 3)
            mm(X[2][:, 0:GROUPS * NCMP], w2_sb[:, 0:P], gel_k)
            for g in range(GROUPS):
                last = mm(TB[2][:, g * P:(g + 1) * P], gel_v[:, g * P:(g + 1) * P], w2_sb[:, P:2 * P])
            last.then_inc(S("cmp_done"), 1)
            gemm(Idx(7), Idx(7))
            gemm(Idx(8), Idx(8))
            for n in range(4):
                gemm(Idx(9 + n), Idx(9 + n))
                pe.wait_ge(*drained(Idx(8 + n)))
                wait(pe, S("v_ready"), n - 1)
                for m in range(NT):
                    at = slice(m * P, (m + 1) * P)
                    last = pe.transpose(TB[n % 2][:, at], vT2[:, (n % 2) * T + m * P:(n % 2) * T + (m + 1) * P], ident)
                last.then_inc(S("v_turned"), 1)

            def scores(g, keys, cmp_too, sem):
                for ti, bank, at in SCORES:
                    n = (ti + 1) * P
                    last = mm(bank[:, at:at + n], qT[:, ti * P:(ti + 1) * P], keys[g][:, 0:n])
                if cmp_too:
                    for ti in range(NT):
                        last = mm(X[2][:, 256 + 32 * ti:256 + 32 * ti + NCMP], qT[:, ti * P:(ti + 1) * P],
                                  kcT[:, g * NCMP:(g + 1) * NCMP])
                last.then_inc(S(sem), 1)

            def turn_probs(cmp_too, sem):
                if cmp_too:
                    pe.transpose(TB[2][:, 256:384], probc, ident)
                for ti in range(NT):
                    for mj in range(ti + 1):
                        at = TOFF[mj] + (ti - mj) * P
                        last = pe.transpose(TB[at // T][:, at % T:at % T + P], prob_of(ti)[:, mj * P:(mj + 1) * P], ident)
                last.then_inc(S(sem), 1)

            def values(v, g, start, stop):
                for mj in range(NT):
                    n = T - mj * P
                    last = mm(O[:, mj * P:T], v[g][:, mj * P:(mj + 1) * P], probT[:, TOFF[mj]:TOFF[mj] + n],
                              start and mj == 0, stop and mj == NT - 1)
                return last

            def level(h, l):
                bank = X[(l + 1) % 3]
                if l == DIAG:
                    a, b = kk, qq
                else:
                    e = LEVEL_OF.index(l)
                    pe.wait_ge(S("level_ready"), h * 7 + (e + 1))
                    a = b = ring[e % 3]
                if l >= 3:
                    pe.wait_ge(S("level_copied"), h * LEVELS + (l - 2))
                for c in range(NT):
                    at = slice(c * P, (c + 1) * P)
                    last = mm(bank[:, at], a[:, at], b[:, at])
                last.then_inc(S("level_done"), 1)

            def state_sums(h):
                pe.wait_ge(S("kp_ready"), h)
                pe.wait_ge(S("vi_ready"), h)
                for c in range(NT - 1):
                    at = slice(c * P, (c + 1) * P)
                    last = mm(TB[2][:, at], kp[:, at], vi[:, at])
                last.then_inc(S("sums_done"), 1)

            def hgrn_out(h):
                pe.wait_ge(S("level_copied"), h * LEVELS)
                pe.wait_ge(S("state_ready"), h)
                for c in range(NT):
                    at = slice(c * P, (c + 1) * P)
                    last = mm(TB[0][:, at], vi[:, at], AT[:, at], True, c == 0)
                    if c:
                        last = mm(TB[0][:, at], state[:, (c - 1) * P:c * P], qg[:, at], False, True)
                last.then_inc(S("o_done"), 1)

            def head(h, g, first=False):
                w = [head_tile(h, k) for k in range(6)]
                gemm(w[0], w[0])
                if first:
                    pe.wait_ge(*drained(Idx(12)))
                    for m in range(NT):
                        last = pe.transpose(TB[2][:, 256 + 24 * m:280 + 24 * m], gT[:, m * P:(m + 1) * P],
                                            par[0:24, C_ID:C_ID + 24])
                    last.then_inc(S("gates_turned"), 1)
                else:
                    state_sums(h)
                gemm(w[1], w[1])
                if first:
                    pe.wait_ge(S("v_ready"), 4)
                    pe.wait_ge(S("cmp_ready"), 2)
                else:
                    hgrn_out(h)
                pe.wait_ge(*drained(w[0]))
                scores(g, ksT, True, "scores_s")
                gemm(w[2], w[2])
                pe.wait_ge(S("logits"), h * 12 + 8)
                scores(g, kwT, False, "scores_w")
                pe.wait_ge(S("probs"), h * 9 + 5)
                if not first:
                    pe.wait_ge(S("o_copied"), h)
                turn_probs(True, "turned_s")
                gemm(w[3], w[3])
                pe.wait_ge(S("probT_a"), h * 2 + 1)
                pe.wait_ge(S("probT_v"), h * 5 + 3)
                pe.wait_ge(S("probs"), h * 9 + 9)
                values(vs, g, True, False)
                mm(O[:, :], vc4[:, g, :], probcT, False, False)
                turn_probs(False, "turned_w")
                if not first:
                    pe.wait_ge(S("sq_ready"), h)
                    mm(X[1][:, :], ones[:, :], sq_h).then_inc(S("ms_done"), 1)
                gemm(w[4], w[4])
                pe.wait_ge(S("probT_a"), h * 2 + 2)
                pe.wait_ge(S("probT_v"), h * 5 + 5)
                values(vw, g, False, True).then_inc(S("attn_done"), 1)
                if not first:
                    pe.wait_ge(S("ms_ready"), h)
                level(h, 0)
                level(h, 1)
                gemm(w[5], w[5])
                pe.wait_ge(*drained(w[4]))
                for c in range(NT):
                    at = slice(c * P, (c + 1) * P)
                    last = pe.transpose(TB[0][:, at], viT[:, at], ident)
                last.then_inc(S("vi_turned"), 1)
                pe.wait_ge(S("kpT_ready"), h + 1)
                for c in range(NT):
                    at = slice(c * P, (c + 1) * P)
                    last = pe.transpose(TB[1][:, at], kpT[:, at], ident)
                last.then_inc(S("kp_turned"), 1)
                pe.wait_ge(S("y_attn"), h + 1)
                for l in range(2, LEVELS):
                    level(h, l)

            pe.wait_ge(S("par_landed"), 16)
            pe.wait_ge(S("ones_set"), 1)
            head(0, 0, first=True)
            with pe.Fori(1, HPG) as h:
                head(h, 0)
            with pe.Fori(HPG, HEADS) as h:
                head(h, 1)
            ple_pack(0, 0)
            state_sums(HEADS)
            hgrn_out(HEADS)
            ple_pack(0, 1)
            pe.wait_ge(S("sq_ready"), HEADS)
            mm(X[1][:, :], ones[:, :], sq_h).then_inc(S("ms_done"), 1)

            def ln_stats(n):
                pe.wait_ge(S("summed"), (n + 1) * KC)
                mm(X[0][:, :], ones[:, :], ln_sum).then_inc(S("mean_done"), 1)
                for j in range(KC):
                    pe.wait_ge(S("ln_squared"), n * KC + j + 1)
                    mm(X[2][:, :], ones[:, :], ln_sq[j % 2], j == 0, j == KC - 1).then_inc(S("ln_var"), 1)

            def second_part(layer):
                for w, g, acts in ((W_OUT, G_OUT, "act_split"), (W_GATE, G_GATE, "x1_split")):
                    gemm(Idx(w[layer]), Idx(g[layer]), acts=f"{acts}{layer}")
                    gemm(Idx(w[layer] + 1), Idx(g[layer] + 1))
                    gemms(w[layer] + 2, g[layer] + 2, KC - 2)
                    if w is W_OUT:
                        ln_stats(2 * layer)

            second_part(0)
            gemm(Idx(W_CONV), Idx(G_CONV), acts="x2_split")
            gemm(Idx(W_CONV + 1), Idx(G_CONV + 1))
            gemms(W_CONV + 2, G_CONV + 2, 3 * KC - 2)
            ln_stats(1)
            ple_pack(1, 0)
            ple_pack(1, 1)
            second_part(1)


        @block.scalar
        def _(act):
            f = act.activation

            def split(w):
                act.wait_ge(*landed(w))
                if w.mul or w.base >= 2:
                    act.wait_ge(S("gemm_done"), w.n(-1))
                f(w_hi[:, w.slot, :], w_raw[:, w.slot, :], ACT.Copy).then_inc(S("w_hi"), 1)

            def high(j, sem):
                f(a_hi[:, j, :], chunk(Y, j), ACT.Copy).then_inc(S(sem), 1)

            split(Idx(0))
            for k in range(KC):
                if k % 4 == 0:
                    act.wait_ge(S(f"x_landed{k // 4}"), 16)
                f(a_hi[:, k, :], chunk(Z, k), ACT.Copy).then_inc(S("x_hi"), 1)
            act.wait_ge(S("p0_landed"), 16)
            f(p_hi[:, :, :].rearrange("p k t -> p (k t)"), p_raw0, ACT.Copy).then_inc(S("p_hi"), 1)
            split(Idx(1))
            act.wait_ge(S("lb_step"), 1)
            f(lb[:, 0, :], lb[:, 0, :], ACT.Exp).then_inc(S("lb_exp"), 1)
            for i in range(1, 13):
                split(Idx(i + 1))
                t = Idx(i - 1)
                act.wait_ge(S("gemm_done"), i)
                if 4 <= t.base < 8:
                    frees(f((ksT + kwT)[t.base - 4], G[t.slot][:, :], ACT.Copy), t)
                if 8 <= t.base < 12:
                    n = t.base - 8
                    wait(act, S("v_turned"), n - 1)
                    if n == 0:
                        act.wait_ge(S("masks_ready"), 1)
                    frees(f(vT2[:, (n % 2) * T:(n % 2 + 1) * T], G[t.slot][:, :], ACT.Copy), t)
                if i == 6:
                    act.wait_ge(S("cmp_hidden"), 2)
                    f(gel_k, X[0][:, 0:GROUPS * NCMP], ACT.Gelu_apprx_tanh).then_inc(S("gelu_done"), 1)
                    act.wait_ge(S("pads_set"), 2)
                    src = X[1][:, 0:GROUPS * NCMP].rearrange("p (g n) -> p g n", g=GROUPS)
                    for g in range(GROUPS):
                        dst = gel_v[:, g * P:(g + 1) * P].rearrange("p (t n) -> p t n", t=NT)[:, :, 0:NCMP]
                        f(dst, src[:, g:g + 1, :].broadcast_to([P, NT, NCMP]), ACT.Gelu_apprx_tanh).then_inc(S("gelu_done"), 1)

            def prev_hz(h, hz):
                act.wait_ge(S("gemm_done"), hz.n(1))
                f(sg, G[hz.slot][:, :], ACT.Sigmoid).then_inc(S("sg_hz"), 1)
                act.wait_ge(S("vi_turned"), h)
                f(vi, TB[0][:, :], ACT.Copy).then_inc(S("vi_ready"), 1)

            def prev_square(h):
                act.wait_ge(S("o_done"), h)
                f(sq_h, TB[0][:, :], ACT.Square).then_inc(S("sq_ready"), 1)
                f(osb, TB[0][:, :], ACT.Copy).then_inc(S("o_copied"), 1)

            def prev_rms(h):
                act.wait_ge(S("ms_ready"), h)
                f(rst_h, rst_h, ACT.Ln).then_inc(S("rms_log"), 1)
                act.wait_ge(S("rms_log"), h)
                f(rst_h, rst_h, ACT.Exp, scale=-0.5).then_inc(S("rms_inv"), 1)

            def head(h, first=False):
                w = [head_tile(h, k) for k in range(7)]

                def exps(tiles, o):
                    for ti in tiles:
                        f(prob_of(ti), prob_of(ti), ACT.Exp, bias=nmx[:, o + ti:o + ti + 1],
                          accum_out=rsum[:, o + ti:o + ti + 1]).then_inc(S("exps"), 1)

                def decay(e):
                    act.wait_ge(S("gap"), h * 14 + (2 * e + 2))
                    f(ring[e % 3], ring[e % 3], ACT.Exp).then_inc(S("decay"), 1)

                split(w[1])
                if first:
                    act.wait_ge(S("gemm_done"), W_HEAD)
                    frees(f(gT, G[0][0:3 * HEADS, :], ACT.Sigmoid), Idx(12))
                else:
                    prev_hz(h, before(w[5]))
                split(w[2])
                act.wait_ge(S("gemm_done"), w[0].n(1))
                if not first:
                    act.wait_ge(S("level_done"), h * LEVELS)
                frees(f(qT, G[w[0].slot][:, :], ACT.Copy, scale=P ** -0.5), w[0])
                split(w[3])
                act.wait_ge(S("gemm_done"), w[1].n(1))
                if first:
                    act.wait_ge(S("v_turned"), 4)
                else:
                    act.wait_ge(*drained(before(w[5])))
                f(sg, G[w[1].slot][:, :], ACT.Sigmoid).then_inc(S("sg_nz"), 1)
                if not first:
                    prev_square(h)
                act.wait_ge(S("neg_max"), h * 2 + 1)
                exps(range(NT), 0)
                for ti in range(NT):
                    f(probc31[:, ti, :], probc31[:, ti, :], ACT.Exp, bias=nmx[:, 4 + ti:5 + ti],
                      accum_out=rsum[:, 4 + ti:5 + ti]).then_inc(S("exps"), 1)
                split(w[4])
                act.wait_ge(S("gemm_done"), w[2].n(1))
                act.wait_ge(*drained(w[1]))
                f(kk, G[w[2].slot][:, :], ACT.Sigmoid, scale=-1.0).then_inc(S("sg_not"), 1)
                frees(f(sg, G[w[2].slot][:, :], ACT.Sigmoid), w[2])
                act.wait_ge(S("turned_s"), h + 1)
                f(probT[:, 0:T], TB[0][:, :], ACT.Copy).then_inc(S("probT_a"), 1)
                act.wait_ge(S("neg_max"), h * 2 + 2)
                exps(range(NT), 8)
                act.wait_ge(S("f_ready"), h + 1)
                f(gg, sg, ACT.Ln).then_inc(S("logf"), 1)
                split(w[5])
                act.wait_ge(S("turned_w"), h + 1)
                f(probT[:, 0:T], TB[0][:, :], ACT.Copy).then_inc(S("probT_a"), 1)
                act.wait_ge(S("gemm_done"), w[3].n(1))
                act.wait_ge(S("logf"), h + 1)
                f(sg, G[w[3].slot][:, :], ACT.Sigmoid).then_inc(S("sg_hq"), 1)
                decay(0)
                decay(1)
                if not first:
                    prev_rms(h)
                split(w[6])
                act.wait_ge(S("gemm_done"), w[4].n(1))
                act.wait_ge(S("attn_done"), h + 1)
                frees(f(viT, G[w[4].slot][:, :], ACT.Copy), w[4])
                if not first:
                    act.wait_ge(S("y_hgrn"), h)
                f(qg, gg, ACT.Exp).then_inc(S("decay_q"), 1)
                act.wait_ge(S("gap_k"), h + 1)
                f(kpT, kpT, ACT.Exp).then_inc(S("decay_k"), 1)
                for e in range(2, 7):
                    decay(e)

            head(0, first=True)
            with act.Fori(1, HEADS) as h:
                head(h)

            def ple_out(layer, u, c):
                g = Idx(G_PLE[layer] + 8 * u + c)
                if c == 7:
                    act.wait_ge(S("gemm_done"), W_PLE[layer] + u + 1)
                else:
                    act.wait_ge(S("ple_done"), 14 * layer + 7 * u + c + 1)
                frees(f(chunk(Z, 8 * u + c), G[g.slot][:, :], ACT.Copy), g)

            split(Idx(W_PLE[0] + 1))
            prev_hz(HEADS, Idx(W_PLE[0] - 1))
            for c in range(8):
                ple_out(0, 0, c)
                high(c, "act_hi0")
            split(Idx(W_PLE[0] + 2))
            prev_square(HEADS)
            for c in range(8):
                ple_out(0, 1, c)
                if c < 7:
                    high(8 + c, "act_hi0")

            def ln_stats(n):
                for j in range(KC):
                    act.wait_ge(S("centred"), n * KC + j + 1)
                    wait(act, S("ln_var"), n * KC + j - 1 if j >= 2 or n else 0)
                    f(ln_sq[j % 2], chunk(Y, j), ACT.Square).then_inc(S("ln_squared"), 1)
                act.wait_ge(S("ln_v"), n + 1)
                f(ln_rst, ln_v, ACT.Ln).then_inc(S("ln_log"), 1)
                act.wait_ge(S("ln_log"), n + 1)
                f(ln_rst, ln_rst, ACT.Exp, scale=-0.5).then_inc(S("ln_guess"), 1)

            def second_part(layer):
                w, g = W_OUT[layer], G_OUT[layer]
                split(Idx(w + 1))
                if layer == 0:
                    prev_rms(HEADS)
                    act.wait_ge(S("y_hgrn"), HEADS)
                    high(KC - 1, "act_hi0")
                with act.Fori(0, KC // 2) as i:
                    for k in range(2):
                        split(Idx(w + 2 + k, 2, i))
                ln_stats(2 * layer)
                for j in range(KC):
                    act.wait_ge(S("normed"), 2 * layer * KC + j + 1)
                    f(chunk(Y, j), chunk(Y, j), ACT.Identity, bias=pcol(C_LNB + KC * layer, j)).then_inc(S("x1_ready"), 1)
                    act.wait_ge(S("x1_ready"), layer * KC + j + 1)
                    high(j, f"x1_hi{layer}")

                def gate(w, g, n_out):
                    act.wait_ge(S("gemm_done"), w.n(1))
                    wait(act, S(f"x_out{layer}"), n_out)
                    frees(f(ln_sq[g.slot], G[g.slot][:, :], ACT.Sigmoid), g)

                w, g = W_GATE[layer], G_GATE[layer]
                for j in range(2):
                    split(Idx(w + j + 2))
                    gate(Idx(w + j), Idx(g + j), 0)
                with act.Fori(1, KC // 2 - 1) as i:
                    for k in range(2):
                        split(Idx(w + 2 + k, 2, i))
                        gate(Idx(w + k, 2, i), Idx(g + k, 2, i), i * 2 + (k - 1))
                for j in range(KC - 2, KC):
                    if w + j + 2 < W_TILES:
                        split(Idx(w + j + 2))
                    gate(Idx(w + j), Idx(g + j), j - 1)

            second_part(0)

            act.wait_ge(S("gemm_done"), W_CONV)
            for j in range(KC):
                act.wait_ge(S("x_out0"), j + 1)
                high(j, "x2_hi")
            act.wait_ge(S("p1_landed"), 16)
            f(p_hi[:, :, :].rearrange("p k t -> p (k t)"), p_raw1, ACT.Copy).then_inc(S("p_hi"), 1)

            def silu_z(w, j):
                g = Idx(w.base - W_CONV + G_CONV, w.mul, w.var)
                act.wait_ge(S("gemm_done"), w.n(1))
                frees(f(chunk(Z, j), G[g.slot][:, :], ACT.Silu), g)

            def conv_slots(i, w, first=False):
                for k in range(6):
                    if not (first and k == 0):
                        split(w.plus(k + 1))
                    if k % 3 == 1:
                        b = w.plus(k - 1)
                        g = Idx(b.base - W_CONV + G_CONV, b.mul, b.var)
                        act.wait_ge(S("gemm_done"), b.n(1))
                        if k == 1 and not first:
                            act.wait_ge(*drained(Idx(g.base - 2, g.mul, g.var)))
                        if k == 4:
                            act.wait_ge(*drained(Idx(g.base - 2, g.mul, g.var)))
                        frees(f(conv_sg, G[g.slot][:, :], ACT.Sigmoid), g)
                    if k == 3:
                        silu_z(w.plus(2), i * 2)
                    if k == 0 and not first:
                        silu_z(w.plus(-1), i * 2 - 1)

            conv_slots(0, Idx(W_CONV), first=True)
            with act.Fori(1, KC // 2) as i:
                conv_slots(i, Idx(W_CONV, 6, i))
            split(Idx(W_PLE[1] + 1))
            act.wait_ge(S("p_split"), 2)
            silu_z(Idx(W_PLE[1] - 1), KC - 1)
            ln_stats(1)
            for j in range(KC):
                if j == 8:
                    split(Idx(W_PLE[1] + 2))
                act.wait_ge(S("normed"), KC + j + 1)
                f(chunk(Y, j), chunk(Y, j), ACT.Silu, bias=pcol(C_CB, j)).then_inc(S("silu_c"), 1)
                act.wait_ge(S("gated"), j + 1)
                high(j, "act_hi1")
                ple_out(1, j // 8, j % 8)
            second_part(1)

        @block.vector
        def _(dve):
            tt, ts, stt = dve.tensor_tensor, dve.tensor_scalar, dve.scalar_tensor_tensor

            def split(w):
                dve.wait_ge(S("w_hi"), w.n(1))
                tt(w_lo[:, w.slot, :], w_raw[:, w.slot, :], w_hi[:, w.slot, :].bitcast(F), ALU.subtract).then_inc(S("w_split"), 1)

            def low(j, src, hi_sem, sem, n=None):
                dve.wait_ge(S(hi_sem), j + 1)
                tt(a_lo[:, j, :], src, a_hi[:, j, :].bitcast(F), ALU.subtract).then_inc(S(sem), 1)

            def p_low(raw, n):
                dve.wait_ge(S("p_hi"), n)
                tt(p_lo[:, :, :].rearrange("p k t -> p (k t)"), raw,
                   p_hi[:, :, :].rearrange("p k t -> p (k t)").bitcast(F), ALU.subtract).then_inc(S("p_split"), 1)

            def wait_alone(*waits):
                for sem, value in waits:
                    dve.wait_ge(S(sem), value)
                if not isinstance(value, int):
                    dve.sem_inc(S("passed"), 1)

            def value_tile(n):
                dve.wait_ge(S("v_turned"), n + 1)
                dve.tensor_copy((vs + vw)[n], TB[n % 2][:, :]).then_inc(S("v_ready"), 1)

            dve.memset(ones[:, :], 1.0).then_inc(S("ones_set"), 1)
            dve.memset(gel_v, 0.0).then_inc(S("pads_set"), 1)
            dve.memset(probc, 0.0).then_inc(S("pads_set"), 1)
            split(Idx(0))
            for k in range(KC):
                low(k, chunk(Z, k), "x_hi", "x_split")
            p_low(p_raw0, 1)
            split(Idx(1))
            dve.wait_ge(S("par_landed"), 16)
            raw = par[:, C_LBRAW:C_LBRAW + HEADS]
            tt(lb[:, 0, :], raw, raw, ALU.subtract).then_inc(S("lb_step"), 1)
            for i in range(1, 13):
                split(Idx(i + 1))
                t = Idx(i - 1)
                if t.base < 4:
                    n, g = t.base // 2, t.base % 2
                    dve.wait_ge(S("gemm_done"), i)
                    dve.wait_ge(S("x_split"), KC)
                    src = G[t.slot][:, :].rearrange("p (n l) -> p l n", l=CMP_STRIDE)
                    for half in range(2):
                        ls = slice(half * CMP_STRIDE, (half + 1) * CMP_STRIDE)
                        pe_col = par[:, C_PE + CMP_LEN * n:C_PE + CMP_LEN * (n + 1)][:, ls].unsqueeze(2)
                        last = tt(blk[n][:, ls, g * NCMP:(g + 1) * NCMP], src[:, :, half:half + NCMP],
                                  pe_col.broadcast_to([P, CMP_STRIDE, NCMP]), ALU.add)
                    frees(last, t)
                if i == 5:
                    dve.wait_ge(S("msk_landed"), 16)
                    dve.tensor_copy(msk[:, :, :].rearrange("p l t -> p (l t)"), p_raw0).then_inc(S("masks_ready"), 1)
                    dve.wait_ge(S("lb_exp"), 1)
                    dve.reciprocal(lb[:, 1, :], lb[:, 0, :]).then_inc(S("lb_step"), 1)
                    dve.wait_ge(S("lb_step"), 2)
                    tt(lb[:, 1, :], lb[:, 0, :], lb[:, 1, :], ALU.mult).then_inc(S("lb_step"), 1)
                    dve.wait_ge(S("lb_step"), 3)
                    tt(lb[:, 2, :], lb[:, 1, :], lb[:, 1, :], ALU.subtract).then_inc(S("lb_step"), 1)
                    dve.wait_ge(S("lb_step"), 4)
                    ts(lb[:, 3, :], lb[:, 2, :], -1.0, 1.0, ALU.mult, ALU.add).then_inc(S("lb_step"), 1)
                if i == 8:
                    dve.wait_ge(S("cmp_done"), 1)
                    dve.tensor_copy(kcT[:, :], X[2][:, 0:GROUPS * NCMP]).then_inc(S("cmp_ready"), 1)
                    dve.tensor_copy(vc4[:, :, :].rearrange("p g d -> p (g d)"), TB[2][:, 0:GROUPS * P]).then_inc(S("cmp_ready"), 1)
                if 10 <= i:
                    value_tile(i - 10)

            def prev_hz(h, hz):
                dve.wait_ge(S("kp_turned"), h)
                dve.tensor_copy(kp, TB[1][:, :]).then_inc(S("kp_ready"), 1)
                dve.wait_ge(S("sg_hz"), h)
                frees(tt(hz_s, G[hz.slot][:, :], sg, ALU.mult), hz)

            def prev_state(h):
                dve.wait_ge(S("sums_done"), h)
                dve.tensor_copy(state[:, 0:P], TB[2][:, 0:P]).then_inc(S("state_step"), 1)
                dve.wait_ge(S("state_step"), h * 2 - 1)
                stt(state[:, P:2 * P], state[:, 0:P], eglast[:, 1:2], TB[2][:, P:2 * P], op0=ALU.mult, op1=ALU.add).then_inc(
                    S("state_step"), 1)
                dve.wait_ge(S("state_step"), h * 2)
                stt(state[:, 2 * P:3 * P], state[:, P:2 * P], eglast[:, 2:3], TB[2][:, 2 * P:3 * P], op0=ALU.mult,
                    op1=ALU.add).then_inc(S("state_ready"), 1)

            def prev_ms(h):
                dve.wait_ge(S("ms_done"), h)
                ts(rst_h, X[1][:, :], 1.0 / P, EPS, ALU.mult, ALU.add).then_inc(S("ms_ready"), 1)

            def prev_y(h):
                dve.wait_ge(S("rms_inv"), h)
                tt(osb, osb, rst_h, ALU.mult).then_inc(S("o_normed"), 1)
                dve.wait_ge(S("o_normed"), h)
                stt(chunk(Y, h + (HEADS - 1)), osb, pcol(C_NORM - 1, h), hz_s, op0=ALU.mult, op1=ALU.mult).then_inc(S("y_hgrn"), 1)

            def head(h, first=False):
                w = [head_tile(h, k) for k in range(7)]

                def logits(tiles, branch):
                    for ti, bank, at in SCORES:
                        n = (ti + 1) * P
                        m = 4 * branch + ti
                        dve.tensor_tensor_reduce(out=prob_of(ti), in0=bias[:, T - n:T], in1=bank[:, at:at + n], scale=1.0,
                                                 scalar=-3e38, op0=ALU.add, op1=ALU.max, accum_out=mx[:, m:m + 1]).then_inc(
                                                     S("logits"), 1)

                def normalise(branch_cols, n_exps, n_norms):
                    lo, hi = branch_cols[0][0], branch_cols[-1][0] + 4
                    dve.wait_ge(S("exps"), h * 12 + n_exps)
                    dve.reciprocal(rg[:, lo:hi], rsum[:, lo:hi]).then_inc(S("norms"), 1)
                    dve.wait_ge(S("norms"), h * 5 + n_norms)
                    for c, b in branch_cols:
                        gcol = gates[:, ds(h * 3 + b, 1), :].rearrange("p a t -> p (a t)") if not first else gates[:, b, :]
                        tt(rg[:, c:c + 4], rg[:, c:c + 4], gcol, ALU.mult).then_inc(S("norms"), 1)
                    dve.wait_ge(S("norms"), h * 5 + n_norms + len(branch_cols))

                def halves(e, buf):
                    v = buf.rearrange("p (b n) -> p b n", n=2 * HALVES[e])
                    return v[:, :, 0:HALVES[e]], v[:, :, HALVES[e]:2 * HALVES[e]]

                def gap(e):
                    g1, g2 = halves(e, gg)
                    r1, r2 = halves(e, ring[e % 3])
                    ref = g1[:, :, HALVES[e] - 1:HALVES[e]].broadcast_to(list(g1.shape))
                    tt(r1, ref, g1, ALU.subtract).then_inc(S("gap"), 1)
                    tt(r2, g2, ref, ALU.subtract).then_inc(S("gap"), 1)

                def gate_level(e):
                    dve.wait_ge(S("decay"), h * 7 + (e + 1))
                    r1, r2 = halves(e, ring[e % 3])
                    k1, _ = halves(e, kk)
                    _, q2 = halves(e, qq)
                    tt(r1, r1, k1, ALU.mult).then_inc(S("level_k"), 1)
                    tt(r2, r2, q2, ALU.mult).then_inc(S("level_ready"), 1)

                def take_level(l):
                    if l:
                        wait_alone(("level_copied", h * LEVELS + l), ("level_done", h * LEVELS + (l + 1)))
                    else:
                        dve.wait_ge(S("level_done"), h * LEVELS + 1)
                    src = X[(l + 1) % 3][:, :].rearrange("p (c t) -> p c t", c=NT)
                    dst = AT.rearrange("p (c t) -> p c t", c=NT)
                    m = msk[:, l:l + 1, :].broadcast_to([P, NT, P])
                    if l == 0:
                        tt(dst, src, m, ALU.mult).then_inc(S("level_copied"), 1)
                    else:
                        dve.copy_predicated(dst, m, src).then_inc(S("level_copied"), 1)

                split(w[1])
                if first:
                    value_tile(3)
                else:
                    prev_hz(h, before(w[5]))
                split(w[2])
                if first:
                    dve.wait_ge(S("gates_turned"), 1)
                    dve.tensor_copy(gates[:, :, :], TB[2][:, 256:256 + 24 * NT].rearrange("p (t b) -> p b t", t=NT)).then_inc(
                        S("gates_step"), 1)
                    dve.wait_ge(S("gates_step"), 1)
                    gc = gates[:, :, :].rearrange("p (h b) t -> p h b t", b=3)[:, :, 0, 0]
                    ts(gc, gc, pcol(C_SEEN, 0), None, ALU.mult).then_inc(S("gates_step"), 1)
                    dve.wait_ge(S("gates_step"), 2)
                else:
                    prev_state(h)
                slope = pcol(C_SLOPE, h)
                ts(bias[:, 0:T], par[:, C_DIST:C_DIST + T], slope, None, ALU.mult).then_inc(S("bias_ready"), 1)
                ts(bias[:, T:], par[:, C_DISTC:C_DISTC + NT * NCMP], slope, None, ALU.mult).then_inc(S("bias_ready"), 1)
                split(w[3])
                dve.wait_ge(S("sg_nz"), h + 1)
                frees(tt(nz_s, G[w[1].slot][:, :], sg, ALU.mult), w[1])
                wait_alone(("scores_s", h + 1), ("bias_ready", h * 2 + 2))
                logits(range(NT), 0)
                for ti in range(NT):
                    dve.tensor_tensor_reduce(out=probc31[:, ti, :], in0=bias[:, T + ti * NCMP:T + (ti + 1) * NCMP],
                                             in1=X[2][:, 256 + 32 * ti:256 + 32 * ti + NCMP], scale=1.0, scalar=-3e38,
                                             op0=ALU.add, op1=ALU.max, accum_out=mx[:, 4 + ti:5 + ti]).then_inc(S("logits"), 1)
                dve.wait_ge(S("logits"), h * 12 + 8)
                ts(nmx[:, 0:8], mx[:, 0:8], -1.0, None, ALU.mult).then_inc(S("neg_max"), 1)
                normalise(((0, 1), (4, 0)), 8, 1)
                for ti in range(NT):
                    ts(prob_of(ti), prob_of(ti), rg[:, ti:ti + 1], None, ALU.mult).then_inc(S("probs"), 1)
                tt(probc31, probc31, rg[:, 4:8].unsqueeze(2).broadcast_to([P, NT, NCMP]), ALU.mult).then_inc(S("probs"), 1)
                split(w[4])
                wait_alone(("scores_w", h + 1), ("turned_s", h + 1))
                logits(range(NT), 2)
                dve.wait_ge(S("logits"), h * 12 + 12)
                ts(nmx[:, 8:12], mx[:, 8:12], -1.0, None, ALU.mult).then_inc(S("neg_max"), 1)
                lbh, omlb = lb[:, 2, :], lb[:, 3, :]
                lbh, omlb = (lbh[:, 0:1], omlb[:, 0:1]) if first else (lbh[:, ds(h, 1)], omlb[:, ds(h, 1)])
                dve.wait_ge(*drained(w[2]))
                ts(sg, sg, omlb, lbh, ALU.mult, ALU.add).then_inc(S("f_step"), 1)
                dve.wait_ge(S("f_step"), h + 1)
                ts(sg, sg, LN_FLOOR, None, ALU.max).then_inc(S("f_ready"), 1)
                ts(kk, kk, omlb, None, ALU.mult).then_inc(S("k_ready"), 1)
                dve.tensor_copy(probT[:, T:2 * T], TB[1][:, :]).then_inc(S("probT_v"), 1)
                dve.tensor_copy(probT[:, 2 * T:2 * T + 256], TB[2][:, 0:256]).then_inc(S("probT_v"), 1)
                tt(probcT.rearrange("p (c t) -> p c t", c=NT), TB[2][:, 256:384].unsqueeze(1).broadcast_to([P, NT, P]),
                   par[:, C_TILE:C_TILE + NT].unsqueeze(2).broadcast_to([P, NT, P]), ALU.mult).then_inc(S("probT_v"), 1)
                normalise(((8, 2),), 12, 4)
                for ti in range(NT):
                    ts(prob_of(ti), prob_of(ti), rg[:, 8 + ti:9 + ti], None, ALU.mult).then_inc(S("probs"), 1)
                dve.wait_ge(S("logf"), h + 1)
                for c in range(NT):
                    at = gg[:, c * P:(c + 1) * P]
                    dve.tensor_tensor_scan(at, ones[:, :], at, 0.0, ALU.mult, ALU.add).then_inc(S("scan"), 1)
                split(w[5])
                dve.wait_ge(S("turned_w"), h + 1)
                dve.tensor_copy(probT[:, T:2 * T], TB[1][:, :]).then_inc(S("probT_v"), 1)
                dve.tensor_copy(probT[:, 2 * T:2 * T + 256], TB[2][:, 0:256]).then_inc(S("probT_v"), 1)
                if not first:
                    prev_ms(h)
                dve.wait_ge(S("scan"), h * 4 + 4)
                gap(0)
                gap(1)
                dve.wait_ge(S("sg_hq"), h + 1)
                frees(tt(qq, G[w[3].slot][:, :], sg, ALU.mult), w[3])
                dve.wait_ge(S("k_ready"), h + 1)
                dve.wait_ge(*drained(w[3]))
                gate_level(0)
                gate_level(1)
                if not first:
                    prev_y(h)
                split(w[6])
                dve.wait_ge(S("attn_done"), h + 1)
                tt(chunk(Y, h), O[:, :], nz_s, ALU.mult).then_inc(S("y_attn"), 1)
                g4 = gg.rearrange("p (c t) -> p c t", c=NT)
                tt(kpT.rearrange("p (c t) -> p c t", c=NT), g4[:, :, P - 1:P].broadcast_to([P, NT, P]), g4,
                   ALU.subtract).then_inc(S("gap_k"), 1)
                gap(2)
                dve.wait_ge(S("decay_q"), h + 1)
                dve.tensor_copy(eglast[:, :], qg.rearrange("p (c t) -> p c t", c=NT)[:, :, P - 1]).then_inc(S("eglast"), 1)
                dve.wait_ge(S("eglast"), h + 1)
                tt(qg, qg, qq, ALU.mult).then_inc(S("q_decayed"), 1)
                dve.wait_ge(S("decay_k"), h + 1)
                tt(kpT, kpT, kk, ALU.mult).then_inc(S("kpT_ready"), 1)
                take_level(0)
                gap(3)
                take_level(1)
                gap(4)
                gate_level(2)
                gate_level(3)
                gate_level(4)
                take_level(2)
                gap(5)
                take_level(3)
                gap(6)
                gate_level(5)
                take_level(4)
                gate_level(6)
                for l in range(5, LEVELS):
                    take_level(l)

            head(0, first=True)
            with dve.Fori(1, HEADS) as h:
                head(h)

            split(Idx(W_PLE[0] + 1))
            prev_hz(HEADS, Idx(W_PLE[0] - 1))
            for c in range(8):
                low(c, chunk(Y, c), "act_hi0", "act_split0")
            split(Idx(W_PLE[0] + 2))
            prev_state(HEADS)
            for c in range(8, KC - 1):
                low(c, chunk(Y, c), "act_hi0", "act_split0")

            def sum_tokens(j, src):
                if isinstance(j, int) and j == 0:
                    dve.tensor_copy(ln_sum, src).then_inc(S("summed"), 1)
                else:
                    tt(ln_sum, ln_sum, src, ALU.add).then_inc(S("summed"), 1)

            def ln_stats(n):
                dve.wait_ge(S("mean_done"), n + 1)
                ts(ln_v, X[0][:, :], 1.0 / D, None, ALU.mult).then_inc(S("mean_ready"), 1)
                dve.wait_ge(S("mean_ready"), n + 1)
                for j in range(KC):
                    tt(chunk(Y, j), chunk(Y, j), ln_v, ALU.subtract).then_inc(S("centred"), 1)
                dve.wait_ge(S("ln_var"), (n + 1) * KC)
                dve.wait_ge(S("centred"), (n + 1) * KC)
                ts(ln_v, X[2][:, :], 1.0 / D, EPS, ALU.mult, ALU.add).then_inc(S("ln_v"), 1)
                dve.wait_ge(S("ln_guess"), n + 1)
                tt(ln_sum, ln_rst, ln_rst, ALU.mult).then_inc(S("newton"), 1)
                dve.wait_ge(S("newton"), 4 * n + 1)
                tt(ln_sum, ln_sum, ln_v, ALU.mult).then_inc(S("newton"), 1)
                dve.wait_ge(S("newton"), 4 * n + 2)
                ts(ln_sum, ln_sum, -0.5, 1.5, ALU.mult, ALU.add).then_inc(S("newton"), 1)
                dve.wait_ge(S("newton"), 4 * n + 3)
                tt(ln_rst, ln_rst, ln_sum, ALU.mult).then_inc(S("newton"), 1)
                dve.wait_ge(S("newton"), 4 * n + 4)

            def norm(j, c_gain):
                stt(chunk(Y, j), chunk(Y, j), pcol(c_gain, j), ln_rst, op0=ALU.mult, op1=ALU.mult).then_inc(S("normed"), 1)

            def second_part(layer):
                w, g = W_OUT[layer], G_OUT[layer]

                def out_chunk(w, g, j, n_before):
                    dve.wait_ge(S("gemm_done"), w.n(1))
                    frees(stt(chunk(Y, j), chunk(Y, j), ALPHA, G[g.slot][:, :], op0=ALU.mult, op1=ALU.add), g)
                    dve.wait_ge(*drained(g))
                    wait(dve, S("summed"), n_before)
                    sum_tokens(j, chunk(Y, j))

                split(Idx(w + 1))
                if layer == 0:
                    prev_ms(HEADS)
                    prev_y(HEADS)
                    low(KC - 1, chunk(Y, KC - 1), "act_hi0", "act_split0")
                for n in range(4):
                    dve.wait_ge(S(f"res_landed{layer}_{n}"), 16)
                s0 = 2 * layer * KC
                for j in range(2):
                    split(Idx(w + j + 2))
                    out_chunk(Idx(w + j), Idx(g + j), j, s0 + j)
                with dve.Fori(1, KC // 2) as i:
                    for k in range(2):
                        split(Idx(w + 2 + k, 2, i))
                        out_chunk(Idx(w + k, 2, i), Idx(g + k, 2, i), i * 2 + k, i * 2 + (s0 + k))
                ln_stats(2 * layer)
                for j in range(KC):
                    norm(j, C_LNG + KC * layer)
                    if j:
                        low(j - 1, chunk(Y, j - 1), f"x1_hi{layer}", f"x1_split{layer}")
                low(KC - 1, chunk(Y, KC - 1), f"x1_hi{layer}", f"x1_split{layer}")

                def gate(g, j, n_gate):
                    dve.wait_ge(*drained(g))
                    tt(ln_sq[g.slot], ln_sq[g.slot], chunk(Z, j), ALU.mult).then_inc(S("ple_gated"), 1)
                    dve.wait_ge(S("ple_gated"), n_gate)
                    tt(chunk(Y, j), chunk(Y, j), ln_sq[g.slot], ALU.add).then_inc(S(f"x_out{layer}"), 1)

                w, g = W_GATE[layer], G_GATE[layer]
                with dve.Fori(0, KC // 2 - 1) as i:
                    for k in range(2):
                        split(Idx(w + 2 + k, 2, i))
                        gate(Idx(g + k, 2, i), i * 2 + k, i * 2 + (layer * KC + k + 1))
                for j in range(KC - 2, KC):
                    if w + j + 2 < W_TILES:
                        split(Idx(w + j + 2))
                    gate(Idx(g + j), j, layer * KC + j + 1)

            second_part(0)

            for j in range(KC):
                low(j, chunk(Y, j), "x2_hi", "x2_split")
            p_low(p_raw1, 2)
            for n in range(2):
                dve.memset(U[n][:, 0:CONV_K - 1], 0.0).then_inc(S("history_set"), 1)
            dve.wait_ge(S("history_set"), 2)
            dve.wait_ge(S("stored0"), 16 * KC)
            dve.wait_ge(S("x2_split"), KC)

            TAPS = (range(0, 11), range(11, 21), range(21, CONV_K))

            def taps(j, part, u):
                for n in TAPS[part]:
                    src = U[u][:, n:n + T]
                    cw = par[:, ds(j * CONV_K + (C_CW + n), 1)] if not isinstance(j, int) else pcol(C_CW + n, j * CONV_K)
                    acc = chunk(Y, j) if n % 2 == 0 else odd
                    if n == 0:
                        ts(acc, src, cw, pcol(C_CBIAS, j), ALU.mult, ALU.add).then_inc(S("tap"), 1)
                    elif n == 1:
                        ts(acc, src, cw, None, ALU.mult).then_inc(S("tap"), 1)
                    else:
                        dve.wait_ge(S("tap"), j * CONV_K + (n - 1))
                        stt(acc, src, cw, acc, op0=ALU.mult, op1=ALU.add).then_inc(S("tap"), 1)
                if part == 2:
                    dve.wait_ge(S("tap"), j * CONV_K + CONV_K)
                    tt(chunk(Y, j), chunk(Y, j), odd, ALU.add).then_inc(S("conv_done"), 1)
                    dve.wait_ge(S("conv_done"), j + 1)
                    wait(dve, S("summed"), j + KC)
                    sum_tokens(j, chunk(Y, j))

            def glu(w, u):
                g = Idx(w.base - W_CONV + G_CONV, w.mul, w.var)
                dve.wait_ge(S("gemm_done"), w.n(1))
                dve.wait_ge(*drained(Idx(g.base - 1, g.mul, g.var)))
                frees(tt(U[u][:, CONV_K - 1:UW], G[g.slot][:, :], conv_sg, ALU.mult), g)
                dve.wait_ge(*drained(g))

            def conv_slots(i, w, first=False):
                for k in range(6):
                    if not (first and k == 0):
                        split(w.plus(k + 1))
                    if k == 2 or k == 5:
                        glu(w.plus(k - 1), k // 3)
                        taps(i * 2 + k // 3, 0, k // 3)
                    if k == 3 or k == 4:
                        taps(i * 2, k - 2, 0)
                    if k < 2 and not first:
                        taps(i * 2 - 1, k + 1, 1)

            conv_slots(0, Idx(W_CONV), first=True)
            with dve.Fori(1, KC // 2) as i:
                conv_slots(i, Idx(W_CONV, 6, i))
            split(Idx(W_PLE[1] + 1))
            taps(KC - 1, 1, 1)
            taps(KC - 1, 2, 1)
            ln_stats(1)
            for j in range(KC + 1):
                if j < KC:
                    norm(j, C_CG)
                    dve.wait_ge(S("silu_c"), j + 1)
                    tt(chunk(Y, j), chunk(Y, j), chunk(Z, j), ALU.mult).then_inc(S("gated"), 1)
                if j:
                    low(j - 1, chunk(Y, j - 1), "act_hi1", "act_split1")
                if j == 8:
                    split(Idx(W_PLE[1] + 2))
            second_part(1)

    return nc


def chunks(a):
    return np.ascontiguousarray(a.reshape(-1, P, a.shape[-1]).transpose(1, 0, 2)).reshape(P, -1)


def tiles(w):
    n = w.shape[1] // P
    return w.reshape(KC, P, n, P).transpose(2, 1, 0, 3).reshape(n, P, D)


def kernel(x, p, ev_w_in, ev_cmp_pe_k, ev_cmp_w1_k, ev_cmp_w2_k, ev_cmp_pe_v, ev_cmp_w1_v, ev_cmp_w2_v, ev_hg_norm,
           hgrn_lb, ev_w_out, od_w_in, od_conv_w, od_conv_b, od_ln_g, od_ln_b, od_w_out, post_ln_g, post_ln_b, ple_w,
           ple_gate_w):
    from concourse import bacc
    from concourse.bass_utils import run_bass_kernel_spmd

    ev = np.asarray(ev_w_in)[0]
    at, parts = 0, {}
    for name, n in (("nq", 1024), ("kv", 1536), ("ng", 24), ("nz", 1024), ("hq", 1024), ("hf", 1024), ("hi", 1024), ("hz", 1024)):
        parts[name] = ev[:, at:at + n]
        at += n
    kv = tiles(parts["kv"])
    kv = kv[[0, 1, 2, 3, 4, 5, 8, 9, 6, 7, 10, 11]]
    ng = tiles(np.concatenate([parts["ng"], np.zeros((D, P - 24), np.float32)], axis=1))
    heads = np.stack([tiles(parts[n]) for n in ("nq", "nz", "hf", "hq", "hi", "hz")], axis=1).reshape(-1, P, D)

    def ple(layer):
        w = np.asarray(ple_w)[layer].reshape(PLE_K, P, 2, 8, P)
        return w.transpose(2, 1, 3, 0, 4).reshape(2, P, D)

    a, b, z = [tiles(w) for w in np.split(np.asarray(od_w_in)[0], 3, axis=1)]
    conv = np.stack([b, a, z], axis=1).reshape(-1, P, D)
    gate = np.asarray(ple_gate_w)
    wall = np.concatenate([kv, ng, heads, ple(0), tiles(np.asarray(ev_w_out)[0]), tiles(gate[0]), conv,
                           ple(1), tiles(np.asarray(od_w_out)[0]), tiles(gate[1])])

    def vec(v):
        return np.asarray(v).reshape(-1, P).T

    cols, masks = constants()
    taps = np.asarray(od_conv_w)[0].reshape(CONV_K, KC, P).transpose(2, 1, 0).reshape(P, -1)
    par = np.concatenate([vec(post_ln_g), vec(post_ln_b), vec(od_ln_g), vec(od_ln_b), vec(od_conv_b), taps,
                          vec(ev_hg_norm), vec(hgrn_lb), np.asarray(ev_cmp_pe_k)[0].T, np.asarray(ev_cmp_pe_v)[0].T, cols], axis=1)

    def w1(w):
        return np.asarray(w)[0].reshape(CMP_LEN, P, P).transpose(1, 0, 2).reshape(P, -1)

    arrays = {
        "xT": chunks(np.asarray(x)[0].T),
        "wall": wall,
        "w1": np.stack([w1(ev_cmp_w1_k), w1(ev_cmp_w1_v)]),
        "w2": np.concatenate([np.asarray(ev_cmp_w2_k)[0], np.asarray(ev_cmp_w2_v)[0]], axis=1),
        "pT": np.stack([chunks(np.asarray(p)[n, 0].T) for n in range(2)]),
        "par": par,
        "masks": masks,
    }
    arrays = {n + "_in": np.ascontiguousarray(v) for n, v in arrays.items()}
    nc = bacc.Bacc("TRN2", target_bir_lowering=False, num_devices=1)
    args = [nc.dram_tensor(n, v.shape, mybir.dt.from_np(v.dtype), kind="ExternalInput").ap() for n, v in arrays.items()]
    out = nc.dram_tensor("out", (P, KC * T), mybir.dt.float32, kind="ExternalOutput").ap()
    build(nc, *args, out)
    r = run_bass_kernel_spmd(nc, [arrays], core_ids=[0])
    y = r.results[0]["out"]
    return np.ascontiguousarray(y.reshape(P, KC, T).transpose(2, 1, 0)).reshape(1, T, D)
```

```python
import numpy as np
from contextlib import ExitStack

import concourse.bass as bass
from concourse import mybir

P = 128
T = 512
D = 2048
KC = D // P
NT = T // P
HEADS = 8
GROUPS = 2
HPG = HEADS // GROUPS
CMP_LEN, CMP_STRIDE = 32, 16
NCMP = T // CMP_STRIDE - 1
CONV_K = 31
PLE_K = 2
ALPHA = (2.0 * 2) ** 0.25
EPS = 1e-5
LAG = 6
NEG = -1e30
LN_FLOOR = 2.0 ** -63

W_KV = 0
W_HEAD = 13
W_PLE = ((61, 78), (143, 160))
W_OUT = (62, 144)
W_GATE = (79, 161)
W_CONV = 95
W_TILES = 177
G_PLE = ((61, 85), (157, 181))
G_OUT = (69, 165)
G_GATE = (93, 189)
G_CONV = 109

HALVES = (64, 32, 16, 8, 4, 2, 1)
LEVELS = 8
HALF = P // 2

MASKS = P + len(HALVES) * HALF

C_LNG = 0
C_LNB = C_LNG + 32
C_CG = C_LNB + 32
C_CB = C_CG + KC
C_CBIAS = C_CB + KC
C_CW = C_CBIAS + KC
C_NORM = C_CW + KC * CONV_K
C_LBRAW = C_NORM + HEADS
C_PE = C_LBRAW + HEADS
C_SLOPE = C_PE + 2 * CMP_LEN
C_SEEN = C_SLOPE + HEADS
C_ID = C_SEEN + 1
C_DIST = C_ID + P
C_DISTC = C_DIST + T
C_TILE = C_DISTC + NT * NCMP
NPAR = C_TILE + NT


def constants():
    t = np.arange(P)[:, None]
    slope = np.broadcast_to(2.0 ** (-8.0 * np.arange(1, HEADS + 1) / HEADS), (P, HEADS))
    seen = (t >= CMP_LEN - 1).astype(np.float32)
    x = np.arange(T)[None, :] - (T - P) - t
    dist = np.where(x <= 0, x, NEG)
    end = np.arange(NCMP) * CMP_STRIDE + CMP_LEN - 1
    tt = np.arange(NT)[None, :, None] * P + t[:, :, None]
    distc = np.where(end <= tt, end - tt, NEG).reshape(P, -1)
    tile = np.arange(P)[:, None] // 32 == np.arange(NT)[None, :]
    cols = np.concatenate([slope, seen, np.eye(P), dist, distc, tile], axis=1).astype(np.float32)
    masks = np.zeros((P, MASKS), np.float32)
    masks[:, :P] = np.eye(P)
    s, u = np.arange(P)[:, None], np.arange(P)
    for e, half in enumerate(HALVES):
        second = u[u % (2 * half) >= half]
        masks[:, P + e * HALF:P + (e + 1) * HALF] = (s // (2 * half) == second // (2 * half)) & (s % (2 * half) < half)
    return cols, masks


LN_COUNTS = dict(
    half_summed=8, shift_done=1, shift_ready=1, sums_set=3, centred=16, c_summed=15, squared=16, sq_summed=15, mean_sum=1,
    var_sum=1, ln_step=6, var=1, ln_log=1, ln_guess=1, diag_d=1, diag_r=1, mean_spread=1, dev_spread=1, less_mean=16, normed=16)


class Idx:

    def __init__(self, base, mul=0, var=0):
        self.base, self.mul, self.var = base, mul, var

    def n(self, off=0):
        return self.var * self.mul + (self.base + off) if self.mul else self.base + off

    def half(self, off=0):
        return self.var * (self.mul // 2) + (self.base // 2 + off) if self.mul else self.base // 2 + off

    def plus(self, k):
        return Idx(self.base + k, self.mul, self.var)

    @property
    def slot(self):
        return self.base % 2


def wait(eng, sem, value):
    if not isinstance(value, int) or value > 0:
        eng.wait_ge(sem, value)


def build(nc, xT, wall, w1, w2, pT, par_in, masks_in, out):
    F = mybir.dt.float32
    R = mybir.dt.float32r
    U8 = mybir.dt.uint8
    ALU = mybir.AluOpType
    ACT = mybir.ActivationFunctionType
    ds = bass.ds
    x2_dram = nc.dram_tensor("x2_residual", [P, KC * T], F).ap()

    with ExitStack() as ctx:
        def sb(name, shape, dt=F):
            return ctx.enter_context(nc.sbuf_tensor(name, shape, dt))

        sems = {}

        def S(name):
            if name not in sems:
                sems[name] = ctx.enter_context(nc.semaphore(name))
            return sems[name]

        w_raw = sb("w_raw", [P, 2, D])
        w_hi = sb("w_hi", [P, 2, D], R)
        w_lo = sb("w_lo", [P, 2, D], R)
        a_hi = sb("a_hi", [P, KC, T], R)
        a_lo = sb("a_lo", [P, KC, T], R)
        Y = sb("Y", [P, KC * T])
        Z = sb("Z", [P, KC * T])
        tmp = sb("tmp", [P, 2688])
        par = sb("par", [P, NPAR])
        msk = sb("msk", [P, MASKS], U8)
        ones = sb("ones", [P, P])
        p_hi = sb("p_hi", [P, PLE_K, T], R)
        p_lo = sb("p_lo", [P, PLE_K, T], R)
        bias = sb("bias", [P, T + NT * NCMP])
        kcT = sb("kcT", [P, GROUPS * NCMP])
        vc4 = sb("vc4", [P, GROUPS, P])
        gates = sb("gates", [P, 3 * HEADS, NT])
        mx = sb("mx", [P, 12])
        nmx = sb("nmx", [P, 12])
        rsum = sb("rsum", [P, 12])
        rg = sb("rg", [P, 12])
        eglast = sb("eglast", [P, NT])
        stat = sb("stat", [P, 5 * NT])
        lb = sb("lb", [P, 4, HEADS])
        ident = par[:, C_ID:C_ID + P]

        def pcol(c, j):
            return par[:, ds(j + c, 1)] if not isinstance(j, int) else par[:, c + j:c + j + 1]

        def chunk(buf, j):
            return buf[:, ds(j * T, T)] if not isinstance(j, int) else buf[:, j * T:(j + 1) * T]

        ksT, kwT, vs, vw = [[Z[:, (2 * n + g) * T:(2 * n + g + 1) * T] for g in range(GROUPS)] for n in range(4)]
        ZU = 8 * T
        prob = Z[:, ZU:ZU + 1280]
        qT = Z[:, ZU + 1280:ZU + 1792]
        ring = [Z[:, ZU + T * r:ZU + T * (r + 1)] for r in range(3)]
        pair = Z[:, ZU + 3 * T:ZU + 3 * T + T // 2]
        kp = Z[:, ZU:ZU + T]
        probT = Z[:, ZU + 1792:ZU + 3072]
        viT = Z[:, ZU + 1792:ZU + 1792 + T]
        kpT = Z[:, ZU + 1792 + T:ZU + 1792 + 2 * T]
        gg = Z[:, ZU + 3072:ZU + 3584]
        vi = gg
        kk = Z[:, ZU + 3584:ZU + 4096]
        blk = [Z[:, ZU + n * 1984:ZU + (n + 1) * 1984].rearrange("p (l n) -> p l n", l=CMP_LEN) for n in range(2)]
        sg = tmp[:, 0:T]
        osb = tmp[:, T:2 * T]
        qg = tmp[:, 2 * T:3 * T]
        sq_h = rst_h = qg
        qq = tmp[:, 3 * T:4 * T]
        state = tmp[:, 3 * T:3 * T + 3 * P]
        probcT = tmp[:, 4 * T:5 * T]
        AT = tmp[:, 4 * T:5 * T]
        probc = tmp[:, 5 * T:5 * T + P]
        probc31 = probc.rearrange("p (t n) -> p t n", t=NT)[:, :, 0:NCMP]
        nz_s = Y[:, 7 * T:8 * T]
        hz_s = Y[:, 15 * T:16 * T]
        p_raw0 = vT2 = tmp[:, 0:2 * T]
        gT = tmp[0:3 * HEADS, 2 * T:3 * T]
        gel_k = tmp[:, 3 * T:3 * T + GROUPS * NCMP]
        gel_v = tmp[:, 3 * T + 64:3 * T + 64 + GROUPS * P]
        w2_sb = tmp[:, 3 * T + 320:3 * T + 320 + 2 * P]
        w1_sb = [Y[:, 4096 * n:4096 * (n + 1)] for n in range(2)]
        ln_sq = [tmp[:, 0:T], tmp[:, T:2 * T]]
        ln_shift = diag_d = tmp[:, 2 * T:3 * T]
        ln_sqs = tmp[:, 3 * T:4 * T]
        ln_rst = tmp[:, 2 * T:3 * T]
        ln_v = tmp[:, 3 * T:4 * T]
        ln_sum = diag_r = tmp[:, 2108:2108 + T]
        UW = T + CONV_K - 1
        U = [tmp[:, n * UW:(n + 1) * UW] for n in range(2)]
        odd = tmp[:, 2 * UW:2 * UW + T]
        conv_sg = tmp[:, 2 * UW + T:2 * UW + 2 * T]
        p_raw1 = Z[:, 14 * T:16 * T]

        POFF = (0, 128, 384, 768)
        TOFF = (0, 512, 1024, 896)

        def prob_of(ti):
            return prob[:, POFF[ti]:POFF[ti] + (ti + 1) * P]

        def pb(name):
            return ctx.enter_context(nc.psum_tensor(name, [P, T], F))

        G = [pb("G0"), pb("G1")]
        X = [pb("X0"), pb("X1"), pb("X2")]
        TB = [pb("T0"), pb("T1"), pb("T2")]
        O = X[0]
        LEVEL_AT = ((X[1], 0), (X[2], 0), (X[2], 256), (TB[2], 0), (X[0], 0), (X[0], 256), (X[1], 0), (X[1], 256))
        LEVEL_BANK_DONE = (1, 3, 3, 4, 6, 6, 8, 8)
        SCORES = ((3, X[0], 0), (2, X[1], 0), (0, X[1], 3 * P), (1, X[2], 0))

        def drained(g):
            return S(f"bank_free{g.slot}"), g.half(1)

        def frees(ins, g):
            ins.then_inc(S(f"bank_free{g.slot}"), 1)

        def landed(w):
            return S(f"w_landed{w.slot}"), w.half(1) * 16

        def after(name, layer, n):
            return S(name), n + LN_COUNTS[name] * layer

        def head_tile(h, k):
            return Idx(W_HEAD + 6 * h + k) if isinstance(h, int) else Idx(W_HEAD + k, 6, h)

        def before(w):
            return Idx(w.base - 6, w.mul, w.var)

        block = ctx.enter_context(nc.Block())

        @block.sync
        def _(sp):
            for n in range(4):
                at = slice(n * 4 * T, (n + 1) * 4 * T)
                sp.dma_start(Z[:, at], xT[:, at]).then_inc(S(f"x_landed{n}"), 16)
                if n < 2:
                    sp.dma_start(w_raw[:, n, :], wall[n]).then_inc(S(f"w_landed{n}"), 16)
            sp.wait_ge(S("w_split"), 1)
            sp.dma_start(w_raw[:, 0, :], wall[2]).then_inc(S("w_landed0"), 16)
            with sp.Fori(0, (W_TILES - 3) // 2) as i:
                for k in range(2):
                    sp.wait_ge(S("w_split"), i * 2 + (k + 2))
                    sp.dma_start(w_raw[:, 1 - k, :], wall[ds(i * 2 + (k + 3), 1)].rearrange("a p n -> p (a n)")).then_inc(
                        S(f"w_landed{1 - k}"), 16)

        @block.gpsimd
        def _(pool):
            pool.dma_start(par[:, :], par_in).then_inc(S("par_landed"), 16)
            pool.dma_start(p_raw0, pT[0]).then_inc(S("p0_landed"), 16)
            pool.dma_start(w1_sb[0], w1[0]).then_inc(S("w1k_landed"), 16)
            pool.dma_start(w1_sb[1], w1[1]).then_inc(S("w1v_landed"), 16)
            pool.dma_start(w2_sb, w2).then_inc(S("w2_landed"), 16)
            pool.wait_ge(S("p_split"), 1)
            pool.dma_start(p_raw0[:, 0:MASKS], masks_in).then_inc(S("msk_landed"), 16)
            for layer in range(2):
                for n in range(4):
                    pool.wait_ge(S(f"act_split{layer}"), 4 * (n + 1))
                    src = (xT, x2_dram)[layer][:, n * 4 * T:(n + 1) * 4 * T]
                    pool.dma_start(Y[:, n * 4 * T:(n + 1) * 4 * T], src).then_inc(S(f"res_landed{layer}_{n}"), 16)
                for j in range(KC):
                    pool.wait_ge(S(f"x1_hi{layer}"), j + 1)
                    pool.tensor_tensor(a_lo[:, j, :], chunk(Y, j), a_hi[:, j, :].bitcast(F), ALU.subtract).then_inc(
                        S(f"x1_split{layer}"), 1)
                dst = (x2_dram, out)[layer]
                with pool.Fori(0, KC) as j:
                    pool.wait_ge(S(f"x_out{layer}"), j + 1)
                    pool.dma_start(chunk(dst, j), chunk(Y, j)).then_inc(S(f"stored{layer}"), 16)
                if layer == 0:
                    pool.dma_start(p_raw1, pT[1]).then_inc(S("p1_landed"), 16)
                pool.wait_ge(S(f"stored{layer}"), 16 * KC)

        @block.tensor
        def _(pe):
            def mm(o, l, r, start=True, stop=True):
                return pe.matmul(o, l, r, start=start, stop=stop)

            def gemm(w, g, acts=None):
                pe.wait_ge(S("w_split"), w.n(1))
                wait(pe, S(f"bank_free{g.slot}"), g.half())
                o = G[g.slot][:, :]
                for k in range(KC):
                    if acts:
                        pe.wait_ge(S(acts), k + 1)
                    hi, lo = w_hi[:, w.slot, k * P:(k + 1) * P], w_lo[:, w.slot, k * P:(k + 1) * P]
                    mm(o, hi, a_hi[:, k, :], k == 0, False)
                    mm(o, hi, a_lo[:, k, :], False, False)
                    last = mm(o, lo, a_hi[:, k, :], False, k == KC - 1)
                last.then_inc(S("gemm_done"), 1)

            def gemm_pair(w, g, acts, between=None):
                for k in range(KC + LAG):
                    for n, kn in ((0, k), (1, k - LAG)):
                        if not 0 <= kn < KC:
                            continue
                        wn, gn = Idx(w + n), Idx(g + n)
                        if kn == 0:
                            pe.wait_ge(S("w_split"), wn.n(1))
                            pe.wait_ge(S(f"bank_free{gn.slot}"), gn.half())
                        if n == 0:
                            pe.wait_ge(S(acts), k + 1)
                        o, at = G[gn.slot][:, :], slice(kn * P, (kn + 1) * P)
                        hi, lo = w_hi[:, wn.slot, at], w_lo[:, wn.slot, at]
                        mm(o, hi, a_hi[:, kn, :], kn == 0, False)
                        mm(o, hi, a_lo[:, kn, :], False, False)
                        last = mm(o, lo, a_hi[:, kn, :], False, kn == KC - 1)
                        if kn == KC - 1:
                            last.then_inc(S("gemm_done"), 1)
                    if between and k in between:
                        between[k]()

            def gemms(w, g, n):
                with pe.Fori(0, n // 2) as i:
                    for k in range(2):
                        gemm(Idx(w + k, 2, i), Idx(g + k, 2, i))

            def ple_pack(layer, u, cs=range(8)):
                w = Idx(W_PLE[layer][u])
                for c in cs:
                    if c == 0:
                        pe.wait_ge(S("w_split"), w.n(1))
                        pe.wait_ge(S("p_split"), layer + 1)
                    g = Idx(G_PLE[layer][u] + c)
                    pe.wait_ge(S(f"bank_free{g.slot}"), g.half())
                    o = G[g.slot][:, :]
                    for k in range(PLE_K):
                        at = (c * PLE_K + k) * P
                        hi, lo = w_hi[:, w.slot, at:at + P], w_lo[:, w.slot, at:at + P]
                        mm(o, hi, p_hi[:, k, :], k == 0, False)
                        mm(o, hi, p_lo[:, k, :], False, False)
                        last = mm(o, lo, p_hi[:, k, :], False, k == PLE_K - 1)
                    last.then_inc(S("gemm_done" if c == 7 else "ple_done"), 1)

            gemm(Idx(0), Idx(0), acts="x_split")
            gemm(Idx(1), Idx(1))
            gemms(2, 2, 4)
            for n in range(2):
                pe.wait_ge(S("w1k_landed" if n == 0 else "w1v_landed"), 16)
                pe.wait_ge(*drained(Idx(2 * n + 1)))
                for l in range(CMP_LEN):
                    last = mm(X[n][:, 0:GROUPS * NCMP], w1_sb[n][:, l * P:(l + 1) * P], blk[n][:, l, :],
                              l == 0, l == CMP_LEN - 1)
                last.then_inc(S("cmp_hidden"), 1)
            gemm(Idx(6), Idx(6))
            pe.wait_ge(S("w2_landed"), 16)
            pe.wait_ge(S("gelu_done"), 3)
            mm(X[2][:, 0:GROUPS * NCMP], w2_sb[:, 0:P], gel_k)
            for g in range(GROUPS):
                last = mm(TB[2][:, g * P:(g + 1) * P], gel_v[:, g * P:(g + 1) * P], w2_sb[:, P:2 * P])
            last.then_inc(S("cmp_done"), 1)
            gemm(Idx(7), Idx(7))
            gemm(Idx(8), Idx(8))
            for n in range(4):
                gemm(Idx(9 + n), Idx(9 + n))
                pe.wait_ge(*drained(Idx(8 + n)))
                wait(pe, S("v_ready"), n - 1)
                for m in range(NT):
                    at = slice(m * P, (m + 1) * P)
                    last = pe.transpose(TB[n % 2][:, at], vT2[:, (n % 2) * T + m * P:(n % 2) * T + (m + 1) * P], ident)
                last.then_inc(S("v_turned"), 1)

            def scores(g, keys, cmp_too, sem):
                for ti, bank, at in SCORES:
                    n = (ti + 1) * P
                    last = mm(bank[:, at:at + n], qT[:, ti * P:(ti + 1) * P], keys[g][:, 0:n])
                if cmp_too:
                    for ti in range(NT):
                        last = mm(X[2][:, 256 + 32 * ti:256 + 32 * ti + NCMP], qT[:, ti * P:(ti + 1) * P],
                                  kcT[:, g * NCMP:(g + 1) * NCMP])
                last.then_inc(S(sem), 1)

            def turn_probs(cmp_too, sem):
                if cmp_too:
                    pe.transpose(TB[2][:, 256:384], probc, ident)
                for ti in range(NT):
                    for mj in range(ti + 1):
                        at = TOFF[mj] + (ti - mj) * P
                        last = pe.transpose(TB[at // T][:, at % T:at % T + P], prob_of(ti)[:, mj * P:(mj + 1) * P], ident)
                last.then_inc(S(sem), 1)

            def values(v, g, start, stop):
                for mj in range(NT):
                    n = T - mj * P
                    last = mm(O[:, mj * P:T], v[g][:, mj * P:(mj + 1) * P], probT[:, TOFF[mj]:TOFF[mj] + n],
                              start and mj == 0, stop and mj == NT - 1)
                return last

            def level(h, l):
                bank, at = LEVEL_AT[l]
                for c in range(NT):
                    cs = slice(c * P, (c + 1) * P)
                    if l == 0:
                        last = mm(bank[:, cs], kk[:, cs], qq[:, cs])
                        continue
                    e = l - 1
                    half = HALVES[e]
                    if c == 0:
                        pe.wait_ge(S("level_ready"), h * 7 + l)
                    if half > 1:
                        keys = ring[e % 3][:, cs]
                        queries = keys.rearrange("p (b n) -> p b n", n=2 * half)[:, :, half:2 * half]
                    else:
                        keys, queries = kk[:, cs], pair[:, c * HALF:(c + 1) * HALF]
                    last = mm(bank[:, at + c * HALF:at + (c + 1) * HALF], keys, queries)
                last.then_inc(S("level_done"), 1)

            def state_sums(h):
                pe.wait_ge(S("kp_ready"), h)
                pe.wait_ge(S("vi_ready"), h)
                for c in range(NT - 1):
                    at = slice(c * P, (c + 1) * P)
                    last = mm(TB[2][:, at], kp[:, at], vi[:, at])
                last.then_inc(S("sums_done"), 1)

            def hgrn_out(h):
                pe.wait_ge(S("level_copied"), h * LEVELS)
                pe.wait_ge(S("state_ready"), h)
                for c in range(NT):
                    at = slice(c * P, (c + 1) * P)
                    last = mm(TB[0][:, at], vi[:, at], AT[:, at], True, c == 0)
                    if c:
                        last = mm(TB[0][:, at], state[:, (c - 1) * P:c * P], qg[:, at], False, True)
                last.then_inc(S("o_done"), 1)

            def head(h, g, first=False):
                w = [head_tile(h, k) for k in range(6)]
                gemm(w[0], w[0])
                if first:
                    pe.wait_ge(*drained(Idx(12)))
                    for m in range(NT):
                        last = pe.transpose(TB[2][:, 256 + 24 * m:280 + 24 * m], gT[:, m * P:(m + 1) * P],
                                            par[0:24, C_ID:C_ID + 24])
                    last.then_inc(S("gates_turned"), 1)
                else:
                    state_sums(h)
                gemm(w[1], w[1])
                if first:
                    pe.wait_ge(S("v_ready"), 4)
                    pe.wait_ge(S("cmp_ready"), 2)
                else:
                    hgrn_out(h)
                pe.wait_ge(*drained(w[0]))
                scores(g, ksT, True, "scores_s")
                gemm(w[2], w[2])
                pe.wait_ge(S("logits"), h * 12 + 8)
                scores(g, kwT, False, "scores_w")
                pe.wait_ge(S("probs"), h * 9 + 5)
                if not first:
                    pe.wait_ge(S("o_copied"), h)
                turn_probs(True, "turned_s")
                gemm(w[3], w[3])
                pe.wait_ge(S("probT_a"), h * 2 + 1)
                pe.wait_ge(S("probT_v"), h * 5 + 3)
                pe.wait_ge(S("probs"), h * 9 + 9)
                values(vs, g, True, False)
                mm(O[:, :], vc4[:, g, :], probcT, False, False)
                turn_probs(False, "turned_w")
                if not first:
                    pe.wait_ge(S("sq_ready"), h)
                    mm(X[1][:, :], ones[:, :], sq_h).then_inc(S("ms_done"), 1)
                gemm(w[4], w[4])
                pe.wait_ge(S("probT_a"), h * 2 + 2)
                pe.wait_ge(S("probT_v"), h * 5 + 5)
                values(vw, g, False, True).then_inc(S("attn_done"), 1)
                if not first:
                    pe.wait_ge(S("ms_ready"), h)
                pe.wait_ge(S("k_ready"), h + 1)
                pe.wait_ge(*drained(w[3]))
                for l in range(4):
                    level(h, l)
                gemm(w[5], w[5])
                pe.wait_ge(*drained(w[4]))
                for c in range(NT):
                    at = slice(c * P, (c + 1) * P)
                    last = pe.transpose(TB[0][:, at], viT[:, at], ident)
                last.then_inc(S("vi_turned"), 1)
                pe.wait_ge(S("kpT_ready"), h + 1)
                for c in range(NT):
                    at = slice(c * P, (c + 1) * P)
                    last = pe.transpose(TB[1][:, at], kpT[:, at], ident)
                last.then_inc(S("kp_turned"), 1)
                pe.wait_ge(S("y_attn"), h + 1)
                pe.wait_ge(S("level_copied"), h * LEVELS + 1)
                for l in range(4, LEVELS):
                    level(h, l)

            pe.wait_ge(S("par_landed"), 16)
            pe.wait_ge(S("ones_set"), 1)
            head(0, 0, first=True)
            with pe.Fori(1, HPG) as h:
                head(h, 0)
            with pe.Fori(HPG, HEADS) as h:
                head(h, 1)
            ple_pack(0, 0, range(0, 4))
            state_sums(HEADS)
            ple_pack(0, 0, range(4, 8))
            hgrn_out(HEADS)

            def last_square():
                pe.wait_ge(S("sq_ready"), HEADS)
                mm(X[1][:, :], ones[:, :], sq_h).then_inc(S("ms_done"), 1)

            def c_stats():
                pe.wait_ge(S("summed"), KC)
                mm(X[0][:, :], ones[:, :], ln_sum).then_inc(S("mean_done"), 1)
                for j in range(KC):
                    pe.wait_ge(S("ln_squared"), j + 1)
                    mm(X[2][:, :], ones[:, :], ln_sq[j % 2], j == 0, j == KC - 1).then_inc(S("ln_var"), 1)

            def to_tokens(bank, a, b):
                for m in range(NT):
                    o, tokens = bank[:, m:m + 1], slice(m * P, (m + 1) * P)
                    mm(o, a[:, tokens], ones[:, 0:1], True, False)
                    last = mm(o, b[:, tokens], ones[:, 0:1], False, True)
                return last

            def second_part(layer, between=None):
                w, g = W_OUT[layer], G_OUT[layer]
                gemm_pair(w, g, f"act_split{layer}", between)
                gemms(w + 2, g + 2, 6)
                gemm(Idx(w + 8), Idx(g + 8))
                pe.wait_ge(*after("half_summed", layer, KC // 2))
                mm(X[0][:, :], ones[:, :], ln_sum).then_inc(S("shift_done"), 1)
                gemms(w + 9, g + 9, 6)
                gemm(Idx(w + 15), Idx(g + 15))
                ple_pack(layer, 1, range(0, 1))
                pe.wait_ge(*after("shift_ready", layer, 1))
                pe.wait_ge(*after("c_summed", layer, KC - 1))
                pe.wait_ge(*after("centred", layer, KC))
                to_tokens(X[0], ln_sum, chunk(Y, KC - 1)).then_inc(S("mean_sum"), 1)
                ple_pack(layer, 1, range(1, 2))
                pe.wait_ge(*after("sq_summed", layer, KC - 1))
                pe.wait_ge(*after("squared", layer, KC))
                to_tokens(TB[0], ln_sqs, ln_sq[(KC - 1) % 2]).then_inc(S("var_sum"), 1)
                ple_pack(layer, 1, range(2, 4))
                pe.wait_ge(*after("diag_d", layer, 1))
                mm(X[1][:, :], ones[:, :], diag_d).then_inc(S("mean_spread"), 1)
                ple_pack(layer, 1, range(4, 7))
                pe.wait_ge(*after("diag_r", layer, 1))
                mm(X[2][:, :], ones[:, :], diag_r).then_inc(S("dev_spread"), 1)
                ple_pack(layer, 1, range(7, 8))
                w, g = W_GATE[layer], G_GATE[layer]
                gemm_pair(w, g, f"x1_split{layer}")
                gemms(w + 2, g + 2, KC - 2)

            second_part(0, {2: last_square})
            gemm_pair(W_CONV, G_CONV, "x2_split")
            gemms(W_CONV + 2, G_CONV + 2, 3 * KC - 2)
            c_stats()
            ple_pack(1, 0)
            second_part(1)


        @block.scalar
        def _(act):
            f = act.activation

            def split(w):
                act.wait_ge(*landed(w))
                if w.mul or w.base >= 2:
                    act.wait_ge(S("gemm_done"), w.n(-1))
                f(w_hi[:, w.slot, :], w_raw[:, w.slot, :], ACT.Copy).then_inc(S("w_hi"), 1)

            def high(j, sem):
                f(a_hi[:, j, :], chunk(Y, j), ACT.Copy).then_inc(S(sem), 1)

            split(Idx(0))
            for k in range(KC):
                if k % 4 == 0:
                    act.wait_ge(S(f"x_landed{k // 4}"), 16)
                f(a_hi[:, k, :], chunk(Z, k), ACT.Copy).then_inc(S("x_hi"), 1)
            act.wait_ge(S("p0_landed"), 16)
            f(p_hi[:, :, :].rearrange("p k t -> p (k t)"), p_raw0, ACT.Copy).then_inc(S("p_hi"), 1)
            split(Idx(1))
            act.wait_ge(S("lb_step"), 1)
            f(lb[:, 0, :], lb[:, 0, :], ACT.Exp).then_inc(S("lb_exp"), 1)
            for i in range(1, 13):
                split(Idx(i + 1))
                t = Idx(i - 1)
                act.wait_ge(S("gemm_done"), i)
                if 4 <= t.base < 8:
                    frees(f((ksT + kwT)[t.base - 4], G[t.slot][:, :], ACT.Copy), t)
                if 8 <= t.base < 12:
                    n = t.base - 8
                    wait(act, S("v_turned"), n - 1)
                    if n == 0:
                        act.wait_ge(S("masks_ready"), 1)
                    frees(f(vT2[:, (n % 2) * T:(n % 2 + 1) * T], G[t.slot][:, :], ACT.Copy), t)
                if i == 6:
                    act.wait_ge(S("cmp_hidden"), 2)
                    f(gel_k, X[0][:, 0:GROUPS * NCMP], ACT.Gelu_apprx_tanh).then_inc(S("gelu_done"), 1)
                    act.wait_ge(S("pads_set"), 2)
                    src = X[1][:, 0:GROUPS * NCMP].rearrange("p (g n) -> p g n", g=GROUPS)
                    for g in range(GROUPS):
                        dst = gel_v[:, g * P:(g + 1) * P].rearrange("p (t n) -> p t n", t=NT)[:, :, 0:NCMP]
                        f(dst, src[:, g:g + 1, :].broadcast_to([P, NT, NCMP]), ACT.Gelu_apprx_tanh).then_inc(S("gelu_done"), 1)

            def prev_hz(h, hz):
                act.wait_ge(S("gemm_done"), hz.n(1))
                f(sg, G[hz.slot][:, :], ACT.Sigmoid).then_inc(S("sg_hz"), 1)
                act.wait_ge(S("vi_turned"), h)
                act.wait_ge(S("decay_q"), h)
                f(vi, TB[0][:, :], ACT.Copy).then_inc(S("vi_ready"), 1)

            def prev_square(h):
                act.wait_ge(S("o_done"), h)
                f(sq_h, TB[0][:, :], ACT.Square).then_inc(S("sq_ready"), 1)
                f(osb, TB[0][:, :], ACT.Copy).then_inc(S("o_copied"), 1)

            def prev_rms(h):
                act.wait_ge(S("ms_ready"), h)
                f(rst_h, rst_h, ACT.Ln).then_inc(S("rms_log"), 1)
                act.wait_ge(S("rms_log"), h)
                f(rst_h, rst_h, ACT.Exp, scale=-0.5).then_inc(S("rms_inv"), 1)

            def head(h, first=False):
                w = [head_tile(h, k) for k in range(7)]

                def exps(tiles, o):
                    for ti in tiles:
                        f(prob_of(ti), prob_of(ti), ACT.Exp, bias=nmx[:, o + ti:o + ti + 1],
                          accum_out=rsum[:, o + ti:o + ti + 1]).then_inc(S("exps"), 1)

                def decay(e):
                    act.wait_ge(S("gap"), h * 13 + min(2 * e + 2, 13))
                    buf = ring[e % 3] if e < 6 else pair
                    f(buf, buf, ACT.Exp).then_inc(S("decay"), 1)

                split(w[1])
                if first:
                    act.wait_ge(S("gemm_done"), W_HEAD)
                    frees(f(gT, G[0][0:3 * HEADS, :], ACT.Sigmoid), Idx(12))
                else:
                    prev_hz(h, before(w[5]))
                split(w[2])
                act.wait_ge(S("gemm_done"), w[0].n(1))
                if not first:
                    act.wait_ge(S("level_done"), h * LEVELS)
                frees(f(qT, G[w[0].slot][:, :], ACT.Copy, scale=P ** -0.5), w[0])
                split(w[3])
                act.wait_ge(S("gemm_done"), w[1].n(1))
                if first:
                    act.wait_ge(S("v_turned"), 4)
                else:
                    act.wait_ge(*drained(before(w[5])))
                f(sg, G[w[1].slot][:, :], ACT.Sigmoid).then_inc(S("sg_nz"), 1)
                if not first:
                    prev_square(h)
                act.wait_ge(S("neg_max"), h * 2 + 1)
                exps(range(NT), 0)
                for ti in range(NT):
                    f(probc31[:, ti, :], probc31[:, ti, :], ACT.Exp, bias=nmx[:, 4 + ti:5 + ti],
                      accum_out=rsum[:, 4 + ti:5 + ti]).then_inc(S("exps"), 1)
                split(w[4])
                act.wait_ge(S("gemm_done"), w[2].n(1))
                act.wait_ge(*drained(w[1]))
                f(kk, G[w[2].slot][:, :], ACT.Sigmoid, scale=-1.0).then_inc(S("sg_not"), 1)
                frees(f(sg, G[w[2].slot][:, :], ACT.Sigmoid), w[2])
                act.wait_ge(S("turned_s"), h + 1)
                f(probT[:, 0:T], TB[0][:, :], ACT.Copy).then_inc(S("probT_a"), 1)
                act.wait_ge(S("neg_max"), h * 2 + 2)
                exps(range(NT), 8)
                act.wait_ge(S("f_ready"), h + 1)
                f(gg, sg, ACT.Ln).then_inc(S("logf"), 1)
                split(w[5])
                act.wait_ge(S("turned_w"), h + 1)
                f(probT[:, 0:T], TB[0][:, :], ACT.Copy).then_inc(S("probT_a"), 1)
                act.wait_ge(S("gemm_done"), w[3].n(1))
                act.wait_ge(S("logf"), h + 1)
                f(sg, G[w[3].slot][:, :], ACT.Sigmoid).then_inc(S("sg_hq"), 1)
                for e in range(3):
                    decay(e)
                if not first:
                    prev_rms(h)
                split(w[6])
                act.wait_ge(S("gemm_done"), w[4].n(1))
                act.wait_ge(S("attn_done"), h + 1)
                frees(f(viT, G[w[4].slot][:, :], ACT.Copy), w[4])
                if not first:
                    act.wait_ge(S("y_hgrn"), h)
                f(qg, gg, ACT.Exp).then_inc(S("decay_q"), 1)
                act.wait_ge(S("gap_k"), h + 1)
                f(kpT, kpT, ACT.Exp).then_inc(S("decay_k"), 1)
                for e in range(3, 7):
                    decay(e)

            head(0, first=True)
            with act.Fori(1, HEADS) as h:
                head(h)

            def ple_out(layer, u, c):
                g = Idx(G_PLE[layer][u] + c)
                if c == 7:
                    act.wait_ge(S("gemm_done"), W_PLE[layer][u] + 1)
                else:
                    act.wait_ge(S("ple_done"), 14 * layer + 7 * u + c + 1)
                frees(f(chunk(Z, 8 * u + c), G[g.slot][:, :], ACT.Copy), g)

            split(Idx(W_OUT[0]))
            prev_hz(HEADS, Idx(W_PLE[0][0] - 1))
            for c in range(4):
                ple_out(0, 0, c)
                high(c, "act_hi0")
            for c in range(4, 8):
                ple_out(0, 0, c)
                high(c, "act_hi0")
            split(Idx(W_OUT[0] + 1))
            prev_square(HEADS)
            for c in range(8, KC - 1):
                high(c, "act_hi0")

            def c_stats():
                for j in range(KC):
                    act.wait_ge(S("conv_centred"), j + 1)
                    wait(act, S("ln_var"), j - 1)
                    f(ln_sq[j % 2], chunk(Y, j), ACT.Square).then_inc(S("ln_squared"), 1)
                act.wait_ge(S("ln_v"), 1)
                f(ln_rst, ln_v, ACT.Ln).then_inc(S("conv_ln_log"), 1)
                act.wait_ge(S("conv_ln_log"), 1)
                f(ln_rst, ln_rst, ACT.Exp, scale=-0.5).then_inc(S("conv_ln_guess"), 1)

            def second_part(layer):
                w, g = W_OUT[layer], G_OUT[layer]
                if layer == 0:
                    prev_rms(HEADS)
                    act.wait_ge(S("y_hgrn"), HEADS)
                    high(KC - 1, "act_hi0")

                def square(c, slot, again=True):
                    act.wait_ge(*after("centred", layer, c + 1))
                    if again:
                        act.wait_ge(*after("sq_summed", layer, c - 1))
                    f(ln_sq[slot], chunk(Y, c), ACT.Square).then_inc(S("squared"), 1)

                with act.Fori(0, KC // 4) as i:
                    for k in range(2):
                        split(Idx(w + 2 + k, 2, i))
                split(Idx(w + 10))
                for c in range(3):
                    square(c, c % 2, c >= 2)
                with act.Fori(0, 3) as i:
                    for k in range(2):
                        split(Idx(w + 11 + k, 2, i))
                        for n in range(2):
                            square(i * 4 + (3 + 2 * k + n), (1 + n) % 2)
                split(Idx(w + 17))
                square(KC - 1, (KC - 1) % 2)
                ple_out(layer, 1, 0)
                ple_out(layer, 1, 1)
                var, dev = stat[:, 2 * NT:3 * NT], stat[:, 3 * NT:4 * NT]
                act.wait_ge(*after("var", layer, 1))
                f(dev, var, ACT.Ln).then_inc(S("ln_log"), 1)
                act.wait_ge(*after("ln_log", layer, 1))
                f(dev, dev, ACT.Exp, scale=-0.5).then_inc(S("ln_guess"), 1)

                def x1_high(j):
                    act.wait_ge(S(f"x1_ready{layer}"), j + 1)
                    high(j, f"x1_hi{layer}")

                for c in range(2, 6):
                    ple_out(layer, 1, c)
                for j in range(KC):
                    if j == 0:
                        ple_out(layer, 1, 6)
                    if j == 1:
                        ple_out(layer, 1, 7)
                    if j == 2:
                        split(Idx(w + 18))
                    act.wait_ge(*after("normed", layer, j + 1))
                    f(chunk(Y, j), chunk(Y, j), ACT.Identity, scale=pcol(C_LNG + KC * layer, j),
                      bias=pcol(C_LNB + KC * layer, j)).then_inc(S(f"x1_ready{layer}"), 1)
                    if j:
                        x1_high(j - 1)
                x1_high(KC - 1)

                def gate(w, g, n_out):
                    act.wait_ge(S("gemm_done"), w.n(1))
                    wait(act, S(f"x_out{layer}"), n_out)
                    frees(f(ln_sq[g.slot], G[g.slot][:, :], ACT.Sigmoid), g)

                w, g = W_GATE[layer], G_GATE[layer]
                for j in range(2):
                    split(Idx(w + j + 2))
                    gate(Idx(w + j), Idx(g + j), 0)
                with act.Fori(1, KC // 2 - 1) as i:
                    for k in range(2):
                        split(Idx(w + 2 + k, 2, i))
                        gate(Idx(w + k, 2, i), Idx(g + k, 2, i), i * 2 + (k - 1))
                gate_end = W_GATE[layer] + KC
                if gate_end < W_TILES:
                    split(Idx(gate_end))
                gate(Idx(gate_end - 2), Idx(g + KC - 2), KC - 3)
                if layer == 0:
                    act.wait_ge(S("gemm_done"), W_CONV)
                    for j in range(3):
                        act.wait_ge(S("x_out0"), j + 1)
                        high(j, "x2_hi")
                gate(Idx(gate_end - 1), Idx(g + KC - 1), KC - 2)

            second_part(0)

            for j in range(3, KC):
                act.wait_ge(S("x_out0"), j + 1)
                high(j, "x2_hi")
                if j == 8:
                    split(Idx(W_CONV + 1))
            act.wait_ge(S("p1_landed"), 16)
            f(p_hi[:, :, :].rearrange("p k t -> p (k t)"), p_raw1, ACT.Copy).then_inc(S("p_hi"), 1)

            def silu_z(w, j):
                g = Idx(w.base - W_CONV + G_CONV, w.mul, w.var)
                act.wait_ge(S("gemm_done"), w.n(1))
                frees(f(chunk(Z, j), G[g.slot][:, :], ACT.Silu), g)

            def conv_slots(i, w, first=False):
                for k in range(6):
                    if not (first and k == 0):
                        split(w.plus(k + 1))
                    if k % 3 == 1:
                        b = w.plus(k - 1)
                        g = Idx(b.base - W_CONV + G_CONV, b.mul, b.var)
                        act.wait_ge(S("gemm_done"), b.n(1))
                        if k == 1 and not first:
                            act.wait_ge(*drained(Idx(g.base - 2, g.mul, g.var)))
                        if k == 4:
                            act.wait_ge(*drained(Idx(g.base - 2, g.mul, g.var)))
                        frees(f(conv_sg, G[g.slot][:, :], ACT.Sigmoid), g)
                    if k == 3:
                        silu_z(w.plus(2), i * 2)
                    if k == 0 and not first:
                        silu_z(w.plus(-1), i * 2 - 1)

            conv_slots(0, Idx(W_CONV), first=True)
            with act.Fori(1, KC // 2) as i:
                conv_slots(i, Idx(W_CONV, 6, i))
            split(Idx(W_OUT[1]))
            act.wait_ge(S("p_split"), 2)
            silu_z(Idx(W_PLE[1][0] - 1), KC - 1)
            c_stats()
            for j in range(KC):
                act.wait_ge(S("conv_normed"), j + 1)
                f(chunk(Y, j), chunk(Y, j), ACT.Silu, bias=pcol(C_CB, j)).then_inc(S("silu_c"), 1)
                act.wait_ge(S("gated"), j + 1)
                high(j, "act_hi1")
                if j < 8:
                    ple_out(1, 0, j)
                if j == 8:
                    split(Idx(W_OUT[1] + 1))
            second_part(1)

        @block.vector
        def _(dve):
            tt, ts, stt = dve.tensor_tensor, dve.tensor_scalar, dve.scalar_tensor_tensor

            def split(w):
                dve.wait_ge(S("w_hi"), w.n(1))
                tt(w_lo[:, w.slot, :], w_raw[:, w.slot, :], w_hi[:, w.slot, :].bitcast(F), ALU.subtract).then_inc(S("w_split"), 1)

            def low(j, src, hi_sem, sem, n=None):
                dve.wait_ge(S(hi_sem), j + 1)
                tt(a_lo[:, j, :], src, a_hi[:, j, :].bitcast(F), ALU.subtract).then_inc(S(sem), 1)

            def p_low(raw, n):
                dve.wait_ge(S("p_hi"), n)
                tt(p_lo[:, :, :].rearrange("p k t -> p (k t)"), raw,
                   p_hi[:, :, :].rearrange("p k t -> p (k t)").bitcast(F), ALU.subtract).then_inc(S("p_split"), 1)

            def wait_alone(*waits):
                for sem, value in waits:
                    dve.wait_ge(S(sem), value)
                if not isinstance(value, int):
                    dve.sem_inc(S("passed"), 1)

            def value_tile(n):
                dve.wait_ge(S("v_turned"), n + 1)
                dve.tensor_copy((vs + vw)[n], TB[n % 2][:, :]).then_inc(S("v_ready"), 1)

            dve.memset(ones[:, :], 1.0).then_inc(S("ones_set"), 1)
            dve.memset(gel_v, 0.0).then_inc(S("pads_set"), 1)
            dve.memset(probc, 0.0).then_inc(S("pads_set"), 1)
            split(Idx(0))
            for k in range(KC):
                low(k, chunk(Z, k), "x_hi", "x_split")
            p_low(p_raw0, 1)
            split(Idx(1))
            dve.wait_ge(S("par_landed"), 16)
            raw = par[:, C_LBRAW:C_LBRAW + HEADS]
            tt(lb[:, 0, :], raw, raw, ALU.subtract).then_inc(S("lb_step"), 1)
            for i in range(1, 13):
                split(Idx(i + 1))
                t = Idx(i - 1)
                if t.base < 4:
                    n, g = t.base // 2, t.base % 2
                    dve.wait_ge(S("gemm_done"), i)
                    dve.wait_ge(S("x_split"), KC)
                    src = G[t.slot][:, :].rearrange("p (n l) -> p l n", l=CMP_STRIDE)
                    for half in range(2):
                        ls = slice(half * CMP_STRIDE, (half + 1) * CMP_STRIDE)
                        pe_col = par[:, C_PE + CMP_LEN * n:C_PE + CMP_LEN * (n + 1)][:, ls].unsqueeze(2)
                        last = tt(blk[n][:, ls, g * NCMP:(g + 1) * NCMP], src[:, :, half:half + NCMP],
                                  pe_col.broadcast_to([P, CMP_STRIDE, NCMP]), ALU.add)
                    frees(last, t)
                if i == 5:
                    dve.wait_ge(S("msk_landed"), 16)
                    dve.tensor_copy(msk[:, :], p_raw0[:, 0:MASKS]).then_inc(S("masks_ready"), 1)
                    dve.wait_ge(S("lb_exp"), 1)
                    dve.reciprocal(lb[:, 1, :], lb[:, 0, :]).then_inc(S("lb_step"), 1)
                    dve.wait_ge(S("lb_step"), 2)
                    tt(lb[:, 1, :], lb[:, 0, :], lb[:, 1, :], ALU.mult).then_inc(S("lb_step"), 1)
                    dve.wait_ge(S("lb_step"), 3)
                    tt(lb[:, 2, :], lb[:, 1, :], lb[:, 1, :], ALU.subtract).then_inc(S("lb_step"), 1)
                    dve.wait_ge(S("lb_step"), 4)
                    ts(lb[:, 3, :], lb[:, 2, :], -1.0, 1.0, ALU.mult, ALU.add).then_inc(S("lb_step"), 1)
                if i == 8:
                    dve.wait_ge(S("cmp_done"), 1)
                    dve.tensor_copy(kcT[:, :], X[2][:, 0:GROUPS * NCMP]).then_inc(S("cmp_ready"), 1)
                    dve.tensor_copy(vc4[:, :, :].rearrange("p g d -> p (g d)"), TB[2][:, 0:GROUPS * P]).then_inc(S("cmp_ready"), 1)
                if 10 <= i:
                    value_tile(i - 10)

            def prev_hz(h, hz):
                dve.wait_ge(S("kp_turned"), h)
                dve.tensor_copy(kp, TB[1][:, :]).then_inc(S("kp_ready"), 1)
                dve.wait_ge(S("sg_hz"), h)
                frees(tt(hz_s, G[hz.slot][:, :], sg, ALU.mult), hz)

            def prev_state(h):
                dve.wait_ge(S("sums_done"), h)
                dve.tensor_copy(state[:, 0:P], TB[2][:, 0:P]).then_inc(S("state_step"), 1)
                dve.wait_ge(S("state_step"), h * 2 - 1)
                stt(state[:, P:2 * P], state[:, 0:P], eglast[:, 1:2], TB[2][:, P:2 * P], op0=ALU.mult, op1=ALU.add).then_inc(
                    S("state_step"), 1)
                dve.wait_ge(S("state_step"), h * 2)
                stt(state[:, 2 * P:3 * P], state[:, P:2 * P], eglast[:, 2:3], TB[2][:, 2 * P:3 * P], op0=ALU.mult,
                    op1=ALU.add).then_inc(S("state_ready"), 1)

            def prev_ms(h):
                dve.wait_ge(S("ms_done"), h)
                ts(rst_h, X[1][:, :], 1.0 / P, EPS, ALU.mult, ALU.add).then_inc(S("ms_ready"), 1)

            def prev_y(h):
                dve.wait_ge(S("rms_inv"), h)
                tt(osb, osb, rst_h, ALU.mult).then_inc(S("o_normed"), 1)
                dve.wait_ge(S("o_normed"), h)
                stt(chunk(Y, h + (HEADS - 1)), osb, pcol(C_NORM - 1, h), hz_s, op0=ALU.mult, op1=ALU.mult).then_inc(S("y_hgrn"), 1)

            def head(h, first=False):
                w = [head_tile(h, k) for k in range(7)]

                def logits(tiles, branch):
                    for ti, bank, at in SCORES:
                        n = (ti + 1) * P
                        m = 4 * branch + ti
                        dve.tensor_tensor_reduce(out=prob_of(ti), in0=bias[:, T - n:T], in1=bank[:, at:at + n], scale=1.0,
                                                 scalar=-3e38, op0=ALU.add, op1=ALU.max, accum_out=mx[:, m:m + 1]).then_inc(
                                                     S("logits"), 1)

                def normalise(branch_cols, n_exps, n_norms):
                    lo, hi = branch_cols[0][0], branch_cols[-1][0] + 4
                    dve.wait_ge(S("exps"), h * 12 + n_exps)
                    dve.reciprocal(rg[:, lo:hi], rsum[:, lo:hi]).then_inc(S("norms"), 1)
                    dve.wait_ge(S("norms"), h * 5 + n_norms)
                    for c, b in branch_cols:
                        gcol = gates[:, ds(h * 3 + b, 1), :].rearrange("p a t -> p (a t)") if not first else gates[:, b, :]
                        tt(rg[:, c:c + 4], rg[:, c:c + 4], gcol, ALU.mult).then_inc(S("norms"), 1)
                    dve.wait_ge(S("norms"), h * 5 + n_norms + len(branch_cols))

                def halves(e, buf):
                    v = buf.rearrange("p (b n) -> p b n", n=2 * HALVES[e])
                    return v[:, :, 0:HALVES[e]], v[:, :, HALVES[e]:2 * HALVES[e]]

                def gap(e):
                    if e == 6:
                        g1, g2 = halves(e, gg)
                        tt(pair.unsqueeze(2), g2, g1, ALU.subtract).then_inc(S("gap"), 1)
                        return
                    g1, g2 = halves(e, gg)
                    r1, r2 = halves(e, ring[e % 3])
                    ref = g1[:, :, HALVES[e] - 1:HALVES[e]].broadcast_to(list(g1.shape))
                    tt(r1, ref, g1, ALU.subtract).then_inc(S("gap"), 1)
                    tt(r2, g2, ref, ALU.subtract).then_inc(S("gap"), 1)

                def gate_level(e):
                    dve.wait_ge(S("decay"), h * 7 + (e + 1))
                    if e == 6:
                        tt(pair.unsqueeze(2), pair.unsqueeze(2), halves(e, qq)[1], ALU.mult).then_inc(S("level_ready"), 1)
                        return
                    r1, r2 = halves(e, ring[e % 3])
                    k1, _ = halves(e, kk)
                    _, q2 = halves(e, qq)
                    tt(r1, r1, k1, ALU.mult).then_inc(S("level_k"), 1)
                    tt(r2, r2, q2, ALU.mult).then_inc(S("level_ready"), 1)

                def take_level(l):
                    if l:
                        wait_alone(("level_copied", h * LEVELS + l), ("level_done", h * LEVELS + LEVEL_BANK_DONE[l]))
                    else:
                        dve.wait_ge(S("level_done"), h * LEVELS + 1)
                    bank, at = LEVEL_AT[l]
                    n = P if l == 0 else HALF
                    half = P if l == 0 else HALVES[l - 1]
                    src = bank[:, at:at + NT * n].rearrange("p (c b n) -> p c b n", c=NT, n=half)
                    m0 = 0 if l == 0 else P + (l - 1) * HALF
                    m = msk[:, m0:m0 + n].rearrange("p (a b n) -> p a b n", a=1, n=half).broadcast_to([P, NT, n // half, half])
                    if l == 0:
                        dst = AT.rearrange("p (c b n) -> p c b n", c=NT, n=half)
                        tt(dst, src, m, ALU.mult).then_inc(S("level_copied"), 1)
                    else:
                        dst = AT.rearrange("p (c b n) -> p c b n", c=NT, n=2 * half)[:, :, :, half:2 * half]
                        dve.copy_predicated(dst, m, src).then_inc(S("level_copied"), 1)

                split(w[1])
                if first:
                    value_tile(3)
                else:
                    prev_hz(h, before(w[5]))
                split(w[2])
                if first:
                    dve.wait_ge(S("gates_turned"), 1)
                    dve.tensor_copy(gates[:, :, :], TB[2][:, 256:256 + 24 * NT].rearrange("p (t b) -> p b t", t=NT)).then_inc(
                        S("gates_step"), 1)
                    dve.wait_ge(S("gates_step"), 1)
                    gc = gates[:, :, :].rearrange("p (h b) t -> p h b t", b=3)[:, :, 0, 0]
                    ts(gc, gc, pcol(C_SEEN, 0), None, ALU.mult).then_inc(S("gates_step"), 1)
                    dve.wait_ge(S("gates_step"), 2)
                else:
                    prev_state(h)
                slope = pcol(C_SLOPE, h)
                ts(bias[:, 0:T], par[:, C_DIST:C_DIST + T], slope, None, ALU.mult).then_inc(S("bias_ready"), 1)
                ts(bias[:, T:], par[:, C_DISTC:C_DISTC + NT * NCMP], slope, None, ALU.mult).then_inc(S("bias_ready"), 1)
                split(w[3])
                dve.wait_ge(S("sg_nz"), h + 1)
                frees(tt(nz_s, G[w[1].slot][:, :], sg, ALU.mult), w[1])
                wait_alone(("scores_s", h + 1), ("bias_ready", h * 2 + 2))
                logits(range(NT), 0)
                for ti in range(NT):
                    dve.tensor_tensor_reduce(out=probc31[:, ti, :], in0=bias[:, T + ti * NCMP:T + (ti + 1) * NCMP],
                                             in1=X[2][:, 256 + 32 * ti:256 + 32 * ti + NCMP], scale=1.0, scalar=-3e38,
                                             op0=ALU.add, op1=ALU.max, accum_out=mx[:, 4 + ti:5 + ti]).then_inc(S("logits"), 1)
                dve.wait_ge(S("logits"), h * 12 + 8)
                ts(nmx[:, 0:8], mx[:, 0:8], -1.0, None, ALU.mult).then_inc(S("neg_max"), 1)
                normalise(((0, 1), (4, 0)), 8, 1)
                for ti in range(NT):
                    ts(prob_of(ti), prob_of(ti), rg[:, ti:ti + 1], None, ALU.mult).then_inc(S("probs"), 1)
                tt(probc31, probc31, rg[:, 4:8].unsqueeze(2).broadcast_to([P, NT, NCMP]), ALU.mult).then_inc(S("probs"), 1)
                split(w[4])
                wait_alone(("scores_w", h + 1), ("turned_s", h + 1))
                logits(range(NT), 2)
                dve.wait_ge(S("logits"), h * 12 + 12)
                ts(nmx[:, 8:12], mx[:, 8:12], -1.0, None, ALU.mult).then_inc(S("neg_max"), 1)
                lbh, omlb = lb[:, 2, :], lb[:, 3, :]
                lbh, omlb = (lbh[:, 0:1], omlb[:, 0:1]) if first else (lbh[:, ds(h, 1)], omlb[:, ds(h, 1)])
                dve.wait_ge(*drained(w[2]))
                ts(sg, sg, omlb, lbh, ALU.mult, ALU.add).then_inc(S("f_step"), 1)
                dve.wait_ge(S("f_step"), h + 1)
                ts(sg, sg, LN_FLOOR, None, ALU.max).then_inc(S("f_ready"), 1)
                ts(kk, kk, omlb, None, ALU.mult).then_inc(S("k_ready"), 1)
                dve.tensor_copy(probT[:, T:2 * T], TB[1][:, :]).then_inc(S("probT_v"), 1)
                dve.tensor_copy(probT[:, 2 * T:2 * T + 256], TB[2][:, 0:256]).then_inc(S("probT_v"), 1)
                tt(probcT.rearrange("p (c t) -> p c t", c=NT), TB[2][:, 256:384].unsqueeze(1).broadcast_to([P, NT, P]),
                   par[:, C_TILE:C_TILE + NT].unsqueeze(2).broadcast_to([P, NT, P]), ALU.mult).then_inc(S("probT_v"), 1)
                normalise(((8, 2),), 12, 4)
                for ti in range(NT):
                    ts(prob_of(ti), prob_of(ti), rg[:, 8 + ti:9 + ti], None, ALU.mult).then_inc(S("probs"), 1)
                dve.wait_ge(S("logf"), h + 1)
                for c in range(NT):
                    at = gg[:, c * P:(c + 1) * P]
                    dve.tensor_tensor_scan(at, ones[:, :], at, 0.0, ALU.mult, ALU.add).then_inc(S("scan"), 1)
                split(w[5])
                dve.wait_ge(S("turned_w"), h + 1)
                dve.tensor_copy(probT[:, T:2 * T], TB[1][:, :]).then_inc(S("probT_v"), 1)
                dve.tensor_copy(probT[:, 2 * T:2 * T + 256], TB[2][:, 0:256]).then_inc(S("probT_v"), 1)
                if not first:
                    prev_ms(h)
                dve.wait_ge(S("scan"), h * 4 + 4)
                for e in range(3):
                    gap(e)
                dve.wait_ge(S("sg_hq"), h + 1)
                frees(tt(qq, G[w[3].slot][:, :], sg, ALU.mult), w[3])
                dve.wait_ge(S("k_ready"), h + 1)
                dve.wait_ge(*drained(w[3]))
                for e in range(3):
                    gate_level(e)
                if not first:
                    prev_y(h)
                split(w[6])
                dve.wait_ge(S("attn_done"), h + 1)
                tt(chunk(Y, h), O[:, :], nz_s, ALU.mult).then_inc(S("y_attn"), 1)
                g4 = gg.rearrange("p (c t) -> p c t", c=NT)
                tt(kpT.rearrange("p (c t) -> p c t", c=NT), g4[:, :, P - 1:P].broadcast_to([P, NT, P]), g4,
                   ALU.subtract).then_inc(S("gap_k"), 1)
                dve.wait_ge(S("level_done"), h * LEVELS + 4)
                for e in range(3, 7):
                    gap(e)
                dve.wait_ge(S("decay_q"), h + 1)
                dve.tensor_copy(eglast[:, :], qg.rearrange("p (c t) -> p c t", c=NT)[:, :, P - 1]).then_inc(S("eglast"), 1)
                dve.wait_ge(S("eglast"), h + 1)
                tt(qg, qg, qq, ALU.mult).then_inc(S("q_decayed"), 1)
                dve.wait_ge(S("decay_k"), h + 1)
                tt(kpT, kpT, kk, ALU.mult).then_inc(S("kpT_ready"), 1)
                for l in range(4):
                    take_level(l)
                for e in range(3, 7):
                    gate_level(e)
                for l in range(4, LEVELS):
                    take_level(l)

            head(0, first=True)
            with dve.Fori(1, HEADS) as h:
                head(h)

            split(Idx(W_OUT[0]))
            prev_hz(HEADS, Idx(W_PLE[0][0] - 1))
            for c in range(4):
                low(c, chunk(Y, c), "act_hi0", "act_split0")
            prev_state(HEADS)
            for c in range(4, 8):
                low(c, chunk(Y, c), "act_hi0", "act_split0")
            split(Idx(W_OUT[0] + 1))
            for c in range(8, KC - 1):
                low(c, chunk(Y, c), "act_hi0", "act_split0")

            def c_stats():
                dve.wait_ge(S("mean_done"), 1)
                ts(ln_v, X[0][:, :], 1.0 / D, None, ALU.mult).then_inc(S("mean_ready"), 1)
                dve.wait_ge(S("mean_ready"), 1)
                for j in range(KC):
                    tt(chunk(Y, j), chunk(Y, j), ln_v, ALU.subtract).then_inc(S("conv_centred"), 1)
                dve.wait_ge(S("ln_var"), KC)
                dve.wait_ge(S("conv_centred"), KC)
                ts(ln_v, X[2][:, :], 1.0 / D, EPS, ALU.mult, ALU.add).then_inc(S("ln_v"), 1)
                dve.wait_ge(S("conv_ln_guess"), 1)
                tt(ln_sum, ln_rst, ln_rst, ALU.mult).then_inc(S("newton"), 1)
                dve.wait_ge(S("newton"), 1)
                tt(ln_sum, ln_sum, ln_v, ALU.mult).then_inc(S("newton"), 1)
                dve.wait_ge(S("newton"), 2)
                ts(ln_sum, ln_sum, -0.5, 1.5, ALU.mult, ALU.add).then_inc(S("newton"), 1)
                dve.wait_ge(S("newton"), 3)
                tt(ln_rst, ln_rst, ln_sum, ALU.mult).then_inc(S("newton"), 1)
                dve.wait_ge(S("newton"), 4)

            def second_part(layer):
                w, g = W_OUT[layer], G_OUT[layer]

                def out_chunk(w, g, j):
                    dve.wait_ge(S("gemm_done"), w.n(1))
                    frees(stt(chunk(Y, j), chunk(Y, j), ALPHA, G[g.slot][:, :], op0=ALU.mult, op1=ALU.add), g)

                if layer == 0:
                    prev_ms(HEADS)
                    prev_y(HEADS)
                    low(KC - 1, chunk(Y, KC - 1), "act_hi0", "act_split0")
                dve.memset(ln_sum, 0.0).then_inc(S("sums_set"), 1)
                dve.wait_ge(*after("sums_set", layer, 1))
                for n in range(4):
                    dve.wait_ge(S(f"res_landed{layer}_{n}"), 16)
                with dve.Fori(0, KC // 4) as i:
                    for k in range(2):
                        split(Idx(w + 2 + k, 2, i))
                        out_chunk(Idx(w + k, 2, i), Idx(g + k, 2, i), i * 2 + k)
                        dve.wait_ge(*drained(Idx(g + k, 2, i)))
                        if k:
                            dve.wait_ge(*after("half_summed", layer, i * 2 + 1))
                        tt(ln_sum, ln_sum, chunk(Y, i * 2 + k), ALU.add).then_inc(S("half_summed"), 1)

                def centre(cs, slot, others):
                    for c in cs:
                        tt(chunk(Y, c), chunk(Y, c), ln_shift, ALU.subtract).then_inc(S("centred"), 1)
                    for n, c in enumerate(cs):
                        dve.wait_ge(*after("centred", layer, c + 1))
                        if others or n:
                            dve.wait_ge(*after("c_summed", layer, c))
                        tt(ln_sum, ln_sum, chunk(Y, c), ALU.add).then_inc(S("c_summed"), 1)
                    for n, c in enumerate(cs):
                        dve.wait_ge(*after("squared", layer, c + 1))
                        if others or n:
                            dve.wait_ge(*after("sq_summed", layer, c))
                        tt(ln_sqs, ln_sqs, ln_sq[(slot + n) % 2], ALU.add).then_inc(S("sq_summed"), 1)

                split(Idx(w + 10))
                out_chunk(Idx(w + 8), Idx(g + 8), 8)
                dve.wait_ge(*after("shift_done", layer, 1))
                ts(ln_shift, X[0][:, :], 2.0 / D, None, ALU.mult).then_inc(S("shift_ready"), 1)
                dve.memset(ln_sum, 0.0).then_inc(S("sums_set"), 1)
                dve.memset(ln_sqs, 0.0).then_inc(S("sums_set"), 1)
                dve.wait_ge(*after("shift_ready", layer, 1))
                dve.wait_ge(*after("sums_set", layer, 3))
                centre(range(3), 0, False)
                with dve.Fori(0, 3) as i:
                    for k in range(2):
                        split(Idx(w + 11 + k, 2, i))
                        out_chunk(Idx(w + 9 + k, 2, i), Idx(g + 9 + k, 2, i), i * 2 + (9 + k))
                        dve.wait_ge(*drained(Idx(g + 9 + k, 2, i)))
                        centre([i * 4 + (3 + 2 * k), i * 4 + (4 + 2 * k)], 1, True)
                out_chunk(Idx(w + 15), Idx(g + 15), KC - 1)
                dve.wait_ge(*drained(Idx(g + 15)))
                tt(chunk(Y, KC - 1), chunk(Y, KC - 1), ln_shift, ALU.subtract).then_inc(S("centred"), 1)
                mean, off, var, dev, rr = [stat[:, n * NT:(n + 1) * NT] for n in range(5)]

                def spread(dst, src):
                    return tt(dst.rearrange("p (c t) -> p c t", c=NT), ident.unsqueeze(1).broadcast_to([P, NT, P]),
                              src.unsqueeze(2).broadcast_to([P, NT, P]), ALU.mult)

                step = S("ln_step")
                dve.wait_ge(*after("mean_sum", layer, 1))
                ts(mean, X[0][:, 0:NT], 1.0 / D, None, ALU.mult).then_inc(step, 1)
                dve.wait_ge(*after("ln_step", layer, 1))
                stt(off, mean, -1.0, mean, op0=ALU.mult, op1=ALU.mult).then_inc(step, 1)
                dve.wait_ge(*after("ln_step", layer, 2))
                ts(off, off, EPS, None, ALU.add).then_inc(step, 1)
                dve.wait_ge(*after("ln_step", layer, 3))
                dve.wait_ge(*after("var_sum", layer, 1))
                stt(var, TB[0][:, 0:NT], 1.0 / D, off, op0=ALU.mult, op1=ALU.add).then_inc(S("var"), 1)
                dve.wait_ge(*after("centred", layer, KC))
                spread(diag_d, mean).then_inc(S("diag_d"), 1)
                split(Idx(w + 17))
                dve.wait_ge(*after("ln_guess", layer, 1))
                stt(rr, dev, -0.5, dev, op0=ALU.mult, op1=ALU.mult).then_inc(step, 1)
                dve.wait_ge(*after("ln_step", layer, 4))
                dve.wait_ge(*after("var", layer, 1))
                tt(rr, rr, var, ALU.mult).then_inc(step, 1)
                dve.wait_ge(*after("ln_step", layer, 5))
                stt(dev, rr, 1.5, dev, op0=ALU.add, op1=ALU.mult).then_inc(step, 1)
                dve.wait_ge(*after("ln_step", layer, 6))
                spread(diag_r, dev).then_inc(S("diag_r"), 1)

                def minus_mean(j):
                    tt(chunk(Y, j), chunk(Y, j), X[1][:, :], ALU.subtract).then_inc(S("less_mean"), 1)

                dve.wait_ge(*after("mean_spread", layer, 1))
                minus_mean(0)
                dve.wait_ge(*after("dev_spread", layer, 1))
                for j in range(KC):
                    if j + 1 < KC:
                        minus_mean(j + 1)
                    dve.wait_ge(*after("less_mean", layer, j + 1))
                    tt(chunk(Y, j), chunk(Y, j), X[2][:, :], ALU.mult).then_inc(S("normed"), 1)
                    if j == 4:
                        split(Idx(w + 18))

                def gate(g, j, n_gate):
                    dve.wait_ge(*drained(g))
                    tt(ln_sq[g.slot], ln_sq[g.slot], chunk(Z, j), ALU.mult).then_inc(S("ple_gated"), 1)
                    dve.wait_ge(S("ple_gated"), n_gate)
                    tt(chunk(Y, j), chunk(Y, j), ln_sq[g.slot], ALU.add).then_inc(S(f"x_out{layer}"), 1)

                w, g = W_GATE[layer], G_GATE[layer]
                with dve.Fori(0, KC // 2 - 1) as i:
                    for k in range(2):
                        split(Idx(w + 2 + k, 2, i))
                        gate(Idx(g + k, 2, i), i * 2 + k, i * 2 + (layer * KC + k + 1))
                if w + KC < W_TILES:
                    split(Idx(w + KC))
                gate(Idx(g + KC - 2), KC - 2, layer * KC + KC - 1)
                if layer == 0:
                    for j in range(3):
                        low(j, chunk(Y, j), "x2_hi", "x2_split")
                gate(Idx(g + KC - 1), KC - 1, layer * KC + KC)

            second_part(0)

            for j in range(3, KC):
                low(j, chunk(Y, j), "x2_hi", "x2_split")
                if j == 8:
                    split(Idx(W_CONV + 1))
            p_low(p_raw1, 2)
            for n in range(2):
                dve.memset(U[n][:, 0:CONV_K - 1], 0.0).then_inc(S("history_set"), 1)
            dve.wait_ge(S("history_set"), 2)
            dve.wait_ge(S("stored0"), 16 * KC)
            dve.wait_ge(S("x2_split"), KC)

            TAPS = (range(0, 11), range(11, 21), range(21, CONV_K))

            def taps(j, part, u):
                for n in TAPS[part]:
                    src = U[u][:, n:n + T]
                    cw = par[:, ds(j * CONV_K + (C_CW + n), 1)] if not isinstance(j, int) else pcol(C_CW + n, j * CONV_K)
                    acc = chunk(Y, j) if n % 2 == 0 else odd
                    if n == 0:
                        ts(acc, src, cw, pcol(C_CBIAS, j), ALU.mult, ALU.add).then_inc(S("tap"), 1)
                    elif n == 1:
                        ts(acc, src, cw, None, ALU.mult).then_inc(S("tap"), 1)
                    else:
                        dve.wait_ge(S("tap"), j * CONV_K + (n - 1))
                        stt(acc, src, cw, acc, op0=ALU.mult, op1=ALU.add).then_inc(S("tap"), 1)
                if part == 2:
                    dve.wait_ge(S("tap"), j * CONV_K + CONV_K)
                    tt(chunk(Y, j), chunk(Y, j), odd, ALU.add).then_inc(S("conv_done"), 1)
                    dve.wait_ge(S("conv_done"), j + 1)
                    if isinstance(j, int) and j == 0:
                        dve.tensor_copy(ln_sum, chunk(Y, j)).then_inc(S("summed"), 1)
                    else:
                        dve.wait_ge(S("summed"), j)
                        tt(ln_sum, ln_sum, chunk(Y, j), ALU.add).then_inc(S("summed"), 1)

            def glu(w, u):
                g = Idx(w.base - W_CONV + G_CONV, w.mul, w.var)
                dve.wait_ge(S("gemm_done"), w.n(1))
                dve.wait_ge(*drained(Idx(g.base - 1, g.mul, g.var)))
                frees(tt(U[u][:, CONV_K - 1:UW], G[g.slot][:, :], conv_sg, ALU.mult), g)
                dve.wait_ge(*drained(g))

            def conv_slots(i, w, first=False):
                for k in range(6):
                    if not (first and k == 0):
                        split(w.plus(k + 1))
                    if k == 2 or k == 5:
                        glu(w.plus(k - 1), k // 3)
                        taps(i * 2 + k // 3, 0, k // 3)
                    if k == 3 or k == 4:
                        taps(i * 2, k - 2, 0)
                    if k < 2 and not first:
                        taps(i * 2 - 1, k + 1, 1)

            conv_slots(0, Idx(W_CONV), first=True)
            with dve.Fori(1, KC // 2) as i:
                conv_slots(i, Idx(W_CONV, 6, i))
            split(Idx(W_OUT[1]))
            taps(KC - 1, 1, 1)
            taps(KC - 1, 2, 1)
            c_stats()
            for j in range(KC + 1):
                if j < KC:
                    stt(chunk(Y, j), chunk(Y, j), pcol(C_CG, j), ln_rst, op0=ALU.mult, op1=ALU.mult).then_inc(S("conv_normed"), 1)
                    dve.wait_ge(S("silu_c"), j + 1)
                    tt(chunk(Y, j), chunk(Y, j), chunk(Z, j), ALU.mult).then_inc(S("gated"), 1)
                if j:
                    low(j - 1, chunk(Y, j - 1), "act_hi1", "act_split1")
                if j == 8:
                    split(Idx(W_OUT[1] + 1))
            second_part(1)

    return nc


def chunks(a):
    return np.ascontiguousarray(a.reshape(-1, P, a.shape[-1]).transpose(1, 0, 2)).reshape(P, -1)


def tiles(w):
    n = w.shape[1] // P
    return w.reshape(KC, P, n, P).transpose(2, 1, 0, 3).reshape(n, P, D)


def kernel(x, p, ev_w_in, ev_cmp_pe_k, ev_cmp_w1_k, ev_cmp_w2_k, ev_cmp_pe_v, ev_cmp_w1_v, ev_cmp_w2_v, ev_hg_norm,
           hgrn_lb, ev_w_out, od_w_in, od_conv_w, od_conv_b, od_ln_g, od_ln_b, od_w_out, post_ln_g, post_ln_b, ple_w,
           ple_gate_w):
    from concourse import bacc
    from concourse.bass_utils import run_bass_kernel_spmd

    ev = np.asarray(ev_w_in)[0]
    at, parts = 0, {}
    for name, n in (("nq", 1024), ("kv", 1536), ("ng", 24), ("nz", 1024), ("hq", 1024), ("hf", 1024), ("hi", 1024), ("hz", 1024)):
        parts[name] = ev[:, at:at + n]
        at += n
    kv = tiles(parts["kv"])
    kv = kv[[0, 1, 2, 3, 4, 5, 8, 9, 6, 7, 10, 11]]
    ng = tiles(np.concatenate([parts["ng"], np.zeros((D, P - 24), np.float32)], axis=1))
    heads = np.stack([tiles(parts[n]) for n in ("nq", "nz", "hf", "hq", "hi", "hz")], axis=1).reshape(-1, P, D)

    def ple(layer):
        w = np.asarray(ple_w)[layer].reshape(PLE_K, P, 2, 8, P)
        return w.transpose(2, 1, 3, 0, 4).reshape(2, P, D)

    a, b, z = [tiles(w) for w in np.split(np.asarray(od_w_in)[0], 3, axis=1)]
    conv = np.stack([b, a, z], axis=1).reshape(-1, P, D)
    gate = np.asarray(ple_gate_w)
    out_w = [tiles(np.asarray(w)[0]) for w in (ev_w_out, od_w_out)]
    second = [np.concatenate([ple(n)[:1], out_w[n], ple(n)[1:], tiles(gate[n])]) for n in range(2)]
    wall = np.concatenate([kv, ng, heads, second[0], conv, second[1]])

    def vec(v):
        return np.asarray(v).reshape(-1, P).T

    cols, masks = constants()
    taps = np.asarray(od_conv_w)[0].reshape(CONV_K, KC, P).transpose(2, 1, 0).reshape(P, -1)
    par = np.concatenate([vec(post_ln_g), vec(post_ln_b), vec(od_ln_g), vec(od_ln_b), vec(od_conv_b), taps,
                          vec(ev_hg_norm), vec(hgrn_lb), np.asarray(ev_cmp_pe_k)[0].T, np.asarray(ev_cmp_pe_v)[0].T, cols], axis=1)

    def w1(w):
        return np.asarray(w)[0].reshape(CMP_LEN, P, P).transpose(1, 0, 2).reshape(P, -1)

    arrays = {
        "xT": chunks(np.asarray(x)[0].T),
        "wall": wall,
        "w1": np.stack([w1(ev_cmp_w1_k), w1(ev_cmp_w1_v)]),
        "w2": np.concatenate([np.asarray(ev_cmp_w2_k)[0], np.asarray(ev_cmp_w2_v)[0]], axis=1),
        "pT": np.stack([chunks(np.asarray(p)[n, 0].T) for n in range(2)]),
        "par": par,
        "masks": masks,
    }
    arrays = {n + "_in": np.ascontiguousarray(v) for n, v in arrays.items()}
    nc = bacc.Bacc("TRN2", target_bir_lowering=False, num_devices=1)
    args = [nc.dram_tensor(n, v.shape, mybir.dt.from_np(v.dtype), kind="ExternalInput").ap() for n, v in arrays.items()]
    out = nc.dram_tensor("out", (P, KC * T), mybir.dt.float32, kind="ExternalOutput").ap()
    build(nc, *args, out)
    r = run_bass_kernel_spmd(nc, [arrays], core_ids=[0])
    y = r.results[0]["out"]
    return np.ascontiguousarray(y.reshape(P, KC, T).transpose(2, 1, 0)).reshape(1, T, D)
```

```python
import numpy as np
from contextlib import ExitStack

import concourse.bass as bass
from concourse import mybir

P = 128
T = 512
D = 2048
KC = D // P
NT = T // P
HEADS = 8
GROUPS = 2
HPG = HEADS // GROUPS
CMP_LEN, CMP_STRIDE = 32, 16
NCMP = T // CMP_STRIDE - 1
CONV_K = 31
PLE_K = 2
ALPHA = (2.0 * 2) ** 0.25
EPS = 1e-5
C_FIRST = 6
WARM_UP = 14
LAG = 6
NEG = -1e30
LN_FLOOR = 2.0 ** -63

W_KV = 0
W_HEAD = 13
W_PLE = ((61, 78), (143, 160))
W_OUT = (62, 144)
W_GATE = (79, 161)
W_CONV = 95
W_TILES = 177
G_PLE = ((61, 85), (157, 181))
G_OUT = (69, 165)
G_GATE = (93, 189)
G_CONV = 109

HALVES = (64, 32, 16, 8, 4, 2, 1)
LEVELS = 8
HALF = P // 2

MASKS = P + len(HALVES) * HALF

C_LNG = 0
C_LNB = C_LNG + 32
C_CG = C_LNB + 32
C_CB = C_CG + KC
C_CBIAS = C_CB + KC
C_CW = C_CBIAS + KC
C_NORM = C_CW + KC * CONV_K
C_LBRAW = C_NORM + HEADS
C_PE = C_LBRAW + HEADS
C_SLOPE = C_PE + 2 * CMP_LEN
C_SEEN = C_SLOPE + HEADS
C_ID = C_SEEN + 1
C_DIST = C_ID + P
C_DISTC = C_DIST + T
C_TILE = C_DISTC + NT * NCMP
NPAR = C_TILE + NT


def constants():
    t = np.arange(P)[:, None]
    slope = np.broadcast_to(2.0 ** (-8.0 * np.arange(1, HEADS + 1) / HEADS), (P, HEADS))
    seen = (t >= CMP_LEN - 1).astype(np.float32)
    x = np.arange(T)[None, :] - (T - P) - t
    dist = np.where(x <= 0, x, NEG)
    end = np.arange(NCMP) * CMP_STRIDE + CMP_LEN - 1
    tt = np.arange(NT)[None, :, None] * P + t[:, :, None]
    distc = np.where(end <= tt, end - tt, NEG).reshape(P, -1)
    tile = np.arange(P)[:, None] // 32 == np.arange(NT)[None, :]
    cols = np.concatenate([slope, seen, np.eye(P), dist, distc, tile], axis=1).astype(np.float32)
    masks = np.zeros((P, MASKS), np.float32)
    masks[:, :P] = np.eye(P)
    s, u = np.arange(P)[:, None], np.arange(P)
    for e, half in enumerate(HALVES):
        second = u[u % (2 * half) >= half]
        masks[:, P + e * HALF:P + (e + 1) * HALF] = (s // (2 * half) == second // (2 * half)) & (s % (2 * half) < half)
    return cols, masks


LN_COUNTS = dict(
    half_summed=4, shift_done=1, shift_ready=1, sums_set=3, centred=16, c_summed=16, squared=16, sq_summed=16, mean_sum=1,
    var_sum=1, ln_step=6, var=1, ln_log=1, ln_guess=1, diag_d=1, diag_r=1, mean_spread=1, dev_spread=1, less_mean=16, normed=16)


class Idx:

    def __init__(self, base, mul=0, var=0):
        self.base, self.mul, self.var = base, mul, var

    def n(self, off=0):
        return self.var * self.mul + (self.base + off) if self.mul else self.base + off

    def half(self, off=0):
        return self.var * (self.mul // 2) + (self.base // 2 + off) if self.mul else self.base // 2 + off

    def plus(self, k):
        return Idx(self.base + k, self.mul, self.var)

    @property
    def slot(self):
        return self.base % 2


def wait(eng, sem, value):
    if not isinstance(value, int) or value > 0:
        eng.wait_ge(sem, value)


def build(nc, xT, wall, w1, w2, pT, par_in, masks_in, out):
    F = mybir.dt.float32
    R = mybir.dt.float32r
    U8 = mybir.dt.uint8
    ALU = mybir.AluOpType
    ACT = mybir.ActivationFunctionType
    ds = bass.ds
    x2_dram = nc.dram_tensor("x2_residual", [P, KC * T], F).ap()

    with ExitStack() as ctx:
        def sb(name, shape, dt=F):
            return ctx.enter_context(nc.sbuf_tensor(name, shape, dt))

        sems = {}

        def S(name):
            if name not in sems:
                sems[name] = ctx.enter_context(nc.semaphore(name))
            return sems[name]

        w_raw = sb("w_raw", [P, 2, D])
        w_hi = sb("w_hi", [P, 2, D], R)
        w_lo = sb("w_lo", [P, 2, D], R)
        a_hi = sb("a_hi", [P, KC, T], R)
        a_lo = sb("a_lo", [P, KC, T], R)
        Y = sb("Y", [P, KC * T])
        Z = sb("Z", [P, KC * T])
        tmp = sb("tmp", [P, 2688])
        par = sb("par", [P, NPAR])
        msk = sb("msk", [P, MASKS], U8)
        ones = sb("ones", [P, P])
        p_hi = sb("p_hi", [P, PLE_K, T], R)
        p_lo = sb("p_lo", [P, PLE_K, T], R)
        bias = sb("bias", [P, T + NT * NCMP])
        kcT = sb("kcT", [P, GROUPS * NCMP])
        vc4 = sb("vc4", [P, GROUPS, P])
        gates = sb("gates", [P, 3 * HEADS, NT])
        mx = sb("mx", [P, 12])
        nmx = sb("nmx", [P, 12])
        rsum = sb("rsum", [P, 12])
        rg = sb("rg", [P, 12])
        eglast = sb("eglast", [P, NT])
        stat = sb("stat", [P, 5 * NT])
        lb = sb("lb", [P, 4, HEADS])
        ident = par[:, C_ID:C_ID + P]

        def pcol(c, j):
            return par[:, ds(j + c, 1)] if not isinstance(j, int) else par[:, c + j:c + j + 1]

        def chunk(buf, j):
            return buf[:, ds(j * T, T)] if not isinstance(j, int) else buf[:, j * T:(j + 1) * T]

        ksT, kwT, vs, vw = [[Z[:, (2 * n + g) * T:(2 * n + g + 1) * T] for g in range(GROUPS)] for n in range(4)]
        ZU = 8 * T
        prob = Z[:, ZU:ZU + 1280]
        qT = Z[:, ZU + 1280:ZU + 1792]
        ring = [Z[:, ZU + T * r:ZU + T * (r + 1)] for r in range(3)]
        pair = Z[:, ZU + 3 * T:ZU + 3 * T + T // 2]
        kp = Z[:, ZU:ZU + T]
        probT = Z[:, ZU + 1792:ZU + 3072]
        viT = Z[:, ZU + 1792:ZU + 1792 + T]
        kpT = Z[:, ZU + 1792 + T:ZU + 1792 + 2 * T]
        gg = Z[:, ZU + 3072:ZU + 3584]
        vi = gg
        kk = Z[:, ZU + 3584:ZU + 4096]
        blk = [Z[:, ZU + n * 1984:ZU + (n + 1) * 1984].rearrange("p (l n) -> p l n", l=CMP_LEN) for n in range(2)]
        sg = tmp[:, 0:T]
        osb = tmp[:, T:2 * T]
        qg = tmp[:, 2 * T:3 * T]
        sq_h = rst_h = qg
        qq = tmp[:, 3 * T:4 * T]
        state = tmp[:, 3 * T:3 * T + 3 * P]
        probcT = tmp[:, 4 * T:5 * T]
        AT = tmp[:, 4 * T:5 * T]
        probc = tmp[:, 5 * T:5 * T + P]
        probc31 = probc.rearrange("p (t n) -> p t n", t=NT)[:, :, 0:NCMP]
        nz_s = Y[:, 7 * T:8 * T]
        hz_s = Y[:, 15 * T:16 * T]
        p_raw0 = vT2 = tmp[:, 0:2 * T]
        gT = tmp[0:3 * HEADS, 2 * T:3 * T]
        gel_k = tmp[:, 3 * T:3 * T + GROUPS * NCMP]
        gel_v = tmp[:, 3 * T + 64:3 * T + 64 + GROUPS * P]
        w2_sb = tmp[:, 3 * T + 320:3 * T + 320 + 2 * P]
        w1_sb = [Y[:, 4096 * n:4096 * (n + 1)] for n in range(2)]
        ln_sq = [tmp[:, 0:T], tmp[:, T:2 * T]]
        ln_shift = diag_d = tmp[:, 2 * T:3 * T]
        ln_sqs = tmp[:, 3 * T:4 * T]
        UW = T + CONV_K - 1
        ln_sum = diag_r = tmp[:, 2 * UW + 2 * T:2 * UW + 3 * T]
        U = [tmp[:, n * UW:(n + 1) * UW] for n in range(2)]
        conv_sg = tmp[:, 2 * UW:2 * UW + T]
        c_shift = c_diag_d = tmp[:, 2 * UW + T:2 * UW + 2 * T]
        c_sq = [Z[:, 12 * T:13 * T], Z[:, 13 * T:14 * T]]
        c_sqs = Z[:, 14 * T:15 * T]
        p_raw1 = Z[:, 14 * T:16 * T]

        POFF = (0, 128, 384, 768)
        TOFF = (0, 512, 1024, 896)

        def prob_of(ti):
            return prob[:, POFF[ti]:POFF[ti] + (ti + 1) * P]

        def pb(name):
            return ctx.enter_context(nc.psum_tensor(name, [P, T], F))

        G = [pb("G0"), pb("G1")]
        X = [pb("X0"), pb("X1"), pb("X2")]
        TB = [pb("T0"), pb("T1"), pb("T2")]
        O = X[0]
        LEVEL_AT = ((X[1], 0), (X[2], 0), (X[2], 256), (TB[2], 0), (X[0], 0), (X[0], 256), (X[1], 0), (X[1], 256))
        LEVEL_BANK_DONE = (1, 3, 3, 4, 6, 6, 8, 8)
        SCORES = ((3, X[0], 0), (2, X[1], 0), (0, X[1], 3 * P), (1, X[2], 0))

        def drained(g):
            return S(f"bank_free{g.slot}"), g.half(1)

        def frees(ins, g):
            ins.then_inc(S(f"bank_free{g.slot}"), 1)

        def landed(w):
            return S(f"w_landed{w.slot}"), w.half(1) * 16

        def after(name, n, steps):
            return S(name), steps + LN_COUNTS[name] * n

        def quarter(q):
            return slice(q * D // 4, (q + 1) * D // 4)

        def quarter_landed(n, q):
            return f"w_landed{n}" if q == 3 else f"w{n}_landed_{q}"

        def head_tile(h, k):
            return Idx(W_HEAD + 6 * h + k) if isinstance(h, int) else Idx(W_HEAD + k, 6, h)

        def before(w):
            return Idx(w.base - 6, w.mul, w.var)

        block = ctx.enter_context(nc.Block())

        @block.sync
        def _(sp):
            for q in range(4):
                at = slice(q * 4 * T, (q + 1) * 4 * T)
                sp.dma_start(w_raw[:, 0, quarter(q)], wall[0][:, quarter(q)]).then_inc(S(quarter_landed(0, q)), 16)
                sp.dma_start(Z[:, at], xT[:, at]).then_inc(S(f"x_landed{q}"), 16)
                sp.dma_start(w_raw[:, 1, quarter(q)], wall[1][:, quarter(q)]).then_inc(S(quarter_landed(1, q)), 16)
            sp.wait_ge(S("w_split"), 1)
            sp.dma_start(w_raw[:, 0, :], wall[2]).then_inc(S("w_landed0"), 16)
            with sp.Fori(0, (W_TILES - 3) // 2) as i:
                for k in range(2):
                    sp.wait_ge(S("w_split"), i * 2 + (k + 2))
                    sp.dma_start(w_raw[:, 1 - k, :], wall[ds(i * 2 + (k + 3), 1)].rearrange("a p n -> p (a n)")).then_inc(
                        S(f"w_landed{1 - k}"), 16)

        @block.gpsimd
        def _(pool):
            pool.wait_ge(S("w_landed1"), 16)
            pool.dma_start(par[:, :], par_in).then_inc(S("par_landed"), 16)
            pool.dma_start(p_raw0, pT[0]).then_inc(S("p0_landed"), 16)
            pool.dma_start(w1_sb[0], w1[0]).then_inc(S("w1k_landed"), 16)
            pool.dma_start(w1_sb[1], w1[1]).then_inc(S("w1v_landed"), 16)
            pool.dma_start(w2_sb, w2).then_inc(S("w2_landed"), 16)
            pool.wait_ge(S("p_split"), 1)
            pool.dma_start(p_raw0[:, 0:MASKS], masks_in).then_inc(S("msk_landed"), 16)

            def residual(layer):
                for n in range(4):
                    pool.wait_ge(S(f"act_split{layer}"), 4 * (n + 1))
                    src = (xT, x2_dram)[layer][:, n * 4 * T:(n + 1) * 4 * T]
                    pool.dma_start(Y[:, n * 4 * T:(n + 1) * 4 * T], src).then_inc(S(f"res_landed{layer}_{n}"), 16)

            def x1_low(layer):
                for j in range(KC):
                    pool.wait_ge(S(f"x1_hi{layer}"), j + 1)
                    pool.tensor_tensor(a_lo[:, j, :], chunk(Y, j), a_hi[:, j, :].bitcast(F), ALU.subtract).then_inc(
                        S(f"x1_split{layer}"), 1)

            def store(layer):
                dst = (x2_dram, out)[layer]
                with pool.Fori(0, KC) as j:
                    pool.wait_ge(S(f"x_out{layer}"), j + 1)
                    pool.dma_start(chunk(dst, j), chunk(Y, j)).then_inc(S(f"stored{layer}"), 16)

            residual(0)
            x1_low(0)
            store(0)
            pool.dma_start(p_raw1, pT[1]).then_inc(S("p1_landed"), 16)
            pool.wait_ge(S("stored0"), 16 * KC)

            def split(k, i=0):
                w = Idx(W_CONV + k, 0 if isinstance(i, int) else 10, i)
                pool.wait_ge(S("w_hi"), w.n(1))
                pool.wait_ge(S("w_split"), w.n())
                pool.tensor_tensor(w_lo[:, w.slot, :], w_raw[:, w.slot, :], w_hi[:, w.slot, :].bitcast(F),
                                   ALU.subtract).then_inc(S("w_split"), 1)

            def passed():
                pool.sem_inc(S("pool_passed"), 1)

            def sum_c(j):
                pool.wait_ge(S("conv_done"), j + 2)
                pool.wait_ge(S("first_summed"), j + 1)
                passed()
                pool.tensor_tensor(ln_sum, ln_sum, chunk(Y, j), ALU.add).then_inc(S("first_summed"), 1)

            def centre_c(c):
                pool.wait_ge(S("conv_done"), c + 2)
                passed()
                pool.tensor_tensor(chunk(Y, c), chunk(Y, c), c_shift, ALU.subtract).then_inc(S("centred"), 1)
                pool.wait_ge(*after("centred", 1, c + 1))
                pool.wait_ge(*after("c_summed", 1, c))
                passed()
                pool.tensor_tensor(ln_sum, ln_sum, chunk(Y, c), ALU.add).then_inc(S("c_summed"), 1)
                pool.wait_ge(*after("squared", 1, c + 1))
                pool.wait_ge(*after("sq_summed", 1, c))
                pool.tensor_tensor(c_sqs, c_sqs, c_sq[0], ALU.add).then_inc(S("sq_summed"), 1)

            pool.wait_ge(*after("sums_set", 1, 1))
            pool.sem_inc(S("first_summed"), 1)
            split(3)
            with pool.Fori(0, 2) as i:
                for n, k in enumerate(range(4, 14)):
                    split(k, i)
                    if k in (6, 8, 10):
                        sum_c(i * (C_FIRST // 2) + (k - 6) // 2)
            pool.wait_ge(S("p_split"), 2)
            pool.wait_ge(*after("shift_done", 1, 1))
            pool.memset(ln_sum, 0.0).then_inc(S("sums_set"), 1)
            pool.memset(c_sqs, 0.0).then_inc(S("sums_set"), 1)
            pool.wait_ge(*after("shift_ready", 1, 1))
            pool.wait_ge(*after("sums_set", 1, 3))
            with pool.Fori(2, 4) as i:
                for k in range(4, 14):
                    split(k, i)
                    if 5 <= k < 12:
                        centre_c(i * 7 + (k - 19))
            for k in range(44, 49):
                split(k)
            residual(1)
            x1_low(1)
            store(1)
            pool.wait_ge(S("stored1"), 16 * KC)

        @block.tensor
        def _(pe):
            def mm(o, l, r, start=True, stop=True):
                return pe.matmul(o, l, r, start=start, stop=stop)

            def gemm(w, g):
                pe.wait_ge(S("w_split"), w.n(1))
                wait(pe, S(f"bank_free{g.slot}"), g.half())
                o = G[g.slot][:, :]
                for k in range(KC):
                    hi, lo = w_hi[:, w.slot, k * P:(k + 1) * P], w_lo[:, w.slot, k * P:(k + 1) * P]
                    mm(o, hi, a_hi[:, k, :], k == 0, False)
                    mm(o, hi, a_lo[:, k, :], False, False)
                    last = mm(o, lo, a_hi[:, k, :], False, k == KC - 1)
                last.then_inc(S("gemm_done"), 1)

            def gemm_pair(w, g, acts, between=None, quarters=False):
                for k in range(KC + LAG):
                    for n, kn in ((0, k), (1, k - LAG)):
                        if not 0 <= kn < KC:
                            continue
                        wn, gn = Idx(w + n), Idx(g + n)
                        if quarters and kn % 4 == 0:
                            pe.wait_ge(*((S("quarter_split"), kn // 2 + n + 1) if kn < 12 else (S("w_split"), n + 1)))
                        elif kn == 0:
                            pe.wait_ge(S("w_split"), wn.n(1))
                            pe.wait_ge(S(f"bank_free{gn.slot}"), gn.half())
                        if n == 0:
                            pe.wait_ge(S(acts), k + 1)
                        o, at = G[gn.slot][:, :], slice(kn * P, (kn + 1) * P)
                        hi, lo = w_hi[:, wn.slot, at], w_lo[:, wn.slot, at]
                        mm(o, hi, a_hi[:, kn, :], kn == 0, False)
                        mm(o, hi, a_lo[:, kn, :], False, False)
                        last = mm(o, lo, a_hi[:, kn, :], False, kn == KC - 1)
                        if kn == KC - 1:
                            last.then_inc(S("gemm_done"), 1)
                    if between and k in between:
                        between[k]()

            def gemms(w, g, n):
                with pe.Fori(0, n // 2) as i:
                    for k in range(2):
                        gemm(Idx(w + k, 2, i), Idx(g + k, 2, i))

            def ple_pack(layer, u, cs=range(8)):
                w = Idx(W_PLE[layer][u])
                for c in cs:
                    if c == 0:
                        pe.wait_ge(S("w_split"), w.n(1))
                        pe.wait_ge(S("p_split"), layer + 1)
                    g = Idx(G_PLE[layer][u] + c)
                    pe.wait_ge(S(f"bank_free{g.slot}"), g.half())
                    o = G[g.slot][:, :]
                    for k in range(PLE_K):
                        at = (c * PLE_K + k) * P
                        hi, lo = w_hi[:, w.slot, at:at + P], w_lo[:, w.slot, at:at + P]
                        mm(o, hi, p_hi[:, k, :], k == 0, False)
                        mm(o, hi, p_lo[:, k, :], False, False)
                        last = mm(o, lo, p_hi[:, k, :], False, k == PLE_K - 1)
                    last.then_inc(S("gemm_done" if c == 7 else "ple_done"), 1)

            pe.wait_ge(S("ones_set"), 1)
            for _ in range(WARM_UP):
                mm(X[0][:, 0:P], ones[:, :], ones[:, :])
            gemm_pair(0, 0, "x_split", quarters=True)
            gemms(2, 2, 4)
            for n in range(2):
                pe.wait_ge(S("w1k_landed" if n == 0 else "w1v_landed"), 16)
                pe.wait_ge(*drained(Idx(2 * n + 1)))
                for l in range(CMP_LEN):
                    last = mm(X[n][:, 0:GROUPS * NCMP], w1_sb[n][:, l * P:(l + 1) * P], blk[n][:, l, :],
                              l == 0, l == CMP_LEN - 1)
                last.then_inc(S("cmp_hidden"), 1)
            gemm(Idx(6), Idx(6))
            pe.wait_ge(S("w2_landed"), 16)
            pe.wait_ge(S("gelu_done"), 3)
            mm(X[2][:, 0:GROUPS * NCMP], w2_sb[:, 0:P], gel_k)
            for g in range(GROUPS):
                last = mm(TB[2][:, g * P:(g + 1) * P], gel_v[:, g * P:(g + 1) * P], w2_sb[:, P:2 * P])
            last.then_inc(S("cmp_done"), 1)
            gemm(Idx(7), Idx(7))
            gemm(Idx(8), Idx(8))
            for n in range(4):
                gemm(Idx(9 + n), Idx(9 + n))
                pe.wait_ge(*drained(Idx(8 + n)))
                wait(pe, S("v_ready"), n - 1)
                for m in range(NT):
                    at = slice(m * P, (m + 1) * P)
                    last = pe.transpose(TB[n % 2][:, at], vT2[:, (n % 2) * T + m * P:(n % 2) * T + (m + 1) * P], ident)
                last.then_inc(S("v_turned"), 1)

            def scores(g, keys, cmp_too, sem):
                for ti, bank, at in SCORES:
                    n = (ti + 1) * P
                    last = mm(bank[:, at:at + n], qT[:, ti * P:(ti + 1) * P], keys[g][:, 0:n])
                if cmp_too:
                    for ti in range(NT):
                        last = mm(X[2][:, 256 + 32 * ti:256 + 32 * ti + NCMP], qT[:, ti * P:(ti + 1) * P],
                                  kcT[:, g * NCMP:(g + 1) * NCMP])
                last.then_inc(S(sem), 1)

            def turn_probs(cmp_too, sem):
                if cmp_too:
                    pe.transpose(TB[2][:, 256:384], probc, ident)
                for ti in range(NT):
                    for mj in range(ti + 1):
                        at = TOFF[mj] + (ti - mj) * P
                        last = pe.transpose(TB[at // T][:, at % T:at % T + P], prob_of(ti)[:, mj * P:(mj + 1) * P], ident)
                last.then_inc(S(sem), 1)

            def values(v, g, start, stop):
                for mj in range(NT):
                    n = T - mj * P
                    last = mm(O[:, mj * P:T], v[g][:, mj * P:(mj + 1) * P], probT[:, TOFF[mj]:TOFF[mj] + n],
                              start and mj == 0, stop and mj == NT - 1)
                return last

            def level(h, l):
                bank, at = LEVEL_AT[l]
                for c in range(NT):
                    cs = slice(c * P, (c + 1) * P)
                    if l == 0:
                        last = mm(bank[:, cs], kk[:, cs], qq[:, cs])
                        continue
                    e = l - 1
                    half = HALVES[e]
                    if c == 0:
                        pe.wait_ge(S("level_ready"), h * 7 + l)
                    if half > 1:
                        keys = ring[e % 3][:, cs]
                        queries = keys.rearrange("p (b n) -> p b n", n=2 * half)[:, :, half:2 * half]
                    else:
                        keys, queries = kk[:, cs], pair[:, c * HALF:(c + 1) * HALF]
                    last = mm(bank[:, at + c * HALF:at + (c + 1) * HALF], keys, queries)
                last.then_inc(S("level_done"), 1)

            def state_sums(h):
                pe.wait_ge(S("kp_ready"), h)
                pe.wait_ge(S("vi_ready"), h)
                for c in range(NT - 1):
                    at = slice(c * P, (c + 1) * P)
                    last = mm(TB[2][:, at], kp[:, at], vi[:, at])
                last.then_inc(S("sums_done"), 1)

            def hgrn_out(h):
                pe.wait_ge(S("level_copied"), h * LEVELS)
                pe.wait_ge(S("state_ready"), h)
                for c in range(NT):
                    at = slice(c * P, (c + 1) * P)
                    last = mm(TB[0][:, at], vi[:, at], AT[:, at], True, c == 0)
                    if c:
                        last = mm(TB[0][:, at], state[:, (c - 1) * P:c * P], qg[:, at], False, True)
                last.then_inc(S("o_done"), 1)

            def head(h, g, first=False):
                w = [head_tile(h, k) for k in range(6)]
                gemm(w[0], w[0])
                if first:
                    pe.wait_ge(*drained(Idx(12)))
                    for m in range(NT):
                        last = pe.transpose(TB[2][:, 256 + 24 * m:280 + 24 * m], gT[:, m * P:(m + 1) * P],
                                            par[0:24, C_ID:C_ID + 24])
                    last.then_inc(S("gates_turned"), 1)
                else:
                    state_sums(h)
                gemm(w[1], w[1])
                if first:
                    pe.wait_ge(S("v_ready"), 4)
                    pe.wait_ge(S("cmp_ready"), 2)
                else:
                    hgrn_out(h)
                pe.wait_ge(*drained(w[0]))
                scores(g, ksT, True, "scores_s")
                gemm(w[2], w[2])
                pe.wait_ge(S("logits"), h * 12 + 8)
                scores(g, kwT, False, "scores_w")
                pe.wait_ge(S("probs"), h * 9 + 5)
                if not first:
                    pe.wait_ge(S("o_copied"), h)
                turn_probs(True, "turned_s")
                gemm(w[3], w[3])
                pe.wait_ge(S("probT_a"), h * 2 + 1)
                pe.wait_ge(S("probT_v"), h * 5 + 3)
                pe.wait_ge(S("probs"), h * 9 + 9)
                values(vs, g, True, False)
                mm(O[:, :], vc4[:, g, :], probcT, False, False)
                turn_probs(False, "turned_w")
                if not first:
                    pe.wait_ge(S("sq_ready"), h)
                    mm(X[1][:, :], ones[:, :], sq_h).then_inc(S("ms_done"), 1)
                gemm(w[4], w[4])
                pe.wait_ge(S("probT_a"), h * 2 + 2)
                pe.wait_ge(S("probT_v"), h * 5 + 5)
                values(vw, g, False, True).then_inc(S("attn_done"), 1)
                if not first:
                    pe.wait_ge(S("ms_ready"), h)
                pe.wait_ge(S("k_ready"), h + 1)
                pe.wait_ge(*drained(w[3]))
                for l in range(4):
                    level(h, l)
                gemm(w[5], w[5])
                pe.wait_ge(*drained(w[4]))
                for c in range(NT):
                    at = slice(c * P, (c + 1) * P)
                    last = pe.transpose(TB[0][:, at], viT[:, at], ident)
                last.then_inc(S("vi_turned"), 1)
                pe.wait_ge(S("kpT_ready"), h + 1)
                for c in range(NT):
                    at = slice(c * P, (c + 1) * P)
                    last = pe.transpose(TB[1][:, at], kpT[:, at], ident)
                last.then_inc(S("kp_turned"), 1)
                pe.wait_ge(S("y_attn"), h + 1)
                pe.wait_ge(S("level_copied"), h * LEVELS + 1)
                for l in range(4, LEVELS):
                    level(h, l)

            pe.wait_ge(S("par_landed"), 16)
            head(0, 0, first=True)
            with pe.Fori(1, HPG) as h:
                head(h, 0)
            with pe.Fori(HPG, HEADS) as h:
                head(h, 1)
            ple_pack(0, 0, range(0, 4))
            state_sums(HEADS)
            ple_pack(0, 0, range(4, 8))
            hgrn_out(HEADS)

            def last_square():
                pe.wait_ge(S("sq_ready"), HEADS)
                mm(X[1][:, :], ones[:, :], sq_h).then_inc(S("ms_done"), 1)

            def to_tokens(bank, src):
                for m in range(NT):
                    last = mm(bank[:, m:m + 1], src[:, m * P:(m + 1) * P], ones[:, 0:1])
                return last

            def shift(sem, n):
                pe.wait_ge(sem, n)
                mm(X[0][:, :], ones[:, :], ln_sum).then_inc(S("shift_done"), 1)

            def token_mean(n):
                pe.wait_ge(*after("shift_ready", n, 1))
                pe.wait_ge(*after("c_summed", n, KC))
                to_tokens(X[0], ln_sum).then_inc(S("mean_sum"), 1)

            def token_var(n, sqs):
                pe.wait_ge(*after("sq_summed", n, KC))
                to_tokens(TB[2], sqs).then_inc(S("var_sum"), 1)

            def spread_mean(n, diag):
                pe.wait_ge(*after("diag_d", n, 1))
                mm(X[1][:, :], ones[:, :], diag).then_inc(S("mean_spread"), 1)

            def spread_dev(n):
                pe.wait_ge(*after("diag_r", n, 1))
                mm(X[2][:, :], ones[:, :], diag_r).then_inc(S("dev_spread"), 1)

            def second_part(layer, between=None):
                w, g = W_OUT[layer], G_OUT[layer]
                gemm_pair(w, g, f"act_split{layer}", between)
                gemms(w + 2, g + 2, 6)
                gemm(Idx(w + 8), Idx(g + 8))
                shift(*after("half_summed", 2 * layer, KC // 2))
                gemms(w + 9, g + 9, 6)
                gemm(Idx(w + 15), Idx(g + 15))
                n = 2 * layer
                ple_pack(layer, 1, range(0, 2))
                token_mean(n)
                token_var(n, ln_sqs)
                ple_pack(layer, 1, range(2, 4))
                spread_mean(n, diag_d)
                ple_pack(layer, 1, range(4, 5))
                spread_dev(n)
                ple_pack(layer, 1, range(5, 8))
                w, g = W_GATE[layer], G_GATE[layer]
                gemm_pair(w, g, f"x1_split{layer}")
                gemms(w + 2, g + 2, KC - 2)

            second_part(0, {2: last_square})
            gemm_pair(W_CONV, G_CONV, "x2_split")
            gemms(W_CONV + 2, G_CONV + 2, 18)
            shift(S("first_summed"), C_FIRST + 1)
            gemms(W_CONV + 20, G_CONV + 20, 22)
            token_mean(1)
            token_var(1, c_sqs)
            spread_mean(1, c_diag_d)
            gemm(Idx(W_CONV + 42), Idx(G_CONV + 42))
            spread_dev(1)
            gemms(W_CONV + 43, G_CONV + 43, 4)
            gemm(Idx(W_CONV + 47), Idx(G_CONV + 47))
            ple_pack(1, 0)
            second_part(1)


        @block.scalar
        def _(act):
            f = act.activation

            def split(w):
                act.wait_ge(*landed(w))
                if w.mul or w.base >= 2:
                    act.wait_ge(S("gemm_done"), w.n(-1))
                f(w_hi[:, w.slot, :], w_raw[:, w.slot, :], ACT.Copy).then_inc(S("w_hi"), 1)

            def high(j, sem):
                f(a_hi[:, j, :], chunk(Y, j), ACT.Copy).then_inc(S(sem), 1)

            def split_quarter(n, q):
                act.wait_ge(S(quarter_landed(n, q)), 16)
                f(w_hi[:, n, quarter(q)], w_raw[:, n, quarter(q)], ACT.Copy).then_inc(S("w_hi" if q == 3 else "quarter_hi"), 1)

            for q in range(4):
                split_quarter(0, q)
                act.wait_ge(S(f"x_landed{q}"), 16)
                for k in range(4 * q, 4 * q + 4):
                    f(a_hi[:, k, :], chunk(Z, k), ACT.Copy).then_inc(S("x_hi"), 1)
                split_quarter(1, q)
            for i in range(1, 13):
                split(Idx(i + 1))
                t = Idx(i - 1)
                if i == 2:
                    act.wait_ge(S("p0_landed"), 16)
                    f(p_hi[:, :, :].rearrange("p k t -> p (k t)"), p_raw0, ACT.Copy).then_inc(S("p_hi"), 1)
                if i == 3:
                    act.wait_ge(S("lb_step"), 1)
                    f(lb[:, 0, :], lb[:, 0, :], ACT.Exp).then_inc(S("lb_exp"), 1)
                act.wait_ge(S("gemm_done"), i)
                if 4 <= t.base < 8:
                    frees(f((ksT + kwT)[t.base - 4], G[t.slot][:, :], ACT.Copy), t)
                if 8 <= t.base < 12:
                    n = t.base - 8
                    wait(act, S("v_turned"), n - 1)
                    if n == 0:
                        act.wait_ge(S("masks_ready"), 1)
                    frees(f(vT2[:, (n % 2) * T:(n % 2 + 1) * T], G[t.slot][:, :], ACT.Copy), t)
                if i == 6:
                    act.wait_ge(S("cmp_hidden"), 2)
                    f(gel_k, X[0][:, 0:GROUPS * NCMP], ACT.Gelu_apprx_tanh).then_inc(S("gelu_done"), 1)
                    act.wait_ge(S("pads_set"), 2)
                    src = X[1][:, 0:GROUPS * NCMP].rearrange("p (g n) -> p g n", g=GROUPS)
                    for g in range(GROUPS):
                        dst = gel_v[:, g * P:(g + 1) * P].rearrange("p (t n) -> p t n", t=NT)[:, :, 0:NCMP]
                        f(dst, src[:, g:g + 1, :].broadcast_to([P, NT, NCMP]), ACT.Gelu_apprx_tanh).then_inc(S("gelu_done"), 1)

            def prev_hz(h, hz):
                act.wait_ge(S("gemm_done"), hz.n(1))
                f(sg, G[hz.slot][:, :], ACT.Sigmoid).then_inc(S("sg_hz"), 1)
                act.wait_ge(S("vi_turned"), h)
                act.wait_ge(S("decay_q"), h)
                f(vi, TB[0][:, :], ACT.Copy).then_inc(S("vi_ready"), 1)

            def prev_square(h):
                act.wait_ge(S("o_done"), h)
                f(sq_h, TB[0][:, :], ACT.Square).then_inc(S("sq_ready"), 1)
                f(osb, TB[0][:, :], ACT.Copy).then_inc(S("o_copied"), 1)

            def prev_rms(h):
                act.wait_ge(S("ms_ready"), h)
                f(rst_h, rst_h, ACT.Ln).then_inc(S("rms_log"), 1)
                act.wait_ge(S("rms_log"), h)
                f(rst_h, rst_h, ACT.Exp, scale=-0.5).then_inc(S("rms_inv"), 1)

            def head(h, first=False):
                w = [head_tile(h, k) for k in range(7)]

                def exps(tiles, o):
                    for ti in tiles:
                        f(prob_of(ti), prob_of(ti), ACT.Exp, bias=nmx[:, o + ti:o + ti + 1],
                          accum_out=rsum[:, o + ti:o + ti + 1]).then_inc(S("exps"), 1)

                def decay(e):
                    act.wait_ge(S("gap"), h * 13 + min(2 * e + 2, 13))
                    buf = ring[e % 3] if e < 6 else pair
                    f(buf, buf, ACT.Exp).then_inc(S("decay"), 1)

                split(w[1])
                if first:
                    act.wait_ge(S("gemm_done"), W_HEAD)
                    frees(f(gT, G[0][0:3 * HEADS, :], ACT.Sigmoid), Idx(12))
                else:
                    prev_hz(h, before(w[5]))
                split(w[2])
                act.wait_ge(S("gemm_done"), w[0].n(1))
                if not first:
                    act.wait_ge(S("level_done"), h * LEVELS)
                frees(f(qT, G[w[0].slot][:, :], ACT.Copy, scale=P ** -0.5), w[0])
                split(w[3])
                act.wait_ge(S("gemm_done"), w[1].n(1))
                if first:
                    act.wait_ge(S("v_turned"), 4)
                else:
                    act.wait_ge(*drained(before(w[5])))
                f(sg, G[w[1].slot][:, :], ACT.Sigmoid).then_inc(S("sg_nz"), 1)
                if not first:
                    prev_square(h)
                act.wait_ge(S("neg_max"), h * 2 + 1)
                exps(range(NT), 0)
                for ti in range(NT):
                    f(probc31[:, ti, :], probc31[:, ti, :], ACT.Exp, bias=nmx[:, 4 + ti:5 + ti],
                      accum_out=rsum[:, 4 + ti:5 + ti]).then_inc(S("exps"), 1)
                split(w[4])
                act.wait_ge(S("gemm_done"), w[2].n(1))
                act.wait_ge(*drained(w[1]))
                f(kk, G[w[2].slot][:, :], ACT.Sigmoid, scale=-1.0).then_inc(S("sg_not"), 1)
                frees(f(sg, G[w[2].slot][:, :], ACT.Sigmoid), w[2])
                act.wait_ge(S("turned_s"), h + 1)
                f(probT[:, 0:T], TB[0][:, :], ACT.Copy).then_inc(S("probT_a"), 1)
                act.wait_ge(S("neg_max"), h * 2 + 2)
                exps(range(NT), 8)
                act.wait_ge(S("f_ready"), h + 1)
                f(gg, sg, ACT.Ln).then_inc(S("logf"), 1)
                split(w[5])
                act.wait_ge(S("turned_w"), h + 1)
                f(probT[:, 0:T], TB[0][:, :], ACT.Copy).then_inc(S("probT_a"), 1)
                act.wait_ge(S("gemm_done"), w[3].n(1))
                act.wait_ge(S("logf"), h + 1)
                f(sg, G[w[3].slot][:, :], ACT.Sigmoid).then_inc(S("sg_hq"), 1)
                for e in range(3):
                    decay(e)
                if not first:
                    prev_rms(h)
                split(w[6])
                act.wait_ge(S("gemm_done"), w[4].n(1))
                act.wait_ge(S("attn_done"), h + 1)
                frees(f(viT, G[w[4].slot][:, :], ACT.Copy), w[4])
                if not first:
                    act.wait_ge(S("y_hgrn"), h)
                f(qg, gg, ACT.Exp).then_inc(S("decay_q"), 1)
                act.wait_ge(S("gap_k"), h + 1)
                f(kpT, kpT, ACT.Exp).then_inc(S("decay_k"), 1)
                for e in range(3, 7):
                    decay(e)

            head(0, first=True)
            with act.Fori(1, HEADS) as h:
                head(h)

            def ple_out(layer, u, c):
                g = Idx(G_PLE[layer][u] + c)
                if c == 7:
                    act.wait_ge(S("gemm_done"), W_PLE[layer][u] + 1)
                else:
                    act.wait_ge(S("ple_done"), 14 * layer + 7 * u + c + 1)
                frees(f(chunk(Z, 8 * u + c), G[g.slot][:, :], ACT.Copy), g)

            prev_hz(HEADS, Idx(W_PLE[0][0] - 1))
            split(Idx(W_OUT[0]))
            for c in range(8):
                ple_out(0, 0, c)
                high(c, "act_hi0")
            split(Idx(W_OUT[0] + 1))
            prev_square(HEADS)
            for c in range(8, KC - 1):
                high(c, "act_hi0")

            def square(n, c, dst, used):
                act.wait_ge(*after("centred", n, c + 1))
                if used is not None:
                    act.wait_ge(*after("sq_summed", n, used))
                f(dst, chunk(Y, c), ACT.Square).then_inc(S("squared"), 1)

            def deviation(n):
                var, dev = stat[:, 2 * NT:3 * NT], stat[:, 3 * NT:4 * NT]
                act.wait_ge(*after("var", n, 1))
                f(dev, var, ACT.Ln).then_inc(S("ln_log"), 1)
                act.wait_ge(*after("ln_log", n, 1))
                f(dev, dev, ACT.Exp, scale=-0.5).then_inc(S("ln_guess"), 1)

            def second_part(layer):
                w, g = W_OUT[layer], G_OUT[layer]
                if layer == 0:
                    prev_rms(HEADS)
                    act.wait_ge(S("y_hgrn"), HEADS)
                    high(KC - 1, "act_hi0")

                n_ln = 2 * layer
                with act.Fori(0, KC // 4) as i:
                    for k in range(2):
                        split(Idx(w + 2 + k, 2, i))
                split(Idx(w + 10))
                for c in range(3):
                    square(n_ln, c, ln_sq[c % 2], 1 if c == 2 else None)
                with act.Fori(0, 3) as i:
                    for k in range(2):
                        split(Idx(w + 11 + k, 2, i))
                        for n in range(2):
                            c = 3 + 2 * k + n
                            square(n_ln, i * 4 + c, ln_sq[c % 2], i * 4 + (c - 1))
                split(Idx(w + 17))
                square(n_ln, KC - 1, ln_sq[1], KC - 2)
                ple_out(layer, 1, 0)
                ple_out(layer, 1, 1)
                deviation(n_ln)

                def x1_high(j):
                    act.wait_ge(S("x1_ready"), layer * KC + j + 1)
                    high(j, f"x1_hi{layer}")

                for c in range(2, 5):
                    ple_out(layer, 1, c)
                for j in range(KC):
                    act.wait_ge(*after("normed", n_ln, j + 1))
                    f(chunk(Y, j), chunk(Y, j), ACT.Identity, scale=pcol(C_LNG + KC * layer, j),
                      bias=pcol(C_LNB + KC * layer, j)).then_inc(S("x1_ready"), 1)
                    if j >= 4:
                        x1_high(j - 1)
                    elif j < 3:
                        x1_high(j)
                        ple_out(layer, 1, j + 5)
                    if j == 6:
                        split(Idx(w + 18))
                x1_high(KC - 1)

                def gate(w, g, n_out):
                    act.wait_ge(S("gemm_done"), w.n(1))
                    wait(act, S(f"x_out{layer}"), n_out)
                    frees(f(ln_sq[g.slot], G[g.slot][:, :], ACT.Sigmoid), g)

                w, g = W_GATE[layer], G_GATE[layer]
                for j in range(2):
                    split(Idx(w + j + 2))
                    gate(Idx(w + j), Idx(g + j), 0)
                with act.Fori(1, KC // 2 - 1) as i:
                    for k in range(2):
                        split(Idx(w + 2 + k, 2, i))
                        gate(Idx(w + k, 2, i), Idx(g + k, 2, i), i * 2 + (k - 1))
                gate_end = W_GATE[layer] + KC
                if gate_end < W_TILES:
                    split(Idx(gate_end))
                gate(Idx(gate_end - 2), Idx(g + KC - 2), KC - 3)
                if layer == 0:
                    act.wait_ge(S("gemm_done"), W_CONV)
                    for j in range(3):
                        act.wait_ge(S("x_out0"), j + 1)
                        high(j, "x2_hi")
                gate(Idx(gate_end - 1), Idx(g + KC - 1), KC - 2)

            second_part(0)

            for j in range(3, KC):
                act.wait_ge(S("x_out0"), j + 1)
                high(j, "x2_hi")
                if j == 8:
                    split(Idx(W_CONV + 1))
            act.wait_ge(S("p1_landed"), 16)
            f(p_hi[:, :, :].rearrange("p k t -> p (k t)"), p_raw1, ACT.Copy).then_inc(S("p_hi"), 1)

            def c_tile(k, i=0):
                mul = 0 if isinstance(i, int) else 10
                return Idx(W_CONV + k, mul, i), Idx(G_CONV + k, mul, i)

            def silu_z(k, j, i=0):
                w, g = c_tile(k, i)
                act.wait_ge(S("gemm_done"), w.n(1))
                frees(f(chunk(Z, j), G[g.slot][:, :], ACT.Silu), g)

            def gate_b(k, a, i):
                w, g = c_tile(k, i)
                act.wait_ge(S("gemm_done"), w.n(1))
                act.wait_ge(*drained(c_tile(a, i)[1]))
                frees(f(conv_sg, G[g.slot][:, :], ACT.Sigmoid), g)

            def conv_slots(i, squares):
                for k in range(10):
                    split(c_tile(k + 2, i)[0])
                    if k in (0, 2, 5, 7):
                        gate_b(k, k - (2 if k in (0, 5) else 1), i)
                    if k in (4, 9):
                        silu_z(k, i * 2 + k // 5, i)
                    if squares and k >= 3:
                        square(1, i * 7 + (k - 17), c_sq[0], i * 7 + (k - 17))

            with act.Fori(0, 2) as i:
                conv_slots(i, False)
            act.wait_ge(*after("shift_done", 1, 1))
            f(c_shift, X[0][:, :], ACT.Copy, scale=1.0 / (C_FIRST * P)).then_inc(S("shift_ready"), 1)
            act.wait_ge(S("p_split"), 2)
            with act.Fori(2, 4) as i:
                conv_slots(i, True)
            split(Idx(W_CONV + 42))
            silu_z(40, 8)
            square(1, KC - 2, c_sq[0], KC - 2)
            square(1, KC - 1, c_sq[1], None)
            deviation(1)
            split(Idx(W_CONV + 43))
            silu_z(41, 9)
            for q in range(4):
                split(Idx(W_CONV + 44 + q))
                if q == 2:
                    act.wait_ge(*after("var_sum", 1, 1))
                silu_z(42 + q, 10 + q)
                for j in range(4 * q, 4 * q + 4):
                    act.wait_ge(*after("normed", 1, j + 1))
                    f(chunk(Y, j), chunk(Y, j), ACT.Silu, scale=pcol(C_CG, j), bias=pcol(C_CB, j)).then_inc(S("silu_c"), 1)
            split(Idx(W_CONV + 48))
            silu_z(46, 14)
            split(Idx(W_OUT[1]))
            silu_z(47, 15)
            for c in range(KC):
                if c < 8:
                    act.wait_ge(S("gated"), c + 1)
                    ple_out(1, 0, c)
                if c == 8:
                    split(Idx(W_OUT[1] + 1))
                act.wait_ge(S("gated"), c + 1)
                high(c, "act_hi1")
            second_part(1)

        @block.vector
        def _(dve):
            tt, ts, stt = dve.tensor_tensor, dve.tensor_scalar, dve.scalar_tensor_tensor

            def split(w):
                dve.wait_ge(S("w_hi"), w.n(1))
                tt(w_lo[:, w.slot, :], w_raw[:, w.slot, :], w_hi[:, w.slot, :].bitcast(F), ALU.subtract).then_inc(S("w_split"), 1)

            def low(j, src, hi_sem, sem, n=None):
                dve.wait_ge(S(hi_sem), j + 1)
                tt(a_lo[:, j, :], src, a_hi[:, j, :].bitcast(F), ALU.subtract).then_inc(S(sem), 1)

            def p_low(raw, n):
                dve.wait_ge(S("p_hi"), n)
                tt(p_lo[:, :, :].rearrange("p k t -> p (k t)"), raw,
                   p_hi[:, :, :].rearrange("p k t -> p (k t)").bitcast(F), ALU.subtract).then_inc(S("p_split"), 1)

            def wait_alone(*waits):
                for sem, value in waits:
                    dve.wait_ge(S(sem), value)
                if not isinstance(value, int):
                    dve.sem_inc(S("passed"), 1)

            def value_tile(n):
                dve.wait_ge(S("v_turned"), n + 1)
                dve.tensor_copy((vs + vw)[n], TB[n % 2][:, :]).then_inc(S("v_ready"), 1)

            dve.memset(ones[:, :], 1.0).then_inc(S("ones_set"), 1)
            dve.memset(gel_v, 0.0).then_inc(S("pads_set"), 1)
            dve.memset(probc, 0.0).then_inc(S("pads_set"), 1)
            def split_quarter(n, q):
                dve.wait_ge(*((S("w_hi"), n + 1) if q == 3 else (S("quarter_hi"), 2 * q + n + 1)))
                tt(w_lo[:, n, quarter(q)], w_raw[:, n, quarter(q)], w_hi[:, n, quarter(q)].bitcast(F), ALU.subtract).then_inc(
                    S("w_split" if q == 3 else "quarter_split"), 1)

            for q in range(4):
                split_quarter(0, q)
                for k in range(4 * q, 4 * q + 4):
                    low(k, chunk(Z, k), "x_hi", "x_split")
                split_quarter(1, q)
            for i in range(1, 13):
                split(Idx(i + 1))
                t = Idx(i - 1)
                if i == 2:
                    p_low(p_raw0, 1)
                    raw = par[:, C_LBRAW:C_LBRAW + HEADS]
                    tt(lb[:, 0, :], raw, raw, ALU.subtract).then_inc(S("lb_step"), 1)
                if t.base < 4:
                    n, g = t.base // 2, t.base % 2
                    dve.wait_ge(S("gemm_done"), i)
                    dve.wait_ge(S("x_split"), KC)
                    dve.wait_ge(S("par_landed"), 16)
                    src = G[t.slot][:, :].rearrange("p (n l) -> p l n", l=CMP_STRIDE)
                    for half in range(2):
                        ls = slice(half * CMP_STRIDE, (half + 1) * CMP_STRIDE)
                        pe_col = par[:, C_PE + CMP_LEN * n:C_PE + CMP_LEN * (n + 1)][:, ls].unsqueeze(2)
                        last = tt(blk[n][:, ls, g * NCMP:(g + 1) * NCMP], src[:, :, half:half + NCMP],
                                  pe_col.broadcast_to([P, CMP_STRIDE, NCMP]), ALU.add)
                    frees(last, t)
                if i == 5:
                    dve.wait_ge(S("msk_landed"), 16)
                    dve.tensor_copy(msk[:, :], p_raw0[:, 0:MASKS]).then_inc(S("masks_ready"), 1)
                    dve.wait_ge(S("lb_exp"), 1)
                    dve.reciprocal(lb[:, 1, :], lb[:, 0, :]).then_inc(S("lb_step"), 1)
                    dve.wait_ge(S("lb_step"), 2)
                    tt(lb[:, 1, :], lb[:, 0, :], lb[:, 1, :], ALU.mult).then_inc(S("lb_step"), 1)
                    dve.wait_ge(S("lb_step"), 3)
                    tt(lb[:, 2, :], lb[:, 1, :], lb[:, 1, :], ALU.subtract).then_inc(S("lb_step"), 1)
                    dve.wait_ge(S("lb_step"), 4)
                    ts(lb[:, 3, :], lb[:, 2, :], -1.0, 1.0, ALU.mult, ALU.add).then_inc(S("lb_step"), 1)
                if i == 8:
                    dve.wait_ge(S("cmp_done"), 1)
                    dve.tensor_copy(kcT[:, :], X[2][:, 0:GROUPS * NCMP]).then_inc(S("cmp_ready"), 1)
                    dve.tensor_copy(vc4[:, :, :].rearrange("p g d -> p (g d)"), TB[2][:, 0:GROUPS * P]).then_inc(S("cmp_ready"), 1)
                if 10 <= i:
                    value_tile(i - 10)

            def prev_hz(h, hz):
                dve.wait_ge(S("kp_turned"), h)
                dve.tensor_copy(kp, TB[1][:, :]).then_inc(S("kp_ready"), 1)
                dve.wait_ge(S("sg_hz"), h)
                frees(tt(hz_s, G[hz.slot][:, :], sg, ALU.mult), hz)

            def prev_state(h):
                dve.wait_ge(S("sums_done"), h)
                dve.tensor_copy(state[:, 0:P], TB[2][:, 0:P]).then_inc(S("state_step"), 1)
                dve.wait_ge(S("state_step"), h * 2 - 1)
                stt(state[:, P:2 * P], state[:, 0:P], eglast[:, 1:2], TB[2][:, P:2 * P], op0=ALU.mult, op1=ALU.add).then_inc(
                    S("state_step"), 1)
                dve.wait_ge(S("state_step"), h * 2)
                stt(state[:, 2 * P:3 * P], state[:, P:2 * P], eglast[:, 2:3], TB[2][:, 2 * P:3 * P], op0=ALU.mult,
                    op1=ALU.add).then_inc(S("state_ready"), 1)

            def prev_ms(h):
                dve.wait_ge(S("ms_done"), h)
                ts(rst_h, X[1][:, :], 1.0 / P, EPS, ALU.mult, ALU.add).then_inc(S("ms_ready"), 1)

            def prev_y(h):
                dve.wait_ge(S("rms_inv"), h)
                tt(osb, osb, rst_h, ALU.mult).then_inc(S("o_normed"), 1)
                dve.wait_ge(S("o_normed"), h)
                stt(chunk(Y, h + (HEADS - 1)), osb, pcol(C_NORM - 1, h), hz_s, op0=ALU.mult, op1=ALU.mult).then_inc(S("y_hgrn"), 1)

            def head(h, first=False):
                w = [head_tile(h, k) for k in range(7)]

                def logits(tiles, branch):
                    for ti, bank, at in SCORES:
                        n = (ti + 1) * P
                        m = 4 * branch + ti
                        dve.tensor_tensor_reduce(out=prob_of(ti), in0=bias[:, T - n:T], in1=bank[:, at:at + n], scale=1.0,
                                                 scalar=-3e38, op0=ALU.add, op1=ALU.max, accum_out=mx[:, m:m + 1]).then_inc(
                                                     S("logits"), 1)

                def normalise(branch_cols, n_exps, n_norms):
                    lo, hi = branch_cols[0][0], branch_cols[-1][0] + 4
                    dve.wait_ge(S("exps"), h * 12 + n_exps)
                    dve.reciprocal(rg[:, lo:hi], rsum[:, lo:hi]).then_inc(S("norms"), 1)
                    dve.wait_ge(S("norms"), h * 5 + n_norms)
                    for c, b in branch_cols:
                        gcol = gates[:, ds(h * 3 + b, 1), :].rearrange("p a t -> p (a t)") if not first else gates[:, b, :]
                        tt(rg[:, c:c + 4], rg[:, c:c + 4], gcol, ALU.mult).then_inc(S("norms"), 1)
                    dve.wait_ge(S("norms"), h * 5 + n_norms + len(branch_cols))

                def halves(e, buf):
                    v = buf.rearrange("p (b n) -> p b n", n=2 * HALVES[e])
                    return v[:, :, 0:HALVES[e]], v[:, :, HALVES[e]:2 * HALVES[e]]

                def gap(e):
                    if e == 6:
                        g1, g2 = halves(e, gg)
                        tt(pair.unsqueeze(2), g2, g1, ALU.subtract).then_inc(S("gap"), 1)
                        return
                    g1, g2 = halves(e, gg)
                    r1, r2 = halves(e, ring[e % 3])
                    ref = g1[:, :, HALVES[e] - 1:HALVES[e]].broadcast_to(list(g1.shape))
                    tt(r1, ref, g1, ALU.subtract).then_inc(S("gap"), 1)
                    tt(r2, g2, ref, ALU.subtract).then_inc(S("gap"), 1)

                def gate_level(e):
                    dve.wait_ge(S("decay"), h * 7 + (e + 1))
                    if e == 6:
                        tt(pair.unsqueeze(2), pair.unsqueeze(2), halves(e, qq)[1], ALU.mult).then_inc(S("level_ready"), 1)
                        return
                    r1, r2 = halves(e, ring[e % 3])
                    k1, _ = halves(e, kk)
                    _, q2 = halves(e, qq)
                    tt(r1, r1, k1, ALU.mult).then_inc(S("level_k"), 1)
                    tt(r2, r2, q2, ALU.mult).then_inc(S("level_ready"), 1)

                def take_level(l):
                    if l:
                        wait_alone(("level_copied", h * LEVELS + l), ("level_done", h * LEVELS + LEVEL_BANK_DONE[l]))
                    else:
                        dve.wait_ge(S("level_done"), h * LEVELS + 1)
                    bank, at = LEVEL_AT[l]
                    n = P if l == 0 else HALF
                    half = P if l == 0 else HALVES[l - 1]
                    src = bank[:, at:at + NT * n].rearrange("p (c b n) -> p c b n", c=NT, n=half)
                    m0 = 0 if l == 0 else P + (l - 1) * HALF
                    m = msk[:, m0:m0 + n].rearrange("p (a b n) -> p a b n", a=1, n=half).broadcast_to([P, NT, n // half, half])
                    if l == 0:
                        dst = AT.rearrange("p (c b n) -> p c b n", c=NT, n=half)
                        tt(dst, src, m, ALU.mult).then_inc(S("level_copied"), 1)
                    else:
                        dst = AT.rearrange("p (c b n) -> p c b n", c=NT, n=2 * half)[:, :, :, half:2 * half]
                        dve.copy_predicated(dst, m, src).then_inc(S("level_copied"), 1)

                split(w[1])
                if first:
                    value_tile(3)
                else:
                    prev_hz(h, before(w[5]))
                split(w[2])
                if first:
                    dve.wait_ge(S("gates_turned"), 1)
                    dve.tensor_copy(gates[:, :, :], TB[2][:, 256:256 + 24 * NT].rearrange("p (t b) -> p b t", t=NT)).then_inc(
                        S("gates_step"), 1)
                    dve.wait_ge(S("gates_step"), 1)
                    gc = gates[:, :, :].rearrange("p (h b) t -> p h b t", b=3)[:, :, 0, 0]
                    ts(gc, gc, pcol(C_SEEN, 0), None, ALU.mult).then_inc(S("gates_step"), 1)
                    dve.wait_ge(S("gates_step"), 2)
                else:
                    prev_state(h)
                slope = pcol(C_SLOPE, h)
                ts(bias[:, 0:T], par[:, C_DIST:C_DIST + T], slope, None, ALU.mult).then_inc(S("bias_ready"), 1)
                ts(bias[:, T:], par[:, C_DISTC:C_DISTC + NT * NCMP], slope, None, ALU.mult).then_inc(S("bias_ready"), 1)
                split(w[3])
                dve.wait_ge(S("sg_nz"), h + 1)
                frees(tt(nz_s, G[w[1].slot][:, :], sg, ALU.mult), w[1])
                wait_alone(("scores_s", h + 1), ("bias_ready", h * 2 + 2))
                logits(range(NT), 0)
                for ti in range(NT):
                    dve.tensor_tensor_reduce(out=probc31[:, ti, :], in0=bias[:, T + ti * NCMP:T + (ti + 1) * NCMP],
                                             in1=X[2][:, 256 + 32 * ti:256 + 32 * ti + NCMP], scale=1.0, scalar=-3e38,
                                             op0=ALU.add, op1=ALU.max, accum_out=mx[:, 4 + ti:5 + ti]).then_inc(S("logits"), 1)
                dve.wait_ge(S("logits"), h * 12 + 8)
                ts(nmx[:, 0:8], mx[:, 0:8], -1.0, None, ALU.mult).then_inc(S("neg_max"), 1)
                normalise(((0, 1), (4, 0)), 8, 1)
                for ti in range(NT):
                    ts(prob_of(ti), prob_of(ti), rg[:, ti:ti + 1], None, ALU.mult).then_inc(S("probs"), 1)
                tt(probc31, probc31, rg[:, 4:8].unsqueeze(2).broadcast_to([P, NT, NCMP]), ALU.mult).then_inc(S("probs"), 1)
                split(w[4])
                wait_alone(("scores_w", h + 1), ("turned_s", h + 1))
                logits(range(NT), 2)
                dve.wait_ge(S("logits"), h * 12 + 12)
                ts(nmx[:, 8:12], mx[:, 8:12], -1.0, None, ALU.mult).then_inc(S("neg_max"), 1)
                lbh, omlb = lb[:, 2, :], lb[:, 3, :]
                lbh, omlb = (lbh[:, 0:1], omlb[:, 0:1]) if first else (lbh[:, ds(h, 1)], omlb[:, ds(h, 1)])
                dve.wait_ge(*drained(w[2]))
                ts(sg, sg, omlb, lbh, ALU.mult, ALU.add).then_inc(S("f_step"), 1)
                dve.wait_ge(S("f_step"), h + 1)
                ts(sg, sg, LN_FLOOR, None, ALU.max).then_inc(S("f_ready"), 1)
                ts(kk, kk, omlb, None, ALU.mult).then_inc(S("k_ready"), 1)
                dve.tensor_copy(probT[:, T:2 * T], TB[1][:, :]).then_inc(S("probT_v"), 1)
                dve.tensor_copy(probT[:, 2 * T:2 * T + 256], TB[2][:, 0:256]).then_inc(S("probT_v"), 1)
                tt(probcT.rearrange("p (c t) -> p c t", c=NT), TB[2][:, 256:384].unsqueeze(1).broadcast_to([P, NT, P]),
                   par[:, C_TILE:C_TILE + NT].unsqueeze(2).broadcast_to([P, NT, P]), ALU.mult).then_inc(S("probT_v"), 1)
                normalise(((8, 2),), 12, 4)
                for ti in range(NT):
                    ts(prob_of(ti), prob_of(ti), rg[:, 8 + ti:9 + ti], None, ALU.mult).then_inc(S("probs"), 1)
                dve.wait_ge(S("logf"), h + 1)
                for c in range(NT):
                    at = gg[:, c * P:(c + 1) * P]
                    dve.tensor_tensor_scan(at, ones[:, :], at, 0.0, ALU.mult, ALU.add).then_inc(S("scan"), 1)
                split(w[5])
                dve.wait_ge(S("turned_w"), h + 1)
                dve.tensor_copy(probT[:, T:2 * T], TB[1][:, :]).then_inc(S("probT_v"), 1)
                dve.tensor_copy(probT[:, 2 * T:2 * T + 256], TB[2][:, 0:256]).then_inc(S("probT_v"), 1)
                if not first:
                    prev_ms(h)
                dve.wait_ge(S("scan"), h * 4 + 4)
                for e in range(3):
                    gap(e)
                dve.wait_ge(S("sg_hq"), h + 1)
                frees(tt(qq, G[w[3].slot][:, :], sg, ALU.mult), w[3])
                dve.wait_ge(S("k_ready"), h + 1)
                dve.wait_ge(*drained(w[3]))
                for e in range(3):
                    gate_level(e)
                if not first:
                    prev_y(h)
                split(w[6])
                dve.wait_ge(S("attn_done"), h + 1)
                tt(chunk(Y, h), O[:, :], nz_s, ALU.mult).then_inc(S("y_attn"), 1)
                g4 = gg.rearrange("p (c t) -> p c t", c=NT)
                tt(kpT.rearrange("p (c t) -> p c t", c=NT), g4[:, :, P - 1:P].broadcast_to([P, NT, P]), g4,
                   ALU.subtract).then_inc(S("gap_k"), 1)
                dve.wait_ge(S("level_done"), h * LEVELS + 4)
                for e in range(3, 7):
                    gap(e)
                dve.wait_ge(S("decay_q"), h + 1)
                dve.tensor_copy(eglast[:, :], qg.rearrange("p (c t) -> p c t", c=NT)[:, :, P - 1]).then_inc(S("eglast"), 1)
                dve.wait_ge(S("eglast"), h + 1)
                tt(qg, qg, qq, ALU.mult).then_inc(S("q_decayed"), 1)
                dve.wait_ge(S("decay_k"), h + 1)
                tt(kpT, kpT, kk, ALU.mult).then_inc(S("kpT_ready"), 1)
                for l in range(4):
                    take_level(l)
                for e in range(3, 7):
                    gate_level(e)
                for l in range(4, LEVELS):
                    take_level(l)

            head(0, first=True)
            with dve.Fori(1, HEADS) as h:
                head(h)

            prev_hz(HEADS, Idx(W_PLE[0][0] - 1))
            split(Idx(W_OUT[0]))
            for c in range(4):
                low(c, chunk(Y, c), "act_hi0", "act_split0")
            prev_state(HEADS)
            for c in range(4, 8):
                low(c, chunk(Y, c), "act_hi0", "act_split0")
            split(Idx(W_OUT[0] + 1))
            for c in range(8, KC - 1):
                low(c, chunk(Y, c), "act_hi0", "act_split0")

            def centre(n, c):
                tt(chunk(Y, c), chunk(Y, c), c_shift if n == 1 else ln_shift, ALU.subtract).then_inc(S("centred"), 1)

            def add_last(n, c, sqs, sq):
                dve.wait_ge(*after("centred", n, c + 1))
                dve.wait_ge(*after("c_summed", n, c))
                tt(ln_sum, ln_sum, chunk(Y, c), ALU.add).then_inc(S("c_summed"), 1)
                dve.wait_ge(*after("squared", n, c + 1))
                dve.wait_ge(*after("sq_summed", n, c))
                tt(sqs, sqs, sq, ALU.add).then_inc(S("sq_summed"), 1)

            def statistics(n, diag_of_mean, between=None):
                mean, off, var, dev, rr = [stat[:, k * NT:(k + 1) * NT] for k in range(5)]

                def spread(dst, src):
                    return tt(dst.rearrange("p (c t) -> p c t", c=NT), ident.unsqueeze(1).broadcast_to([P, NT, P]),
                              src.unsqueeze(2).broadcast_to([P, NT, P]), ALU.mult)

                step = S("ln_step")
                dve.wait_ge(*after("mean_sum", n, 1))
                ts(mean, X[0][:, 0:NT], 1.0 / D, None, ALU.mult).then_inc(step, 1)
                dve.wait_ge(*after("ln_step", n, 1))
                stt(off, mean, -1.0, mean, op0=ALU.mult, op1=ALU.mult).then_inc(step, 1)
                dve.wait_ge(*after("ln_step", n, 2))
                ts(off, off, EPS, None, ALU.add).then_inc(step, 1)
                dve.wait_ge(*after("ln_step", n, 3))
                dve.wait_ge(*after("var_sum", n, 1))
                stt(var, TB[2][:, 0:NT], 1.0 / D, off, op0=ALU.mult, op1=ALU.add).then_inc(S("var"), 1)
                dve.wait_ge(*after("centred", n, KC))
                spread(diag_of_mean, mean).then_inc(S("diag_d"), 1)
                if between:
                    between()
                dve.wait_ge(*after("ln_guess", n, 1))
                stt(rr, dev, -0.5, dev, op0=ALU.mult, op1=ALU.mult).then_inc(step, 1)
                dve.wait_ge(*after("ln_step", n, 4))
                dve.wait_ge(*after("var", n, 1))
                tt(rr, rr, var, ALU.mult).then_inc(step, 1)
                dve.wait_ge(*after("ln_step", n, 5))
                stt(dev, rr, 1.5, dev, op0=ALU.add, op1=ALU.mult).then_inc(step, 1)
                dve.wait_ge(*after("ln_step", n, 6))
                spread(diag_r, dev).then_inc(S("diag_r"), 1)

            def minus_mean(j):
                tt(chunk(Y, j), chunk(Y, j), X[1][:, :], ALU.subtract).then_inc(S("less_mean"), 1)

            def over_deviation(n, j):
                dve.wait_ge(*after("less_mean", n, j + 1))
                tt(chunk(Y, j), chunk(Y, j), X[2][:, :], ALU.mult).then_inc(S("normed"), 1)

            def second_part(layer):
                w, g = W_OUT[layer], G_OUT[layer]

                n_ln = 2 * layer

                def out_chunk(w, g, j):
                    dve.wait_ge(S("gemm_done"), w.n(1))
                    frees(stt(chunk(Y, j), chunk(Y, j), ALPHA, G[g.slot][:, :], op0=ALU.mult, op1=ALU.add), g)

                if layer == 0:
                    prev_ms(HEADS)
                    prev_y(HEADS)
                    low(KC - 1, chunk(Y, KC - 1), "act_hi0", "act_split0")
                dve.memset(ln_sum, 0.0).then_inc(S("sums_set"), 1)
                dve.wait_ge(*after("sums_set", n_ln, 1))
                for n in range(4):
                    dve.wait_ge(S(f"res_landed{layer}_{n}"), 16)
                with dve.Fori(0, KC // 4) as i:
                    for k in range(2):
                        split(Idx(w + 2 + k, 2, i))
                        out_chunk(Idx(w + k, 2, i), Idx(g + k, 2, i), i * 2 + k)
                        dve.wait_ge(*drained(Idx(g + k, 2, i)))
                        if k:
                            dve.wait_ge(*after("half_summed", n_ln, i * 2 + 1))
                        tt(ln_sum, ln_sum, chunk(Y, i * 2 + k), ALU.add).then_inc(S("half_summed"), 1)

                def centre_all(cs, slot, others):
                    for c in cs:
                        tt(chunk(Y, c), chunk(Y, c), ln_shift, ALU.subtract).then_inc(S("centred"), 1)
                    for n, c in enumerate(cs):
                        dve.wait_ge(*after("centred", n_ln, c + 1))
                        if others or n:
                            dve.wait_ge(*after("c_summed", n_ln, c))
                        tt(ln_sum, ln_sum, chunk(Y, c), ALU.add).then_inc(S("c_summed"), 1)
                    for n, c in enumerate(cs):
                        dve.wait_ge(*after("squared", n_ln, c + 1))
                        if others or n:
                            dve.wait_ge(*after("sq_summed", n_ln, c))
                        tt(ln_sqs, ln_sqs, ln_sq[(slot + n) % 2], ALU.add).then_inc(S("sq_summed"), 1)

                split(Idx(w + 10))
                out_chunk(Idx(w + 8), Idx(g + 8), 8)
                dve.wait_ge(*after("shift_done", n_ln, 1))
                ts(ln_shift, X[0][:, :], 2.0 / D, None, ALU.mult).then_inc(S("shift_ready"), 1)
                dve.memset(ln_sum, 0.0).then_inc(S("sums_set"), 1)
                dve.memset(ln_sqs, 0.0).then_inc(S("sums_set"), 1)
                dve.wait_ge(*after("shift_ready", n_ln, 1))
                dve.wait_ge(*after("sums_set", n_ln, 3))
                centre_all(range(3), 0, False)
                with dve.Fori(0, 3) as i:
                    for k in range(2):
                        split(Idx(w + 11 + k, 2, i))
                        out_chunk(Idx(w + 9 + k, 2, i), Idx(g + 9 + k, 2, i), i * 2 + (9 + k))
                        dve.wait_ge(*drained(Idx(g + 9 + k, 2, i)))
                        centre_all([i * 4 + (3 + 2 * k), i * 4 + (4 + 2 * k)], 1, True)
                out_chunk(Idx(w + 15), Idx(g + 15), KC - 1)
                dve.wait_ge(*drained(Idx(g + 15)))
                centre(n_ln, KC - 1)
                add_last(n_ln, KC - 1, ln_sqs, ln_sq[1])
                statistics(n_ln, diag_d, lambda: split(Idx(w + 17)))
                dve.wait_ge(*after("mean_spread", n_ln, 1))
                for j in range(3):
                    minus_mean(j)
                dve.wait_ge(*after("dev_spread", n_ln, 1))
                for j in range(KC):
                    over_deviation(n_ln, j)
                    if j + 3 < KC:
                        minus_mean(j + 3)
                    if j == 9:
                        split(Idx(w + 18))

                def gate(g, j, n_gate):
                    dve.wait_ge(*drained(g))
                    tt(ln_sq[g.slot], ln_sq[g.slot], chunk(Z, j), ALU.mult).then_inc(S("ple_gated"), 1)
                    dve.wait_ge(S("ple_gated"), n_gate)
                    tt(chunk(Y, j), chunk(Y, j), ln_sq[g.slot], ALU.add).then_inc(S(f"x_out{layer}"), 1)

                w, g = W_GATE[layer], G_GATE[layer]
                with dve.Fori(0, KC // 2 - 1) as i:
                    for k in range(2):
                        split(Idx(w + 2 + k, 2, i))
                        gate(Idx(g + k, 2, i), i * 2 + k, i * 2 + (layer * KC + k + 1))
                if w + KC < W_TILES:
                    split(Idx(w + KC))
                gate(Idx(g + KC - 2), KC - 2, layer * KC + KC - 1)
                if layer == 0:
                    for j in range(3):
                        low(j, chunk(Y, j), "x2_hi", "x2_split")
                gate(Idx(g + KC - 1), KC - 1, layer * KC + KC)

            second_part(0)

            for j in range(3, KC):
                low(j, chunk(Y, j), "x2_hi", "x2_split")
                if j == 8:
                    split(Idx(W_CONV + 1))
            p_low(p_raw1, 2)
            split(Idx(W_CONV + 2))
            for n in range(2):
                dve.memset(U[n][:, 0:CONV_K - 1], 0.0).then_inc(S("history_set"), 1)
            dve.memset(ln_sum, 0.0).then_inc(S("sums_set"), 1)
            dve.wait_ge(S("history_set"), 2)
            dve.wait_ge(S("stored0"), 16 * KC)
            dve.wait_ge(S("x2_split"), KC)
            EVEN, ODD = TB[0][:, :], TB[1][:, :]

            def conv(j, k, i, u):
                w, g = Idx(W_CONV + k, 10, i), Idx(G_CONV + k, 10, i)
                dve.wait_ge(S("gemm_done"), w.n(1))
                dve.wait_ge(*drained(Idx(g.base - 1, 10, i)))
                frees(tt(U[u][:, CONV_K - 1:UW], G[g.slot][:, :], conv_sg, ALU.mult), g)
                dve.wait_ge(*drained(g))
                for n in range(CONV_K):
                    src, acc = U[u][:, n:n + T], (EVEN, ODD)[n % 2]
                    cw = par[:, ds(j * CONV_K + (C_CW + n), 1)]
                    if n == 0:
                        dve.wait_ge(S("conv_done"), j + 1)
                        ts(acc, src, cw, pcol(C_CBIAS, j), ALU.mult, ALU.add).then_inc(S("tap"), 1)
                    elif n == 1:
                        ts(acc, src, cw, None, ALU.mult).then_inc(S("tap"), 1)
                    else:
                        dve.wait_ge(S("tap"), j * CONV_K + (n - 1))
                        stt(acc, src, cw, acc, op0=ALU.mult, op1=ALU.add).then_inc(S("tap"), 1)
                dve.wait_ge(S("tap"), j * CONV_K + CONV_K)
                dve.tensor_copy(chunk(Y, j), ODD).then_inc(S("odd_copied"), 1)
                dve.wait_ge(S("odd_copied"), j + 1)
                tt(chunk(Y, j), chunk(Y, j), EVEN, ALU.add).then_inc(S("conv_done"), 1)

            dve.sem_inc(S("conv_done"), 1)
            with dve.Fori(0, 4) as i:
                for n, k in enumerate((1, 3, 6, 8)):
                    conv(i * 4 + n, k, i, n % 2)
            dve.wait_ge(*after("c_summed", 1, KC - 2))
            dve.wait_ge(*after("sq_summed", 1, KC - 2))
            dve.wait_ge(S("conv_done"), KC + 1)
            centre(1, KC - 2)
            centre(1, KC - 1)
            add_last(1, KC - 2, c_sqs, c_sq[0])
            add_last(1, KC - 1, c_sqs, c_sq[1])
            statistics(1, c_diag_d)

            def gate_c(j):
                dve.wait_ge(S("silu_c"), j + 1)
                if j >= 12:
                    dve.wait_ge(*drained(Idx(G_CONV + 32 + j)))
                tt(chunk(Y, j), chunk(Y, j), chunk(Z, j), ALU.mult).then_inc(S("gated"), 1)

            dve.wait_ge(*after("mean_spread", 1, 1))
            minus_mean(0)
            dve.wait_ge(*after("dev_spread", 1, 1))
            for j in range(KC + 4):
                if j + 1 < KC:
                    minus_mean(j + 1)
                if j < KC:
                    over_deviation(1, j)
                if 4 <= j and j < KC + 2:
                    gate_c(j - 4)
            gate_c(KC - 2)
            dve.wait_ge(S("w_split"), W_OUT[1])
            split(Idx(W_OUT[1]))
            gate_c(KC - 1)
            for c in range(KC):
                if c == 8:
                    split(Idx(W_OUT[1] + 1))
                low(c, chunk(Y, c), "act_hi1", "act_split1")
            second_part(1)

    return nc


def chunks(a):
    return np.ascontiguousarray(a.reshape(-1, P, a.shape[-1]).transpose(1, 0, 2)).reshape(P, -1)


def tiles(w):
    n = w.shape[1] // P
    return w.reshape(KC, P, n, P).transpose(2, 1, 0, 3).reshape(n, P, D)


def kernel(x, p, ev_w_in, ev_cmp_pe_k, ev_cmp_w1_k, ev_cmp_w2_k, ev_cmp_pe_v, ev_cmp_w1_v, ev_cmp_w2_v, ev_hg_norm,
           hgrn_lb, ev_w_out, od_w_in, od_conv_w, od_conv_b, od_ln_g, od_ln_b, od_w_out, post_ln_g, post_ln_b, ple_w,
           ple_gate_w):
    from concourse import bacc
    from concourse.bass_utils import run_bass_kernel_spmd

    ev = np.asarray(ev_w_in)[0]
    at, parts = 0, {}
    for name, n in (("nq", 1024), ("kv", 1536), ("ng", 24), ("nz", 1024), ("hq", 1024), ("hf", 1024), ("hi", 1024), ("hz", 1024)):
        parts[name] = ev[:, at:at + n]
        at += n
    kv = tiles(parts["kv"])
    kv = kv[[0, 1, 2, 3, 4, 5, 8, 9, 6, 7, 10, 11]]
    ng = tiles(np.concatenate([parts["ng"], np.zeros((D, P - 24), np.float32)], axis=1))
    heads = np.stack([tiles(parts[n]) for n in ("nq", "nz", "hf", "hq", "hi", "hz")], axis=1).reshape(-1, P, D)

    def ple(layer):
        w = np.asarray(ple_w)[layer].reshape(PLE_K, P, 2, 8, P)
        return w.transpose(2, 1, 3, 0, 4).reshape(2, P, D)

    a, b, z = [tiles(w) for w in np.split(np.asarray(od_w_in)[0], 3, axis=1)]
    b, a = [t.reshape(KC // 2, 2, P, D) for t in (b, a)]
    conv = np.stack([b[:, 0], a[:, 0], b[:, 1], a[:, 1], z[:KC // 2]], axis=1).reshape(-1, P, D)
    conv = np.concatenate([conv, z[KC // 2:]])
    gate = np.asarray(ple_gate_w)
    out_w = [tiles(np.asarray(w)[0]) for w in (ev_w_out, od_w_out)]
    second = [np.concatenate([ple(n)[:1], out_w[n], ple(n)[1:], tiles(gate[n])]) for n in range(2)]
    wall = np.concatenate([kv, ng, heads, second[0], conv, second[1]])

    def vec(v):
        return np.asarray(v).reshape(-1, P).T

    cols, masks = constants()
    taps = np.asarray(od_conv_w)[0].reshape(CONV_K, KC, P).transpose(2, 1, 0).reshape(P, -1)
    par = np.concatenate([vec(post_ln_g), vec(post_ln_b), vec(od_ln_g), vec(od_ln_b), vec(od_conv_b), taps,
                          vec(ev_hg_norm), vec(hgrn_lb), np.asarray(ev_cmp_pe_k)[0].T, np.asarray(ev_cmp_pe_v)[0].T, cols], axis=1)

    def w1(w):
        return np.asarray(w)[0].reshape(CMP_LEN, P, P).transpose(1, 0, 2).reshape(P, -1)

    arrays = {
        "xT": chunks(np.asarray(x)[0].T),
        "wall": wall,
        "w1": np.stack([w1(ev_cmp_w1_k), w1(ev_cmp_w1_v)]),
        "w2": np.concatenate([np.asarray(ev_cmp_w2_k)[0], np.asarray(ev_cmp_w2_v)[0]], axis=1),
        "pT": np.stack([chunks(np.asarray(p)[n, 0].T) for n in range(2)]),
        "par": par,
        "masks": masks,
    }
    arrays = {n + "_in": np.ascontiguousarray(v) for n, v in arrays.items()}
    nc = bacc.Bacc("TRN2", target_bir_lowering=False, num_devices=1)
    args = [nc.dram_tensor(n, v.shape, mybir.dt.from_np(v.dtype), kind="ExternalInput").ap() for n, v in arrays.items()]
    out = nc.dram_tensor("out", (P, KC * T), mybir.dt.float32, kind="ExternalOutput").ap()
    build(nc, *args, out)
    r = run_bass_kernel_spmd(nc, [arrays], core_ids=[0])
    y = r.results[0]["out"]
    return np.ascontiguousarray(y.reshape(P, KC, T).transpose(2, 1, 0)).reshape(1, T, D)
```
